# Optimizing a Trainium2 kernel written in Bass

```python
import jax, jax.numpy as jnp
from jax import lax
import numpy as np

D_MODEL = 1024
BATCH = 1
SEQ = 128
DEPTH = 1
DEC_BATCH = 1
DEC_SEQ = 1024
PAST_LEN = 128

GRID_W = 64
N_HEADS = 16
HEAD_DIM = 64
D_RWKV = N_HEADS * HEAD_DIM
D_CONV = D_MODEL
CONV_W = 3
D_DECAY_LORA = 64
D_AAA_LORA = 64
D_GATE_LORA = 128
D_FF = 4 * D_MODEL
N_BRANCH = 2
D_IN_PROJ = 3 * D_RWKV + 2 * D_DECAY_LORA + 2 * D_AAA_LORA + D_GATE_LORA + 3 * D_CONV + N_BRANCH * D_MODEL
EPS = 1e-6
LNX_EPS = 64e-5

kernel_name = 'bidir_rwkv7_shortconv_flow_step'

def _in_split_points():
    sizes = (D_RWKV, D_RWKV, D_RWKV, 2 * D_DECAY_LORA, 2 * D_AAA_LORA, D_GATE_LORA, D_CONV, D_CONV, D_CONV)
    pts, acc = [], 0
    for s in sizes:
        acc += s
        pts.append(acc)
    return pts

def rms_norm(x, g):
    xf = x.astype(jnp.float32)
    y = xf * lax.rsqrt(jnp.mean(xf * xf, axis=-1, keepdims=True) + EPS)
    return (y * g.astype(jnp.float32)).astype(x.dtype)

def ada_modulation(cvec, w_ada, b_ada):
    m = jax.nn.silu(cvec) @ w_ada + b_ada
    return jnp.split(m[..., None, :], 6, axis=-1)

def centred_conv3(u, w):
    L = u.shape[-2]
    pad = [(0, 0)] * (u.ndim - 2) + [(1, 1), (0, 0)]
    up = jnp.pad(u, pad)
    return w[0] * up[..., 0:L, :] + w[1] * up[..., 1:L + 1, :] + w[2] * up[..., 2:L + 2, :]

def to_heads(u):
    return u.reshape(u.shape[:-1] + (N_HEADS, HEAD_DIM))

def wkv_scan(s0, r, w, k, v, a, b, reverse):
    def seq_major(u):
        return jnp.moveaxis(to_heads(u.astype(jnp.float32)), 1, 0)

    def step(S, inp):
        r_t, w_t, k_t, v_t, a_t, b_t = inp
        sa = jnp.einsum('bhvk,bhk->bhv', S, a_t)
        S = S * w_t[:, :, None, :] + sa[..., None] * b_t[:, :, None, :] + v_t[..., None] * k_t[:, :, None, :]
        return S, jnp.einsum('bhvk,bhk->bhv', S, r_t)

    s_final, y = lax.scan(step, s0.astype(jnp.float32),
                          (seq_major(r), seq_major(w), seq_major(k), seq_major(v), seq_major(a), seq_major(b)),
                          reverse=reverse)
    return jnp.moveaxis(y, 0, 1), s_final.astype(s0.dtype)

def token_mixer(xn, s0_f, s0_b, p, on_grid):
    B, T, _ = xn.shape
    z = xn @ p['w_in']
    r, k, v, wl, al, gl, cb, cc, ch, zg = jnp.split(z, _in_split_points(), axis=-1)

    g_out = jax.nn.sigmoid(gl) @ p['g2']
    kk = to_heads((k * p['k_k']).astype(jnp.float32))
    kk = kk * lax.rsqrt(jnp.maximum(jnp.sum(kk * kk, axis=-1, keepdims=True), 1e-12))
    kk = kk.reshape(B, T, D_RWKV)
    rh = to_heads(r.astype(jnp.float32))
    vh = to_heads(v.astype(jnp.float32))
    ys, bonuses, states = [], [], []
    for d, (s0, reverse) in enumerate(((s0_f, False), (s0_b, True))):
        wl_d = wl[..., d * D_DECAY_LORA:(d + 1) * D_DECAY_LORA]
        al_d = al[..., d * D_AAA_LORA:(d + 1) * D_AAA_LORA]
        w_log = -jax.nn.softplus(-(p['w0'][d] + jnp.tanh(wl_d) @ p['w2'][d])) - 0.5
        decay = jnp.exp(-jnp.exp(w_log.astype(jnp.float32)))
        a = jax.nn.sigmoid(p['a0'][d] + al_d @ p['a2'][d])
        kd = k * (1.0 + (a - 1.0) * p['k_a'])
        y_d, s_d = wkv_scan(s0, r, decay, kd, v, -kk, kk * a, reverse)
        ys.append(y_d)
        bonuses.append(jnp.sum(rh * to_heads(kd.astype(jnp.float32)) * p['r_k'], axis=-1, keepdims=True) * vh)
        states.append(s_d)
    wkv = ys[0] + ys[1]
    mu = jnp.mean(wkv, axis=-1, keepdims=True)
    var = jnp.mean(jnp.square(wkv - mu), axis=-1, keepdims=True)
    ln = ((wkv - mu) * lax.rsqrt(var + LNX_EPS)).reshape(B, T, D_RWKV) * p['lnx_w'] + p['lnx_b']
    x_a = (ln + (bonuses[0] + bonuses[1]).reshape(B, T, D_RWKV)).astype(xn.dtype) * g_out
    y_a = x_a @ p['w_pa']

    u = cc * ch
    if on_grid:
        rows = T // GRID_W
        conv_u = centred_conv3(u.reshape(B, rows, GRID_W, D_CONV), p['conv_w']).reshape(B, T, D_CONV)
    else:
        conv_u = centred_conv3(u, p['conv_w'])
    y_b = (cb * conv_u) @ p['w_pb']

    gate_a, gate_b = jnp.split(jax.nn.sigmoid(zg), 2, axis=-1)
    out = (gate_a * y_a + gate_b * y_b) @ p['w_o']
    return out, states[0], states[1]

def layer_apply(x, cvec, s0_f, s0_b, p, on_grid):
    sh1, sc1, gt1, sh2, sc2, gt2 = ada_modulation(cvec, p['w_ada'], p['b_ada'])
    xn = rms_norm(x, p['norm1_g']) * (1.0 + sc1) + sh1
    mix, s_f, s_b = token_mixer(xn, s0_f, s0_b, p, on_grid)
    x = x + gt1 * mix
    xn = rms_norm(x, p['norm2_g']) * (1.0 + sc2) + sh2
    x = x + gt2 * (jnp.square(jax.nn.relu(xn @ p['w_ff1'])) @ p['w_ff2'])
    return x, s_f, s_b

def setup_inputs(seed: int = 0) -> dict:
    key = jax.random.key(seed)
    ks = jax.random.split(key, 32)

    def nrm(i, shape, scale):
        return scale * jax.random.normal(ks[i], shape, dtype=jnp.float32)

    st_shape = (DEC_BATCH, DEPTH, N_HEADS, HEAD_DIM, HEAD_DIM)
    return {
        'x_prompt': nrm(0, (BATCH, SEQ, D_MODEL), 1.0),
        'x_sample': nrm(1, (DEC_BATCH, DEC_SEQ, D_MODEL), 1.0),
        'state_rwkv_fwd': nrm(2, st_shape, 0.5),
        'state_rwkv_bwd': nrm(3, st_shape, 0.5),
        'c': nrm(4, (DEC_BATCH, D_MODEL), 1.0),
        'c_ctx': nrm(5, (D_MODEL,), 1.0),
        'norm1_g': 1.0 + nrm(6, (DEPTH, D_MODEL), 0.05),
        'norm2_g': 1.0 + nrm(7, (DEPTH, D_MODEL), 0.05),
        'w_ada': nrm(8, (DEPTH, D_MODEL, 6 * D_MODEL), 0.5 * D_MODEL ** -0.5),
        'b_ada': nrm(9, (DEPTH, 6 * D_MODEL), 0.02),
        'w_in': nrm(10, (DEPTH, D_MODEL, D_IN_PROJ), D_MODEL ** -0.5),
        'w0': -1.0 + nrm(11, (DEPTH, 2, D_RWKV), 0.3),
        'w2': nrm(12, (DEPTH, 2, D_DECAY_LORA, D_RWKV), 0.1),
        'a0': nrm(13, (DEPTH, 2, D_RWKV), 0.1),
        'a2': nrm(14, (DEPTH, 2, D_AAA_LORA, D_RWKV), 0.5 * D_AAA_LORA ** -0.5),
        'g2': nrm(15, (DEPTH, D_GATE_LORA, D_RWKV), D_GATE_LORA ** -0.5),
        'k_k': 0.85 + nrm(16, (DEPTH, D_RWKV), 0.05),
        'k_a': 1.0 + nrm(17, (DEPTH, D_RWKV), 0.05),
        'r_k': nrm(18, (DEPTH, N_HEADS, HEAD_DIM), 0.1),
        'lnx_w': 1.0 + nrm(19, (DEPTH, D_RWKV), 0.05),
        'lnx_b': nrm(20, (DEPTH, D_RWKV), 0.02),
        'conv_w': nrm(21, (DEPTH, CONV_W, D_CONV), CONV_W ** -0.5),
        'w_pa': nrm(22, (DEPTH, D_RWKV, D_MODEL), D_RWKV ** -0.5),
        'w_pb': nrm(23, (DEPTH, D_CONV, D_MODEL), D_CONV ** -0.5),
        'w_o': nrm(24, (DEPTH, D_MODEL, D_MODEL), D_MODEL ** -0.5),
        'w_ff1': nrm(25, (DEPTH, D_MODEL, D_FF), D_MODEL ** -0.5),
        'w_ff2': nrm(26, (DEPTH, D_FF, D_MODEL), D_FF ** -0.5),
        'final_norm_g': 1.0 + nrm(27, (D_MODEL,), 0.05),
    }

def reference(x_prompt, x_sample, state_rwkv_fwd, state_rwkv_bwd, c, c_ctx,
              norm1_g, norm2_g, w_ada, b_ada, w_in, w0, w2, a0, a2, g2, k_k, k_a, r_k,
              lnx_w, lnx_b, conv_w, w_pa, w_pb, w_o, w_ff1, w_ff2, final_norm_g):
    stacked = dict(norm1_g=norm1_g, norm2_g=norm2_g, w_ada=w_ada, b_ada=b_ada, w_in=w_in,
                   w0=w0, w2=w2, a0=a0, a2=a2, g2=g2, k_k=k_k, k_a=k_a, r_k=r_k,
                   lnx_w=lnx_w, lnx_b=lnx_b, conv_w=conv_w, w_pa=w_pa, w_pb=w_pb, w_o=w_o,
                   w_ff1=w_ff1, w_ff2=w_ff2)

    h = x_prompt
    zero_state = jnp.zeros((x_prompt.shape[0], N_HEADS, HEAD_DIM, HEAD_DIM), x_prompt.dtype)
    fwd_states, bwd_states = [], []
    for l in range(DEPTH):
        p = {name: arr[l] for name, arr in stacked.items()}
        h, s_f, s_b = layer_apply(h, c_ctx, zero_state, zero_state, p, False)
        fwd_states.append(s_f)
        bwd_states.append(s_b)
    y_prompt = rms_norm(h, final_norm_g)
    new_state_fwd = jnp.stack(fwd_states, axis=1)
    new_state_bwd = jnp.stack(bwd_states, axis=1)

    g = x_sample
    for l in range(DEPTH):
        p = {name: arr[l] for name, arr in stacked.items()}
        g, _, _ = layer_apply(g, c, state_rwkv_fwd[:, l], state_rwkv_bwd[:, l], p, True)
    y_sample = rms_norm(g, final_norm_g)

    return (y_prompt, y_sample, new_state_fwd, new_state_bwd)


_drawn_inputs = setup_inputs


def setup_inputs(seed=0):
    import zlib

    import numpy as np

    out = dict(_drawn_inputs(seed))
    spreads = {}
    factors = {'state_rwkv_fwd': 8.0,
     'state_rwkv_bwd': 8.0,
     'k_k': 22.925,
     'lnx_w': 8.0,
     'lnx_b': 42.744,
     'norm2_g': 3.048}
    for name, (base, spread) in spreads.items():
        noise = np.random.default_rng([zlib.crc32(name.encode()), seed]).standard_normal(out[name].shape)
        drawn = base * np.exp(spread * noise) if base else spread * noise
        out[name] = __import__('jax').numpy.asarray(drawn.astype(out[name].dtype))
    for name, factor in factors.items():
        out[name] = (out[name] * factor).astype(out[name].dtype)
    return out
```

```python
from contextlib import ExitStack

import concourse.bass as bass
from concourse import mybir

F32 = mybir.dt.float32
BF16 = mybir.dt.bfloat16
ALU = mybir.AluOpType
ACT = mybir.ActivationFunctionType

P = 128
D = 1024
KT = D // P
LAT, CTX = 1024, 128
T = LAT + CTX
G = 3
GN = T // G
C = 128
NC_LAT = LAT // C
NC = T // C
PAIRS = 8
HD = 64
ROW = 64
FFQ = 4
WAVE = 6
CH_PAIR = 65
RING = 4
LEVELS = 6
EPS = 1e-6
LNX_EPS = 64e-5
DECAY = 0.6065306597126334

N_ADA_FIRST = 16
N_PRO = N_ADA_FIRST + 3
PAIR_BLOCKS = 12
N_PAIR0 = N_PRO
N_MIX0 = N_PAIR0 + PAIRS * PAIR_BLOCKS
N_WO0 = N_MIX0 + 2 * KT
N_FF0 = N_WO0 + KT
N_BLOCKS = N_FF0 + FFQ * 2 * KT

PK_W2, PK_A2, PK_G2, PK_ST, PK_VEC = 0, 256, 512, 640, 768
V_W0, V_A0, V_KK, V_KA, V_RK, V_LNW, V_LNB, V_CONV, N_VEC = 0, 2, 4, 5, 6, 7, 8, 9, 12
PK = PK_VEC + N_VEC

K_ID, K_BO, K_ONE, K_LM, K_M1, K_GM, K_CM = 0, 128, 256, 384, 384 + 12 * 128, 384 + 14 * 128, 384 + 18 * 128
K_ALL = K_CM + T

GROUPS = [("r", "A"), ("k", "A"), ("v", "A"), ("w0", "A"), ("a0", "A"), ("w1", "A"), ("a1", "A"), ("ks", "D"),
          ("cc", "A"), ("ch", "D"), ("cb", "D"), ("za", "A"), ("zb", "A"),
          ("bon", "A"), ("vt", "D"), ("mu", "D"), ("var", "A"), ("g2", "D")]
GI = {n: i for i, (n, _) in enumerate(GROUPS)}
N_EV = {e: G * sum(1 for _, x in GROUPS if x == e) for e in "AD"}


def emptied(g, cg):
    e = GROUPS[g][1]
    return e, G * sum(1 for _, x in GROUPS[:g] if x == e) + cg + 1


def chunk(d, j):
    return j if d == 0 or j == NC_LAT else NC_LAT - 1 - j


class Chain:

    def __init__(self, eng, sem):
        self.eng, self.sem, self.n, self.base, self.per = eng, sem, 0, 0, 0

    def step(self, ins):
        ins.then_inc(self.sem, 1)
        self.n += 1

    def settle(self):
        self.eng.wait_ge(self.sem, self.base + self.n)

    def enter(self, it, per):
        self.start, self.per = self.n, per
        self.base = it * per

    def leave(self, times):
        assert self.n - self.start == self.per, (self.n - self.start, self.per)
        self.n = self.start + times * self.per
        self.base = 0


def flow_step(nc, xs, xp, wblocks, pack, vecs, csil_in, consts, gfin, y_out, yp_out, st_out):
    ctx = ExitStack()
    with ctx:
        def sem(name):
            return ctx.enter_context(nc.semaphore(name))

        def scratch(name, n=KT):
            return nc.dram_tensor(name, [n, P, T], F32, kind="Internal").ap()

        xt_d, xa_d, xb_d, ga_d, gb_d = (scratch(n) for n in ("xt_d", "xa_d", "xb_d", "ga_d", "gb_d"))

        banks = [ctx.enter_context(nc.psum_tensor(f"bank{i}", [P, 512], F32)) for i in range(8)]

        def sb(st, name, shape, dt=F32):
            return st.enter_context(nc.sbuf_tensor(name, shape, dt))

        ring = [sb(ctx, f"ring{s}", [P, KT, P]) for s in range(RING)]
        ident = sb(ctx, "ident", [P, P])
        bones = sb(ctx, "bones", [P, P])
        ones = sb(ctx, "ones", [P, P])
        mods = sb(ctx, "mods", [P, 48, 2])
        csil = sb(ctx, "csil", [P, KT, 2])
        eps_t = sb(ctx, "eps_t", [P, 2])
        vec = sb(ctx, "vec", [P, 48 + 16])
        mul1 = sb(ctx, "mul1", [P, KT, 2])
        mul2 = sb(ctx, "mul2", [P, KT, 2])
        hgt1 = sb(ctx, "hgt1", [P, KT, 2])

        mark_all = ExitStack()
        pair_st = mark_all
        xn = sb(pair_st, "xn", [P, KT, T])
        wl = sb(pair_st, "wl", [P, T])
        al = sb(pair_st, "al", [P, T])
        gl = sb(pair_st, "gl", [P, T])
        lmask = sb(pair_st, "lmask", [P, 2, LEVELS, P], BF16)
        m1t = sb(pair_st, "m1t", [P, 2, P], BF16)
        gmask = sb(pair_st, "gmask", [P, 2, 2 * P], BF16)
        cmask = sb(pair_st, "cmask", [P, T], BF16)

        pro = ExitStack()
        x0 = sb(pro, "x0", [P, NC, D])
        xnrm = sb(pro, "xnrm", [P, NC, D])
        xt_s = sb(pro, "xt_s", [P, 2, T])
        cst = sb(pro, "cst", [P, K_ALL - K_LM])
        cth = sb(pro, "cth", [P, KT, 2])
        ss1 = sb(pro, "ss1", [P, NC])
        rs1 = sb(pro, "rs1", [P, NC])
        pro.close()

        pw = ExitStack()
        pk = sb(pw, "pk", [P, PK])
        half = sb(pw, "half", [P, 6])
        rt = sb(pw, "rt", [P, T])
        kt = sb(pw, "kt", [P, T])
        kk = sb(pw, "kk", [P, T])
        kds = sb(pw, "kds", [P, T])
        vp = sb(pw, "vp", [P, NC, 2, P])
        ar = [sb(pw, f"ar{d}", [P, NC, 2, C]) for d in range(2)]
        kp = [[sb(pw, f"kp{d}{h}", [P, T]) for h in range(2)] for d in range(2)]
        bp = [[sb(pw, f"bp{d}{h}", [P, T]) for h in range(2)] for d in range(2)]
        mid = [sb(pw, f"mid{d}", [P, NC]) for d in range(2)]
        emid = [sb(pw, f"emid{d}", [P, NC]) for d in range(2)]
        gstep = [sb(pw, f"gstep{d}", [P, NC]) for d in range(2)]
        yf, yb = kt, kk
        sfin = sb(pw, "sfin", [P, 2, HD])
        tmpst = ExitStack()
        thw = [sb(tmpst, f"thw{d}", [P, T]) for d in range(2)]
        tha = [sb(tmpst, f"tha{d}", [P, T]) for d in range(2)]
        cum = sb(tmpst, "cum", [P, T])
        en = sb(tmpst, "en", [P, T])
        tmp = sb(tmpst, "tmp", [P, T])
        cct = sb(tmpst, "cct", [P, T])
        cv = sb(tmpst, "cv", [P, T])
        gat = sb(tmpst, "gat", [P, T])
        tmpst.close()
        gmat = [[[sb(pw, f"gmat{q}{d}{h}", [P, 4, P]) for h in range(2)] for d in range(2)] for q in range(2)]
        tt = [[sb(pw, f"tt{q}{d}", [P, 2, P]) for d in range(2)] for q in range(2)]
        tm = [sb(pw, f"tm{d}", [P, 2, P]) for d in range(2)]
        p1 = [sb(pw, f"p1{d}", [P, 2, P]) for d in range(2)]
        tok = [[sb(pw, f"tok{q}{d}", [P, 2, P]) for d in range(2)] for q in range(2)]
        urp = [sb(pw, f"urp{d}", [P, 2, P]) for d in range(2)]
        up = [sb(pw, f"up{d}", [P, 2, P]) for d in range(2)]
        state = [[sb(pw, f"state{d}{q}", [P, P]) for q in range(2)] for d in range(2)]
        snew = [sb(pw, f"snew{d}", [P, P]) for d in range(2)]
        pw.close()
        pair_st.close()

        fin = ExitStack()
        xa = sb(fin, "xa", [P, KT, T])
        xb = sb(fin, "xb", [P, KT, T])
        mix = sb(fin, "mix", [P, KT, T])
        x2 = sb(fin, "x2", [P, KT, T])
        gts = sb(fin, "gts", [P, 2, 2, T])
        xts = sb(fin, "xts", [P, 2, T])
        xn2, hid = xb, mix
        sq2 = gts[:, :, 0, :]
        rs2 = gts[:, 0, 1, :]
        mtmp = sb(fin, "mtmp", [P, GN])
        yo = xa[:, :, :].rearrange("p k t -> p (k t)")
        gf = sb(fin, "gf", [P, D])
        squares = hid[:, :, :].rearrange("p k t -> p (k t)")
        fss = sb(fin, "fss", [P, NC, 2])
        frs = sb(fin, "frs", [P, NC])
        fin.close()

        names = """x_in cst_in mask_in pro_full pro_act pro_dve xt_out0 xt_out1 cst_ok ss_ok rs_a1 xnrm_ok csil_a csil_ok ada1_full
            zero_ok lora_ok pk_in pj_full half_ok ada_full ada_ok kksq_ok nrms_ok lw_ok exp_ok prod_ok yc_ok
            ysq_ok s0_ok gram_full gram_ok tok_full tok_ok tt0_ok p1_full p1_ok dt_full tt_ok tr_full tm_ok
            ur_full ur_ok u_full u_ok sy_full s_ok y_ok sf_ok xb_out xa_out ga_out sf_out act_chain dve_chain
            pool_chain ab_in gt_in xt_in o_full o_free mix_ok sq_ok sum_full rs_a2 n2_ok h_ok
            fin_full fin_sq fin_sum fin_std fin_free fin_out gf_in""".split()
        S = {n: ctx.enter_context(nc.semaphore(n)) for n in names}
        w_full = [ctx.enter_context(nc.semaphore(f"w_full{s}")) for s in range(RING)]
        ev = {e: ctx.enter_context(nc.semaphore(f"emptied_by_{e}")) for e in "AD"}
        PJ = G * len(GROUPS)
        NS = 2 * (NC - 1)
        NL = 2 * LEVELS
        MIX_FILLS, WO_FILLS = 6 * KT, 3 * KT

        def upto(g):
            return emptied(GI[g], G - 1)[1]

        def s_n(j, d):
            return 2 * (j if j < NC_LAT else j - 1) + d + 1

        def kinds(cg):
            a, b = cg * GN, (cg + 1) * GN
            return [(a, min(b, LAT), 0)] + ([(LAT, b, 1)] if b > LAT else [])

        def cols(cg):
            return slice(cg * GN, (cg + 1) * GN)

        def diag(x):
            return x.rearrange("p h v -> p (h v)").rearrange("p (x v) -> p x v", v=HD)[:, 0::3, :]

        def heads(x):
            return x.rearrange("p (h v) -> p h v", h=2)

        block = ctx.enter_context(nc.Block())

        @block.sync
        def _(sp):
            def load(b, slot):
                sp.dma_start(ring[slot][:], wblocks[b]).then_inc(w_full[slot], 16)

            for dst, k in ((ident, K_ID), (bones, K_BO), (ones, K_ONE)):
                sp.dma_start(dst[:], consts[:, k:k + P]).then_inc(S["cst_in"], 16)
            sp.dma_start(csil[:], csil_in).then_inc(S["cst_in"], 16)
            sp.dma_start(vec[:], vecs).then_inc(S["cst_in"], 16)
            for i in range(NC_LAT):
                sp.dma_start(x0[:, i, :], xs[i * P:(i + 1) * P, :]).then_inc(S["x_in"], 16)
            sp.dma_start(x0[:, NC_LAT, :], xp).then_inc(S["x_in"], 16)
            for b in range(RING):
                load(b, b)
            sp.dma_start(cst[:], consts[:, K_LM:]).then_inc(S["mask_in"], 16)
            for b in range(RING, N_PRO + RING):
                if b - RING < N_ADA_FIRST:
                    sp.wait_ge(S["ada1_full"], b - RING + 1)
                else:
                    sp.wait_ge(S["pro_full"], 2 * G * KT + G * (b - RING - N_ADA_FIRST + 1))
                load(b, b % RING)
            order = ["r", "k", "v", "cc", "ch", "cb", "za", "zb"]
            with sp.Fori(0, PAIRS) as p:
                sp.dma_start(pk[:], pack[p]).then_inc(S["pk_in"], 16)
                for k in range(RING, PAIR_BLOCKS + RING):
                    if k - RING < len(order):
                        sp.wait_ge(S["pj_full"], PJ * p + G * (GI[order[k - RING]] + 1))
                    else:
                        sp.wait_ge(S["ada_full"], 4 * p + k - RING - len(order) + 1)
                    load(PAIR_BLOCKS * p + (N_PAIR0 + k), (N_PAIR0 + k) % RING)
                    if k == RING + 6:
                        sp.wait_ge(ev["D"], N_EV["D"] * p + upto("cb"))
                        sp.dma_start(xb_d[p], cv[:]).then_inc(S["xb_out"], 16)
                        sp.wait_ge(ev["A"], N_EV["A"] * p + upto("za"))
                        sp.dma_start(ga_d[p], gat[:]).then_inc(S["ga_out"], 16)
                sp.wait_ge(ev["A"], N_EV["A"] * p + upto("zb"))
                sp.dma_start(gb_d[p], gat[:]).then_inc(S["ga_out"], 16)
                sp.wait_ge(S["sf_ok"], 4 * p + 4)
                for d in range(2):
                    sp.dma_start(st_out[d, p], sfin[:, d, :]).then_inc(S["sf_out"], 16)
                sp.wait_ge(ev["D"], N_EV["D"] * p + upto("g2"))
                sp.dma_start(xa_d[p], rt[:]).then_inc(S["xa_out"], 16)
            with sp.Fori(0, (N_BLOCKS - N_MIX0 - RING) // RING) as i:
                for s in range(RING):
                    sp.wait_ge(S["o_full"], G * RING * i + G * (s + 1))
                    load(RING * i + (N_MIX0 + RING + s), (N_MIX0 + s) % RING)

        @block.gpsimd
        def _(pool):
            ch = Chain(pool, S["pool_chain"])
            for c in range(KT):
                pool.wait_ge(S["pro_act"], G * (c + 1))
                pool.dma_start(xt_d[c], xt_s[:, c % 2, :]).then_inc(S[f"xt_out{c % 2}"], 16)
            pool.wait_ge(S["pro_full"], 2 * G * KT)
            with pool.Fori(0, PAIRS) as p:
                ch.enter(p, 2 * NC)
                for j in range(NC):
                    for d in range(2):
                        q = j % 2
                        pool.wait_ge(S["gram_ok"], 4 * NC * p + 4 * j + 2 * d + 2)
                        for h in range(2):
                            ins = nc.gpsimd.tensor_tensor(tt[q][d][:, h, :], gmat[q][d][h][:, 0, :], m1t[:, d, :], ALU.mult)
                        ch.step(ins)
                        ch.settle()
                        for h in range(2):
                            ins = nc.gpsimd.tensor_tensor(tt[q][d][:, h, :], tt[q][d][:, h, :], ident[:], ALU.add)
                        ins.then_inc(S["tt0_ok"], 1)
            ch.leave(PAIRS)
            for name, n in (("xa_out", PAIRS), ("xb_out", PAIRS), ("ga_out", 2 * PAIRS), ("sf_out", 2 * PAIRS), ("xt_out0", KT // 2), ("xt_out1", KT // 2)):
                pool.wait_ge(S[name], 16 * n)
            for k in range(KT):
                pool.dma_start(xa[:, k, :], xa_d[k]).then_inc(S["ab_in"], 16)
                pool.dma_start(xb[:, k, :], xb_d[k]).then_inc(S["ab_in"], 16)
            pool.dma_start(gf[:], gfin).then_inc(S["gf_in"], 16)
            for m in range(KT):
                if m >= 2:
                    pool.wait_ge(S["mix_ok"], m - 1)
                pool.dma_start(gts[:, m % 2, 0, :], ga_d[m]).then_inc(S["gt_in"], 16)
                pool.dma_start(gts[:, m % 2, 1, :], gb_d[m]).then_inc(S["gt_in"], 16)
                pool.wait_ge(S["gt_in"], 32 * (m + 1))
            for m in range(KT):
                if m >= 2:
                    pool.wait_ge(S["o_free"], WAVE + MIX_FILLS + G * (m - 1))
                pool.dma_start(xts[:, m % 2, :], xt_d[m]).then_inc(S["xt_in"], 16)
                pool.wait_ge(S["xt_in"], 16 * (m + 1))
            for i in range(NC):
                pool.wait_ge(S["fin_free"], 2 * i + 2)
                dst = y_out[i * P:(i + 1) * P, :] if i < NC_LAT else yp_out
                pool.dma_start(dst, yo[:, i * D:(i + 1) * D]).then_inc(S["fin_out"], 16)
            pool.wait_ge(S["fin_out"], 16 * NC)

        @block.tensor
        def _(pe):
            def mm(out, lhsT, rhs, start, stop):
                return nc.tensor.matmul(out, lhsT, rhs, start=start, stop=stop)

            def weights(b, it=0, per=0):
                pe.wait_ge(w_full[b % RING], it * (16 * per // RING) + 16 * (b // RING + 1))
                return ring[b % RING]

            pe.wait_ge(S["cst_in"], 5 * 16)
            pe.wait_ge(S["x_in"], 16 * NC)
            for c in range(KT):
                for cg in range(G):
                    n = G * c + cg
                    if n >= WAVE:
                        pe.wait_ge(S["pro_act"], n - WAVE + 1)
                    for i in range(G):
                        ins = nc.tensor.transpose(banks[n % WAVE][:, i * P:(i + 1) * P], x0[:, cg * G + i, c * P:(c + 1) * P], ident[:])
                    ins.then_inc(S["pro_full"], 1)
            pe.wait_ge(S["csil_ok"], 1)
            for b in range(N_ADA_FIRST):
                w = weights(b)
                for k in range(KT):
                    ins = mm(banks[6][:, 2 * b:2 * b + 2], w[:, k, :], csil[:, k, :], k == 0, k == KT - 1)
                ins.then_inc(S["ada1_full"], 1)
            pe.wait_ge(S["xnrm_ok"], 1)
            for c in range(KT):
                for cg in range(G):
                    n = G * (KT + c) + cg
                    if n - WAVE < G * KT:
                        pe.wait_ge(S["pro_act"], n - WAVE + 1)
                    else:
                        pe.wait_ge(S["pro_dve"], n - WAVE - G * KT + 1)
                    for i in range(G):
                        ins = nc.tensor.transpose(banks[n % WAVE][:, i * P:(i + 1) * P], xnrm[:, cg * G + i, c * P:(c + 1) * P], ident[:])
                    ins.then_inc(S["pro_full"], 1)
            pe.wait_ge(S["pro_dve"], G * KT)
            for b in range(3):
                w = weights(N_ADA_FIRST + b)
                for cg in range(G):
                    n = G * (2 * KT + b) + cg
                    if n - WAVE >= 2 * G * KT:
                        pe.wait_ge(S["pro_act"], n - WAVE - G * KT + 1)
                    for k in range(KT):
                        ins = mm(banks[n % WAVE][:, :GN], w[:, k, :], xn[:, k, cols(cg)], k == 0, k == KT - 1)
                    ins.then_inc(S["pro_full"], 1)
            pe.wait_ge(S["pro_act"], G * (KT + 3))

            with pe.Fori(0, PAIRS) as p:
                def bank_free(g, cg):
                    if g:
                        e, n = emptied(g - 1, cg)
                        pe.wait_ge(ev[e], p * N_EV[e] + n)

                def project(name, nb):
                    w = weights(N_PAIR0 + nb, p, PAIR_BLOCKS)
                    for cg in range(G):
                        bank_free(GI[name], cg)
                        for k in range(KT):
                            ins = mm(banks[cg][:, :GN], w[:, k, :], xn[:, k, cols(cg)], k == 0, k == KT - 1)
                        ins.then_inc(S["pj_full"], 1)

                def single(name, lhsT, rhs):
                    for cg in range(G):
                        bank_free(GI[name], cg)
                        mm(banks[cg][:, :GN], lhsT, rhs[:, cols(cg)], True, True).then_inc(S["pj_full"], 1)

                project("r", 0)
                project("k", 1)
                w = weights(N_PAIR0 + 2, p, PAIR_BLOCKS)
                for cg in range(G):
                    bank_free(GI["v"], cg)
                    for i in range(G):
                        t = cg * G + i
                        for k in range(KT):
                            ins = mm(banks[cg][:, i * P:(i + 1) * P], xn[:, k, t * P:(t + 1) * P], w[:, k, :], k == 0, k == KT - 1)
                    ins.then_inc(S["pj_full"], 1)
                pe.wait_ge(S["pk_in"], 16 * p + 16)
                for d in range(2):
                    single(f"w{d}", pk[:, PK_W2 + d * P:PK_W2 + (d + 1) * P], wl)
                    single(f"a{d}", pk[:, PK_A2 + d * P:PK_A2 + (d + 1) * P], al)
                pe.wait_ge(S["kksq_ok"], p + 1)
                single("ks", bones[:], tmp)
                for nb, name in enumerate(("cc", "ch", "cb", "za", "zb")):
                    project(name, 3 + nb)
                for b in range(4):
                    w = weights(N_PAIR0 + 8 + b, p, PAIR_BLOCKS)
                    for k in range(KT):
                        ins = mm(banks[7][:, 2 * b:2 * b + 2], w[:, k, :], csil[:, k, :], k == 0, k == KT - 1)
                    ins.then_inc(S["ada_full"], 1)

                def serial_ur(j, d):
                    q, c = j % 2, chunk(d, j)
                    o = banks[6 + d][:, 0:P]
                    if 0 < j < NC_LAT:
                        pe.wait_ge(S["s_ok"], NS * p + s_n(j - 1, d))
                    if j < NC_LAT:
                        mm(o, ar[d][:, c, 0, :], state[d][q][:], True, False)
                    mm(o, gmat[q][d][0][:, 2, :], vp[:, c, 0, :], j == NC_LAT, False)
                    mm(o, gmat[q][d][1][:, 2, :], vp[:, c, 1, :], False, True).then_inc(S["ur_full"], 1)

                def serial_u(j, d):
                    q = j % 2
                    pe.wait_ge(S["ur_ok"], 2 * NC * p + 2 * j + d + 1)
                    o = banks[6 + d][:, P:2 * P]
                    mm(o, tt[q][d][:, 0, :], urp[d][:, 0, :], True, False)
                    mm(o, tt[q][d][:, 1, :], urp[d][:, 1, :], False, True).then_inc(S["u_full"], 1)

                def serial_sy(j, d):
                    q, c = j % 2, chunk(d, j)
                    pe.wait_ge(S["u_ok"], 2 * NC * p + 2 * j + d + 1)
                    if j != NC_LAT - 1:
                        o = heads(banks[6 + d][:, 2 * P:3 * P])
                        mm(o, tok[q][d][:, 0, :], diag(up[d][:]), True, False)
                        mm(o, tok[q][d][:, 1, :], diag(vp[:, c]), False, True)
                    o = banks[6 + d][:, 3 * P:4 * P]
                    if j < NC_LAT:
                        mm(o, state[d][q][:], ar[d][:, c, 1, :], True, False)
                    for h in range(2):
                        mm(o, up[d][:, h, :], gmat[q][d][h][:, 1, :], j == NC_LAT and h == 0, False)
                    for h in range(2):
                        ins = mm(o, vp[:, c, h, :], gmat[q][d][h][:, 3, :], False, h == 1)
                    ins.then_inc(S["sy_full"], 1)

                def serial_free(j, d):
                    if j != NC_LAT - 1:
                        pe.wait_ge(S["s_ok"], NS * p + s_n(j, d))
                    pe.wait_ge(S["y_ok"], 2 * NC * p + 2 * j + d + 1)

                pe.wait_ge(S["s0_ok"], 2 * p + 2)
                for j in range(NC):
                    q = j % 2
                    for d in range(2):
                        c = chunk(d, j)
                        cs = slice(c * C, (c + 1) * C)
                        rhs = ar[d][:, c, :, :].rearrange("p a t -> p (a t)")
                        for h in range(2):
                            if h == 0 and (j or d):
                                pe.wait_ge(S["gram_ok"], 4 * NC * p + 4 * j + 2 * d - 1)
                            if h == 1 and j:
                                pe.wait_ge(S["tt_ok"], NL * NC * p + NL * (j - 1) + 2 * LEVELS - 1 + d)
                            o = banks[3 if h == 0 else 4 + d]
                            mm(o[:, 0:2 * P], bp[d][h][:, cs], rhs, True, True)
                            mm(o[:, 2 * P:4 * P], kp[d][h][:, cs], rhs, True, True).then_inc(S["gram_full"], 1)
                        if j > 1:
                            serial_free(j - 2, d)
                        for x, src in enumerate((bp, kp)):
                            for h in range(2):
                                ins = nc.tensor.transpose(banks[6 + d][:, (2 * x + h) * P:(2 * x + h + 1) * P], src[d][h][:, cs], ident[:])
                        ins.then_inc(S["tok_full"], 1)
                    for lev in range(LEVELS + 1):
                        at = NL * NC * p + NL * j + 2 * (lev - 1) + 1
                        if lev:
                            for d in range(2):
                                pe.wait_ge(S["tm_ok"], at + d)
                                for h in range(2):
                                    ins = mm(banks[4 + d][:, h * P:(h + 1) * P], gmat[q][d][h][:, 0, :], tm[d][:, h, :], True, True)
                                ins.then_inc(S["p1_full"], 1)
                            for d in range(2):
                                pe.wait_ge(S["p1_ok"], at + d)
                                for h in range(2):
                                    ins = mm(banks[4 + d][:, h * P:(h + 1) * P], p1[d][:, h, :], tt[q][d][:, h, :], True, True)
                                ins.then_inc(S["dt_full"], 1)
                        if j:
                            for d in range(2):
                                if lev == 0:
                                    pe.wait_ge(S["tok_ok"], 2 * NC * p + 2 * j + d + 1)
                                    serial_ur(j - 1, d)
                                elif lev == 1:
                                    serial_u(j - 1, d)
                                elif lev == 2:
                                    serial_sy(j - 1, d)
                        if lev < LEVELS:
                            for d in range(2):
                                if lev == 0:
                                    pe.wait_ge(S["tt0_ok"], 2 * NC * p + 2 * j + d + 1)
                                else:
                                    pe.wait_ge(S["tt_ok"], at + d)
                                for h in range(2):
                                    ins = nc.tensor.transpose(banks[4 + d][:, h * P:(h + 1) * P], tt[q][d][:, h, :], ident[:])
                                ins.then_inc(S["tr_full"], 1)
                for d in range(2):
                    pe.wait_ge(S["tt_ok"], NL * NC * p + NL * NC - 1 + d)
                    serial_free(NC - 2, d)
                    serial_ur(NC - 1, d)
                for d in range(2):
                    serial_u(NC - 1, d)
                for d in range(2):
                    serial_sy(NC - 1, d)
                pe.wait_ge(S["prod_ok"], p + 1)
                single("bon", bones[:], kds)
                for cg in range(G):
                    bank_free(GI["vt"], cg)
                    for i in range(G):
                        for h in range(2):
                            ins = mm(banks[cg][:, i * P:(i + 1) * P], vp[:, cg * G + i, h, :], ident[:], h == 0, h == 1)
                    ins.then_inc(S["pj_full"], 1)
                pe.wait_ge(S["yc_ok"], p + 1)
                single("mu", bones[:], yf)
                pe.wait_ge(S["ysq_ok"], p + 1)
                single("var", bones[:], yb)
                pe.wait_ge(S["lora_ok"], 1)
                single("g2", pk[:, PK_G2:PK_G2 + P], gl)
                pe.wait_ge(ev["D"], N_EV["D"] * p + N_EV["D"])

            pe.wait_ge(S["ab_in"], 16 * 2 * KT)

            def wave(n0, it, per_it, b, per_b, src):
                w = weights(b, it, per_b)
                for cg in range(G):
                    n = n0 + cg
                    pe.wait_ge(S["o_free"], it * per_it + n + 1)
                    for k in range(KT):
                        ins = mm(banks[n % WAVE][:, :GN], w[:, k, :], src[:, k, cols(cg)], k == 0, k == KT - 1)
                    ins.then_inc(S["o_full"], 1)

            with pe.Fori(0, KT // 2) as i:
                for s in range(2):
                    wave(6 * s, i, 12, N_MIX0 + 2 * s, 4, xa)
                    wave(6 * s + 3, i, 12, N_MIX0 + 2 * s + 1, 4, xb)
            pe.wait_ge(S["mix_ok"], KT)
            with pe.Fori(0, KT // 4) as i:
                for s in range(4):
                    wave(MIX_FILLS + 3 * s, i, 12, N_WO0 + s, 4, mix)
            n_ff = MIX_FILLS + WO_FILLS
            pe.wait_ge(S["o_free"], WAVE + n_ff)
            for m in range(KT):
                pe.wait_ge(S["sq_ok"], m + 1)
                for cg in range(G):
                    ins = mm(banks[cg][:, :GN], ones[:], sq2[:, m % 2, cols(cg)], m == 0, m == KT - 1)
                ins.then_inc(S["sum_full"], 1)
            pe.wait_ge(S["n2_ok"], KT)
            with pe.Fori(0, FFQ) as i:
                for s in range(KT):
                    wave(n_ff + 3 * s, i, 6 * KT, N_FF0 + s, 2 * KT, xn2)
                pe.wait_ge(S["h_ok"], G * KT * i + G * KT)
                for s in range(KT):
                    wave(n_ff + 3 * (KT + s), i, 6 * KT, N_FF0 + KT + s, 2 * KT, hid)
            pe.wait_ge(S["o_free"], WAVE + n_ff + FFQ * 6 * KT)
            for t in range(NC):
                if t >= 3:
                    pe.wait_ge(S["fin_free"], 2 * (t - 3) + 2)
                for c in range(KT):
                    ins = nc.tensor.transpose(banks[2 * (t % 3) + c // 4][:, (c % 4) * P:(c % 4 + 1) * P], x2[:, c, t * P:(t + 1) * P], ident[:])
                ins.then_inc(S["fin_full"], 1)

        @block.scalar
        def _(act):
            A = nc.scalar.activation
            ch = Chain(act, S["act_chain"])
            act.wait_ge(S["cst_in"], 5 * 16)
            A(cth[:], csil[:], ACT.Tanh, scale=0.5).then_inc(S["csil_a"], 1)
            act.wait_ge(S["x_in"], 16 * NC)
            for i in range(NC):
                A(xnrm[:, i, :], x0[:, i, :], ACT.Square, accum_out=ss1[:, i:i + 1]).then_inc(S["ss_ok"], 1)
            act.wait_ge(S["ss_ok"], NC)
            act.wait_ge(S["cst_ok"], 1)
            A(rs1[:], ss1[:], ACT.Sqrt, scale=1.0 / D, bias=eps_t[:, 0:1]).then_inc(S["rs_a1"], 1)
            for c in range(KT):
                if c >= 2:
                    act.wait_ge(S[f"xt_out{c % 2}"], 16 * (c // 2))
                for cg in range(G):
                    n = G * c + cg
                    act.wait_ge(S["pro_full"], n + 1)
                    A(xt_s[:, c % 2, cols(cg)], banks[n % WAVE][:, :GN], ACT.Copy).then_inc(S["pro_act"], 1)
            for b, (dst, f, sc) in enumerate(((wl, ACT.Tanh, 1.0), (al, ACT.Copy, 1.0), (gl, ACT.Tanh, 0.5))):
                for cg in range(G):
                    n = G * (2 * KT + b) + cg
                    act.wait_ge(S["pro_full"], n + 1)
                    A(dst[:, cols(cg)], banks[n % WAVE][:, :GN], f, scale=sc).then_inc(S["pro_act"], 1)

            with act.Fori(0, PAIRS) as p:
                def empty(name, out, func, **kw):
                    for cg in range(G):
                        act.wait_ge(S["pj_full"], PJ * p + G * GI[name] + cg + 1)
                        A(out(cg), banks[cg][:, :GN] if name != "v" else
                          banks[cg][:, :GN].rearrange("p (t h v) -> p t h v", h=2, v=HD), func, **kw).then_inc(ev["A"], 1)

                def vdiag(cg):
                    x = vp[:, cg * G:(cg + 1) * G, :, :].rearrange("p t h v -> p t (h v)")
                    return x.rearrange("p t (x v) -> p t x v", v=HD)[:, :, 0::3, :]

                empty("r", lambda cg: rt[:, cols(cg)], ACT.Copy)
                empty("k", lambda cg: kt[:, cols(cg)], ACT.Copy)
                act.wait_ge(S["zero_ok"], 1)
                empty("v", vdiag, ACT.Copy)
                act.wait_ge(S["half_ok"], p + 1)
                for d in range(2):
                    empty(f"w{d}", lambda cg: thw[d][:, cols(cg)], ACT.Tanh, scale=0.5, bias=half[:, d:d + 1])
                    empty(f"a{d}", lambda cg: tha[d][:, cols(cg)], ACT.Tanh, scale=0.5, bias=half[:, 2 + d:3 + d])
                act.wait_ge(ev["D"], N_EV["D"] * p + upto("ks"))
                A(en[:], en[:], ACT.Sqrt).then_inc(S["nrms_ok"], 1)
                empty("cc", lambda cg: cct[:, cols(cg)], ACT.Copy)
                for d in range(2):
                    act.wait_ge(S["lw_ok"], 2 * p + d + 1)
                    A(en[:], cum[:], ACT.Exp, scale=-1.0).then_inc(S["exp_ok"], 1)
                    act.wait_ge(S["exp_ok"], 8 * p + 4 * d + 1)
                    A(cum[:], cum[:], ACT.Exp).then_inc(S["exp_ok"], 1)
                    A(thw[d][:], thw[d][:], ACT.Exp).then_inc(S["exp_ok"], 1)
                    A(emid[d][:], mid[d][:], ACT.Exp).then_inc(S["exp_ok"], 1)
                empty("za", lambda cg: gat[:, cols(cg)], ACT.Tanh, scale=0.5)
                act.wait_ge(S["ga_out"], 32 * p + 16)
                empty("zb", lambda cg: gat[:, cols(cg)], ACT.Tanh, scale=0.5)

                def at(j, d):
                    return 2 * NC * p + 2 * j + d + 1

                def to_diag(dst, j, d, full, col, ok):
                    act.wait_ge(S[full], at(j, d))
                    A(diag(dst[d][:]), heads(banks[6 + d][:, col:col + P]), ACT.Copy).then_inc(S[ok], 1)

                def outputs(j, d):
                    act.wait_ge(S["sy_full"], at(j, d))
                    if j != NC_LAT - 1:
                        act.wait_ge(S["s_ok"], NS * p + s_n(j, d))
                    c = chunk(d, j)
                    A((yf, yb)[d][:, c * C:(c + 1) * C], banks[6 + d][:, 3 * P:4 * P], ACT.Copy).then_inc(S["y_ok"], 1)

                for j in range(NC):
                    q = j % 2
                    for d in range(2):
                        act.wait_ge(S["tok_full"], at(j, d))
                        src = banks[6 + d][:, :].rearrange("p (x y v) -> p x y v", x=2, v=HD)[:, :, 0::3, :]
                        dst = tok[q][d][:].rearrange("p x (h v) -> p x h v", h=2)
                        A(dst, src, ACT.Copy).then_inc(S["tok_ok"], 1)
                    for lev in range(LEVELS):
                        if j:
                            for d in range(2):
                                if lev == 0:
                                    to_diag(urp, j - 1, d, "ur_full", 0, "ur_ok")
                                elif lev == 1:
                                    to_diag(up, j - 1, d, "u_full", P, "u_ok")
                                elif lev == 2:
                                    outputs(j - 1, d)
                        for d in range(2):
                            act.wait_ge(S["tr_full"], NL * NC * p + NL * j + 2 * lev + d + 1)
                            A(tm[d][:], heads(banks[4 + d][:, 0:2 * P]), ACT.Copy).then_inc(S["tm_ok"], 1)
                for d in range(2):
                    to_diag(urp, NC - 1, d, "ur_full", 0, "ur_ok")
                for d in range(2):
                    to_diag(up, NC - 1, d, "u_full", P, "u_ok")
                for d in range(2):
                    outputs(NC - 1, d)
                empty("bon", lambda cg: cct[:, cols(cg)], ACT.Copy)
                empty("var", lambda cg: en[:, cols(cg)], ACT.Sqrt, scale=1.0 / HD, bias=eps_t[:, 1:2])
                act.wait_ge(S["xa_out"], 16 * p + 16)

            n_sq = WAVE + MIX_FILLS
            for m in range(KT):
                act.wait_ge(S["o_free"], n_sq + G * (m + 1))
                if m >= 2:
                    act.wait_ge(S["sum_full"], m - 1)
                A(sq2[:, m % 2, :], x2[:, m, :], ACT.Square).then_inc(S["sq_ok"], 1)
            act.wait_ge(S["sum_full"], KT)
            for cg in range(G):
                A(rs2[:, cols(cg)], banks[cg][:, :GN], ACT.Sqrt, scale=1.0 / D, bias=eps_t[:, 0:1]).then_inc(S["rs_a2"], 1)
            with act.Fori(0, FFQ) as i:
                for s in range(KT):
                    for cg in range(G):
                        act.wait_ge(S["o_free"], 6 * KT * i + (n_sq + WO_FILLS + G * s + cg + 1))
                        A(hid[:, s, cols(cg)], hid[:, s, cols(cg)], ACT.Square).then_inc(S["h_ok"], 1)
            for t in range(NC):
                act.wait_ge(S["fin_full"], t + 1)
                for i in range(2):
                    A(squares[:, (2 * t + i) * 512:(2 * t + i + 1) * 512], banks[2 * (t % 3) + i][:, :], ACT.Square, accum_out=fss[:, t, i:i + 1]).then_inc(S["fin_sq"], 1)
                act.wait_ge(S["fin_sum"], t + 1)
                A(frs[:, t:t + 1], fss[:, t, 0:1], ACT.Sqrt, scale=1.0 / D, bias=eps_t[:, 0:1]).then_inc(S["fin_std"], 1)

        @block.vector
        def _(dve):
            V = nc.vector
            ch = Chain(dve, S["dve_chain"])
            mul, add, sub = ALU.mult, ALU.add, ALU.subtract
            stt = V.scalar_tensor_tensor

            def bc(x, n):
                return x.to_broadcast([P, x.shape[1], n]) if len(x.shape) == 3 else x.unsqueeze(2).to_broadcast([P, x.shape[1], n])

            ch.step(V.memset(eps_t[:, 0:1], EPS))
            V.memset(eps_t[:, 1:2], LNX_EPS).then_inc(S["cst_ok"], 1)
            dve.wait_ge(S["csil_a"], 1)
            ch.step(V.tensor_scalar(cth[:], cth[:], 0.5, 0.5, mul, add))
            ch.settle()
            V.tensor_tensor(csil[:], csil[:], cth[:], mul).then_inc(S["csil_ok"], 1)
            dve.wait_ge(S["rs_a1"], 1)
            ch.step(V.reciprocal(rs1[:], rs1[:]))
            ch.settle()
            for i in range(NC):
                ins = V.tensor_scalar(xnrm[:, i, :], x0[:, i, :], rs1[:, i:i + 1], None, mul)
            ins.then_inc(S["xnrm_ok"], 1)
            dve.wait_ge(S["mask_in"], 16)
            for dst, k, n in ((lmask[:].rearrange("p a b c -> p (a b c)"), K_LM, 12 * P), (m1t[:].rearrange("p a b -> p (a b)"), K_M1, 2 * P),
                              (gmask[:].rearrange("p a b -> p (a b)"), K_GM, 4 * P), (cmask[:], K_CM, T)):
                ch.step(V.tensor_copy(dst, cst[:, k - K_LM:k - K_LM + n]))
            dve.wait_ge(S["ada1_full"], N_ADA_FIRST)
            ch.step(V.tensor_tensor(mods[:, 0:16, :], banks[6][:, 0:32].rearrange("p (b c) -> p b c", c=2), bc(vec[:, 0:16], 2), add))
            ch.settle()
            ch.step(V.tensor_scalar(mul1[:], mods[:, 8:16, :], 1.0, None, add))
            ch.settle()
            ch.step(V.tensor_tensor(mul1[:], mul1[:], bc(vec[:, 48:56], 2), mul))
            ch.settle()
            for c in range(KT):
                for cg in range(G):
                    n = G * (KT + c) + cg
                    dve.wait_ge(S["pro_full"], n + 1)
                    for a, b, kind in kinds(cg):
                        ins = V.tensor_scalar(xn[:, c, a:b], banks[n % WAVE][:, a - cg * GN:b - cg * GN],
                                              mul1[:, c, kind:kind + 1], mods[:, c, kind:kind + 1], mul, add)
                    ins.then_inc(S["pro_dve"], 1)
            dve.wait_ge(S["xt_out0"], 8 * KT)
            dve.wait_ge(S["xt_out1"], 8 * KT)
            for x in [b for pair in kp + bp for b in pair]:
                ch.step(V.memset(x[:], 0.0))
            V.memset(vp[:], 0.0).then_inc(S["zero_ok"], 1)
            dve.wait_ge(S["pro_act"], G * (KT + 3))
            V.tensor_scalar(gl[:], gl[:], 0.5, 0.5, mul, add).then_inc(S["lora_ok"], 1)
            dve.wait_ge(S["zero_ok"], 1)
            ch.settle()

            with dve.Fori(0, PAIRS) as p:
                ch.enter(p, CH_PAIR)

                def full(name, cg):
                    dve.wait_ge(S["pj_full"], PJ * p + G * GI[name] + cg + 1)

                def par(i):
                    return pk[:, PK_VEC + i:PK_VEC + i + 1]

                def filled(name):
                    dve.wait_ge(ev["A"], N_EV["A"] * p + upto(name))

                dve.wait_ge(S["pk_in"], 16 * p + 16)
                ch.step(V.tensor_scalar(half[:, 0:4], pk[:, PK_VEC + V_W0:PK_VEC + V_W0 + 4], 0.5, None, mul))
                ch.step(V.tensor_scalar(half[:, 4:5], par(V_KA), 0.5, None, mul))
                V.tensor_scalar(half[:, 5:6], par(V_KA), -0.5, 1.0, mul, add).then_inc(S["half_ok"], 1)
                filled("k")
                ch.step(V.tensor_scalar(kk[:], kt[:], par(V_KK), None, mul))
                ch.settle()
                V.tensor_tensor(tmp[:], kk[:], kk[:], mul).then_inc(S["kksq_ok"], 1)
                for cg in range(G):
                    full("ks", cg)
                    V.tensor_scalar(en[:, cols(cg)], banks[cg][:, :GN], 1e-12, None, ALU.max).then_inc(ev["D"], 1)
                dve.wait_ge(S["nrms_ok"], p + 1)
                ch.step(V.reciprocal(en[:], en[:]))
                ch.settle()
                ch.step(V.tensor_tensor(kk[:], kk[:], en[:], mul))
                for d in range(2):
                    filled(f"a{d}")
                    ch.step(V.tensor_scalar(thw[d][:], thw[d][:], -0.5 * DECAY, -0.5 * DECAY, mul, add))
                    ch.settle()
                    o, x = (cum[:], thw[d][:]) if d == 0 else (cum[:, ::-1], thw[d][:, ::-1])
                    ch.step(V.tensor_tensor_scan(o, cmask[:], x, 0.0, mul, add))
                    ch.settle()
                    cc3 = cum[:].rearrange("p (c t) -> p c t", t=C)
                    end = C - 1 if d == 0 else 0
                    ch.step(V.tensor_scalar(mid[d][:], cc3[:, :, end:end + 1].rearrange("p c t -> p (c t)"), 0.5, None, mul))
                    ch.settle()
                    ch.step(V.tensor_tensor(cc3, cc3, bc(mid[d][:], C), sub))
                    ch.settle()
                    V.tensor_tensor(thw[d][:], cum[:], thw[d][:], sub).then_inc(S["lw_ok"], 1)
                    kd = kds if d == 0 else tmp
                    ch.step(V.tensor_scalar(tmp[:], tha[d][:], half[:, 4:5], half[:, 5:6], mul, add))
                    ch.step(V.tensor_scalar(tha[d][:], tha[d][:], -0.5, -0.5, mul, add))
                    ch.settle()
                    ch.step(V.tensor_tensor(kd[:], tmp[:], kt[:], mul))
                    ch.step(V.tensor_tensor(tha[d][:], tha[d][:], kk[:], mul))
                    ch.settle()
                    dve.wait_ge(S["exp_ok"], 8 * p + 4 * d + 1)
                    for h in range(2):
                        hs = slice(h * HD, (h + 1) * HD)
                        ch.step(V.tensor_tensor(kp[d][h][hs, :], kd[hs, :], en[hs, :], mul))
                        ch.step(V.tensor_tensor(bp[d][h][hs, :], tha[d][hs, :], en[hs, :], mul))
                    a3 = lambda x: x.rearrange("p (c t) -> p c t", t=C)
                    dve.wait_ge(S["exp_ok"], 8 * p + 4 * d + 2)
                    ch.step(V.tensor_tensor(ar[d][:, :, 1, :], a3(rt[:]), a3(cum[:]), mul))
                    dve.wait_ge(S["exp_ok"], 8 * p + 4 * d + 3)
                    ch.step(V.tensor_tensor(ar[d][:, :, 0, :], a3(kk[:]), a3(thw[d][:]), mul))
                    dve.wait_ge(S["exp_ok"], 8 * p + 4 * d + 4)
                    g = gstep[d][:, 0:NC_LAT - 1] if d == 0 else gstep[d][:, 1:NC_LAT]
                    ch.step(V.tensor_tensor(g, emid[d][:, 0:NC_LAT - 1], emid[d][:, 1:NC_LAT], mul))
                    ch.settle()
                    if d == 0:
                        for cg in range(G):
                            full("ch", cg)
                            V.tensor_tensor(cct[:, cols(cg)], banks[cg][:, :GN], cct[:, cols(cg)], mul).then_inc(ev["D"], 1)
                ch.step(V.tensor_tensor(kds[:], kds[:], tmp[:], add))
                ch.settle()
                stt(kds[:], kds[:], par(V_RK), rt[:], mul, mul).then_inc(S["prod_ok"], 1)
                dve.wait_ge(ev["D"], N_EV["D"] * p + upto("ch"))
                ch.step(V.tensor_scalar(cv[:], cct[:], par(V_CONV + 1), None, mul))
                ch.settle()
                for u, o in ((cct[:, :LAT].rearrange("p (r w) -> p r w", w=ROW), cv[:, :LAT].rearrange("p (r w) -> p r w", w=ROW)),
                             (cct[:, LAT:].rearrange("p (r w) -> p r w", w=CTX), cv[:, LAT:].rearrange("p (r w) -> p r w", w=CTX))):
                    n = u.shape[2]
                    ch.step(stt(o[:, :, 1:n], u[:, :, 0:n - 1], par(V_CONV), o[:, :, 1:n], mul, add))
                    ch.settle()
                    ch.step(stt(o[:, :, 0:n - 1], u[:, :, 1:n], par(V_CONV + 2), o[:, :, 0:n - 1], mul, add))
                    ch.settle()
                for cg in range(G):
                    full("cb", cg)
                    V.tensor_tensor(cv[:, cols(cg)], banks[cg][:, :GN], cv[:, cols(cg)], mul).then_inc(ev["D"], 1)
                dve.wait_ge(S["ada_full"], 4 * p + 4)
                V.tensor_tensor(mods[:, bass.ds(4 * p + 16, 4), :], banks[7][:, 0:8].rearrange("p (b c) -> p b c", c=2),
                                bc(vec[:, bass.ds(4 * p + 16, 4)], 2), add).then_inc(S["ada_ok"], 1)
                dve.wait_ge(S["xb_out"], 16 * p + 16)
                dve.wait_ge(S["ga_out"], 32 * p + 32)
                for x in urp + up + [state[0][0], state[1][0]]:
                    ch.step(V.memset(x[:], 0.0))
                ch.settle()
                dve.wait_ge(S["ada_ok"], p + 1)
                for d in range(2):
                    c = chunk(d, 0)
                    for h in range(2):
                        hs = slice(h * HD, (h + 1) * HD)
                        ins = V.tensor_scalar(state[d][0][hs, hs], pk[hs, PK_ST + d * HD:PK_ST + (d + 1) * HD], emid[d][hs, c:c + 1], None, mul)
                    ins.then_inc(S["s0_ok"], 1)

                def states(j, d):
                    q, c = j % 2, chunk(d, j)
                    if j == NC_LAT - 1:
                        return
                    dve.wait_ge(S["sy_full"], 2 * NC * p + 2 * j + d + 1)
                    o = banks[6 + d]
                    if j < NC_LAT:
                        ch.step(V.tensor_tensor(snew[d][:], o[:, 2 * P:3 * P], state[d][q][:], add))
                        ch.settle()
                        stt(state[d][1 - q][:], snew[d][:], gstep[d][:, c:c + 1], bones[:], mul, mul).then_inc(S["s_ok"], 1)
                    else:
                        for h in range(2):
                            hs = slice(h * HD, (h + 1) * HD)
                            V.tensor_scalar(sfin[hs, d, :], o[hs, 2 * P + h * HD:2 * P + (h + 1) * HD],
                                            emid[d][hs, c:c + 1], None, mul).then_inc(S["sf_ok"], 1)
                        dve.wait_ge(S["sf_ok"], 4 * p + 2 * d + 2)
                        V.tensor_copy(snew[d][:, 0:1], emid[d][:, 0:1]).then_inc(S["s_ok"], 1)

                for j in range(NC):
                    q = j % 2
                    for d in range(2):
                        for h in range(2):
                            dve.wait_ge(S["gram_full"], 4 * NC * p + 4 * j + 2 * d + h + 1)
                            V.tensor_tensor(gmat[q][d][h][:].rearrange("p (x a) t -> p x (a t)", x=2),
                                            banks[3 if h == 0 else 4 + d][:, :].rearrange("p (x a) -> p x a", x=2),
                                            gmask[:, d:d + 1, :].to_broadcast([P, 2, 2 * P]), mul).then_inc(S["gram_ok"], 1)
                    for lev in range(LEVELS):
                        at = NL * NC * p + NL * j + 2 * lev + 1
                        for d in range(2):
                            dve.wait_ge(S["p1_full"], at + d)
                            V.tensor_tensor(p1[d][:], heads(banks[4 + d][:, 0:2 * P]),
                                            lmask[:, d, lev:lev + 1, :].to_broadcast([P, 2, P]), mul).then_inc(S["p1_ok"], 1)
                        for d in range(2):
                            dve.wait_ge(S["dt_full"], at + d)
                            V.tensor_tensor(tt[q][d][:], heads(banks[4 + d][:, 0:2 * P]), tt[q][d][:], add).then_inc(S["tt_ok"], 1)
                        if j and lev == 1:
                            for d in range(2):
                                states(j - 1, d)
                for d in range(2):
                    states(NC - 1, d)
                dve.wait_ge(S["y_ok"], 2 * NC * p + 2 * NC)
                V.tensor_tensor(yf[:], yf[:], yb[:], add).then_inc(S["yc_ok"], 1)
                filled("bon")
                for cg in range(G):
                    full("vt", cg)
                    V.tensor_tensor(tmp[:, cols(cg)], banks[cg][:, :GN], cct[:, cols(cg)], mul).then_inc(ev["D"], 1)
                for cg in range(G):
                    full("mu", cg)
                    stt(yf[:, cols(cg)], banks[cg][:, :GN], -1.0 / HD, yf[:, cols(cg)], mul, add).then_inc(ev["D"], 1)
                dve.wait_ge(ev["D"], N_EV["D"] * p + upto("mu"))
                V.tensor_tensor(yb[:], yf[:], yf[:], mul).then_inc(S["ysq_ok"], 1)
                filled("var")
                ch.step(V.reciprocal(en[:], en[:]))
                ch.settle()
                ch.step(V.tensor_tensor(yf[:], yf[:], en[:], mul))
                ch.settle()
                ch.step(V.tensor_scalar(yf[:], yf[:], par(V_LNW), par(V_LNB), mul, add))
                ch.settle()
                ch.step(V.tensor_tensor(yf[:], yf[:], tmp[:], add))
                ch.settle()
                for cg in range(G):
                    full("g2", cg)
                    V.tensor_tensor(rt[:, cols(cg)], banks[cg][:, :GN], yf[:, cols(cg)], mul).then_inc(ev["D"], 1)
                dve.wait_ge(S["sf_out"], 32 * p + 32)
            ch.leave(PAIRS)

            ch.step(V.tensor_scalar(mul2[:], mods[:, 32:40, :], 1.0, None, add))
            ch.settle()
            ch.step(V.tensor_tensor(mul2[:], mul2[:], bc(vec[:, 56:64], 2), mul))
            V.tensor_scalar(hgt1[:], mods[:, 16:24, :], 0.5, None, mul).then_inc(S["o_free"], WAVE)
            dve.wait_ge(S["o_free"], WAVE)
            ch.settle()
            with dve.Fori(0, KT // 2) as i:
                ch.enter(i, 4)
                for s in range(2):
                    m = 2 * i + s
                    dve.wait_ge(S["gt_in"], 64 * i + 32 * s + 32)
                    for x in range(2):
                        for cg in range(G):
                            n = 6 * s + 3 * x + cg
                            dve.wait_ge(S["o_full"], 12 * i + n + 1)
                            if x == 0:
                                stt(mix[:, m, cols(cg)], gts[:, s, 0, cols(cg)], 1.0, banks[n % WAVE][:, :GN], add, mul).then_inc(S["o_free"], 1)
                            else:
                                stt(mtmp[:], gts[:, s, 1, cols(cg)], 1.0, banks[n % WAVE][:, :GN], add, mul).then_inc(S["o_free"], 1)
                                dve.wait_ge(S["o_free"], 12 * i + (WAVE + n + 1))
                                ins = V.tensor_tensor(mix[:, m, cols(cg)], mix[:, m, cols(cg)], mtmp[:], add)
                                if cg < 2:
                                    ch.step(ins)
                                    ch.settle()
                                else:
                                    ins.then_inc(S["mix_ok"], 1)
                                    dve.wait_ge(S["mix_ok"], 2 * i + s + 1)
            ch.leave(KT // 2)
            with dve.Fori(0, KT // 4) as i:
                for s in range(4):
                    m = 4 * i + s
                    dve.wait_ge(S["xt_in"], 64 * i + 16 * s + 16)
                    for cg in range(G):
                        n = MIX_FILLS + 3 * s + cg
                        dve.wait_ge(S["o_full"], 12 * i + (n + 1))
                        for a, b, kind in kinds(cg):
                            ins = stt(x2[:, m, a:b], banks[n % WAVE][:, a - cg * GN:b - cg * GN], hgt1[:, m, kind:kind + 1], xts[:, s % 2, a:b], mul, add)
                        ins.then_inc(S["o_free"], 1)
            dve.wait_ge(S["rs_a2"], G)
            ch.step(V.reciprocal(rs2, rs2))
            ch.settle()
            for m in range(KT):
                for a, b, kind in ((0, LAT, 0), (LAT, T, 1)):
                    ch.step(stt(xn2[:, m, a:b], x2[:, m, a:b], mul2[:, m, kind:kind + 1], rs2[:, a:b], mul, mul))
                ch.settle()
                for a, b, kind in ((0, LAT, 0), (LAT, T, 1)):
                    ins = V.tensor_scalar(xn2[:, m, a:b], xn2[:, m, a:b], mods[:, 24 + m, kind:kind + 1], None, add)
                ins.then_inc(S["n2_ok"], 1)
            dve.wait_ge(S["n2_ok"], KT)
            n_ff = MIX_FILLS + WO_FILLS
            with dve.Fori(0, FFQ) as i:
                for s in range(KT):
                    for cg in range(G):
                        n = n_ff + 3 * s + cg
                        dve.wait_ge(S["o_full"], 6 * KT * i + (n + 1))
                        V.tensor_scalar(hid[:, s, cols(cg)], banks[n % WAVE][:, :GN], 0.0, None, ALU.max).then_inc(S["o_free"], 1)
                for s in range(KT):
                    for cg in range(G):
                        n = n_ff + 3 * (KT + s) + cg
                        dve.wait_ge(S["o_full"], 6 * KT * i + (n + 1))
                        for a, b, kind in kinds(cg):
                            ins = stt(x2[:, s, a:b], banks[n % WAVE][:, a - cg * GN:b - cg * GN], mods[:, 40 + s, kind:kind + 1], x2[:, s, a:b], mul, add)
                        ins.then_inc(S["o_free"], 1)
            dve.wait_ge(S["gf_in"], 16)
            for t in range(NC):
                dve.wait_ge(S["fin_sq"], 2 * t + 2)
                V.tensor_tensor(fss[:, t, 0:1], fss[:, t, 0:1], fss[:, t, 1:2], add).then_inc(S["fin_sum"], 1)
                dve.wait_ge(S["fin_std"], t + 1)
                ch.step(V.reciprocal(frs[:, t:t + 1], frs[:, t:t + 1]))
                ch.settle()
                for i in range(2):
                    stt(yo[:, t * D + i * 512:t * D + (i + 1) * 512], banks[2 * (t % 3) + i][:, :], frs[:, t:t + 1],
                        gf[:, i * 512:(i + 1) * 512], mul, mul).then_inc(S["fin_free"], 1)


def constants():
    import numpy as np
    k = np.zeros((P, K_ALL), np.float32)
    i = np.arange(P)
    k[:, K_ID:K_ID + P] = np.eye(P)
    k[:, K_BO:K_BO + P] = (i[:, None] // HD) == (i[None, :] // HD)
    k[:, K_ONE:K_ONE + P] = 1.0
    for d in range(2):
        for lev in range(LEVELS):
            n = 2 << lev
            same = (i[:, None] // (2 * n)) == (i[None, :] // (2 * n))
            off = same & (i[:, None] // n % 2 == 1) & (i[None, :] // n % 2 == 0)
            c0 = K_LM + (d * LEVELS + lev) * P
            k[:, c0:c0 + P] = off if d == 0 else off.T
        m1 = ((i[:, None] // 2) == (i[None, :] // 2)) & (i[:, None] % 2 == 1) & (i[None, :] % 2 == 0)
        k[:, K_M1 + d * P:K_M1 + (d + 1) * P] = m1.T if d == 0 else m1
        s, t = i[:, None], i[None, :]
        c0 = K_GM + d * 2 * P
        k[:, c0:c0 + P] = (s < t) if d == 0 else (s > t)
        k[:, c0 + P:c0 + 2 * P] = (s <= t) if d == 0 else (s >= t)
    k[:, K_CM:] = np.arange(T)[None, :] % C != 0
    return k


def kernel(x_prompt, x_sample, state_rwkv_fwd, state_rwkv_bwd, c, c_ctx, norm1_g, norm2_g, w_ada, b_ada, w_in,
           w0, w2, a0, a2, g2, k_k, k_a, r_k, lnx_w, lnx_b, conv_w, w_pa, w_pb, w_o, w_ff1, w_ff2, final_norm_g):
    import numpy as np
    import concourse.bacc as bacc
    from concourse.bass_utils import run_bass_kernel_spmd

    def col(w, n):
        return w[:, n * P:(n + 1) * P].reshape(KT, P, P).transpose(1, 0, 2).reshape(P, KT * P)

    wi, wada = np.asarray(w_in)[0], np.asarray(w_ada)[0]
    r1, r2, ro = np.asarray(w_pa)[0], np.asarray(w_pb)[0], np.asarray(w_o)[0]
    f1, f2 = np.asarray(w_ff1)[0], np.asarray(w_ff2)[0]
    blocks = [col(wada, n) for n in range(N_ADA_FIRST)] + [col(wi, 24 + n) for n in range(3)]
    for p in range(PAIRS):
        blocks += [col(wi, n + p) for n in (0, 8, 16, 35, 43, 27, 51, 59)]
        blocks += [col(wada, N_ADA_FIRST + 4 * p + n) for n in range(4)]
    for m in range(KT):
        blocks += [col(r1, m), col(r2, m)]
    blocks += [col(ro, m) for m in range(KT)]
    for q in range(FFQ):
        blocks += [col(f1, q * KT + m) for m in range(KT)]
        blocks += [col(f2[q * D:(q + 1) * D], m) for m in range(KT)]
    wblocks = np.stack(blocks).reshape(N_BLOCKS, P, KT, P)

    w2_, a2_, g2_ = np.asarray(w2)[0], np.asarray(a2)[0], np.asarray(g2)[0]
    pack = np.zeros((PAIRS, P, PK), np.float32)
    rows = [np.asarray(w0)[0, 0], np.asarray(w0)[0, 1], np.asarray(a0)[0, 0], np.asarray(a0)[0, 1], np.asarray(k_k)[0],
            np.asarray(k_a)[0], np.asarray(r_k)[0].reshape(D), np.asarray(lnx_w)[0], np.asarray(lnx_b)[0],
            np.asarray(conv_w)[0, 0], np.asarray(conv_w)[0, 1], np.asarray(conv_w)[0, 2]]
    for p in range(PAIRS):
        cs = slice(p * P, (p + 1) * P)
        for d, st in enumerate((state_rwkv_fwd, state_rwkv_bwd)):
            pack[p, d * HD:(d + 1) * HD, PK_W2 + d * P:PK_W2 + (d + 1) * P] = w2_[d][:, cs]
            pack[p, d * HD:(d + 1) * HD, PK_A2 + d * P:PK_A2 + (d + 1) * P] = a2_[d][:, cs]
            heads_ = np.asarray(st)[0, 0, 2 * p:2 * p + 2].transpose(0, 2, 1).reshape(P, HD)
            pack[p, :, PK_ST + d * HD:PK_ST + (d + 1) * HD] = heads_
        pack[p, :, PK_G2:PK_G2 + P] = g2_[:, cs]
        for i, r in enumerate(rows):
            pack[p, :, PK_VEC + i] = r[cs]
    vecs = np.concatenate([np.asarray(b_ada)[0].reshape(48, P).T, np.asarray(norm1_g)[0].reshape(KT, P).T,
                           np.asarray(norm2_g)[0].reshape(KT, P).T], axis=1)
    cin = np.stack([np.asarray(c)[0].reshape(KT, P).T, np.asarray(c_ctx).reshape(KT, P).T], axis=2)
    gfin = np.broadcast_to(np.asarray(final_norm_g)[None, :], (P, D))

    nc = bacc.Bacc("TRN2", target_bir_lowering=False, num_devices=1)
    arrays = {"xs": np.asarray(x_sample)[0], "xp": np.asarray(x_prompt)[0], "wblocks": wblocks, "pack": pack,
              "vecs": vecs, "cin": cin, "consts": constants(), "gfin": gfin}
    arrays = {f"in_{n}": np.ascontiguousarray(a) for n, a in arrays.items()}
    ins = [nc.dram_tensor(n, a.shape, mybir.dt.from_np(a.dtype), kind="ExternalInput").ap() for n, a in arrays.items()]
    outs = [nc.dram_tensor(n, s, F32, kind="ExternalOutput").ap()
            for n, s in (("y_out", (LAT, D)), ("yp_out", (CTX, D)), ("st_out", (2, PAIRS, P, HD)))]
    flow_step(nc, *ins, *outs)
    res = run_bass_kernel_spmd(nc, [arrays], core_ids=[0]).results[0]
    st = res["st_out"].reshape(2, 1, 1, 2 * PAIRS, HD, HD).transpose(0, 1, 2, 3, 5, 4)
    return (res["yp_out"].reshape(1, CTX, D), res["y_out"].reshape(1, LAT, D), np.ascontiguousarray(st[0]), np.ascontiguousarray(st[1]))
```

```python
from contextlib import ExitStack

import concourse.bass as bass
from concourse import mybir

F32 = mybir.dt.float32
BF16 = mybir.dt.bfloat16
ALU = mybir.AluOpType
ACT = mybir.ActivationFunctionType

P = 128
D = 1024
KT = D // P
LAT, CTX = 1024, 128
T = LAT + CTX
G = 3
GN = T // G
C = 128
NC_LAT = LAT // C
NC = T // C
PAIRS = 8
HD = 64
ROW = 64
FFQ = 4
WAVE = 6
CH_PAIR = 71
POOL_PAIR = 36
RING = 4
LEVELS = 6
EPS = 1e-6
LNX_EPS = 64e-5
DECAY = 0.6065306597126334

N_ADA_FIRST = 16
N_PRO = N_ADA_FIRST + 3
PAIR_BLOCKS = 12
N_PAIR0 = N_PRO
N_MIX0 = N_PAIR0 + PAIRS * PAIR_BLOCKS
N_WO0 = N_MIX0 + 2 * KT
N_FF0 = N_WO0 + KT
N_BLOCKS = N_FF0 + FFQ * 2 * KT

PK_W2, PK_A2, PK_ST, PK_VEC = 0, 256, 512, 640
V_W0, V_A0, V_KK, V_KA, V_RK, V_CONV, N_VEC = 0, 2, 4, 5, 6, 7, 10
PK = PK_VEC + N_VEC
PL_G2, PL_W, PL_B, PL = 0, 128, 129, 130

K_ID, K_BO, K_ONE, K_OFF, K_TRI, K_M1, K_GM, K_ALL = [P * n for n in (0, 1, 2, 3, 9, 15, 16, 20)]

TURN = [("r", "A"), ("k", "A"), ("v", "A"), ("w0", "A"), ("a0", "A"), ("w1", "A"), ("a1", "A"), ("ks", "D"),
        ("bon", "A"), ("vt", "D"), ("za", "A"), ("mu", "D"), ("zb", "A"), ("var", "A"), ("g2", "D"),
        ("cc", "A"), ("ch", "D"), ("cb", "D")]
BEHIND = ("bon", "vt", "mu", "var", "g2")
FIRST = [g for g in TURN if g[0] not in BEHIND]
LAST = [g for g in TURN if g[0] in BEHIND]
STREAM = ["r", "k", "v", "za", "zb", "cc", "ch", "cb"]


class Turn:

    def __init__(self, groups, turns, i=0):
        self.groups = [n for n, _ in groups]
        self.eng = dict(groups)
        per = {e: G * sum(1 for _, x in TURN if x == e) for e in "AD"}
        first = {e: G * sum(1 for _, x in FIRST if x == e) for e in "AD"}
        self.full0 = (G * len(FIRST) if turns else 0) + G * len(TURN) * i
        self.ev0 = {e: (first[e] if turns else 0) + per[e] * i for e in "AD"}

    def full(self, name, cg):
        return self.full0 + (G * self.groups.index(name) + cg + 1)

    def emptied(self, name, cg=G - 1):
        e = self.eng[name]
        before = self.groups[:self.groups.index(name)]
        return e, self.ev0[e] + (G * sum(1 for n in before if self.eng[n] == e) + cg + 1)

    def freed(self, name, cg):
        i = self.groups.index(name)
        if i:
            return self.emptied(self.groups[i - 1], cg)
        if isinstance(self.full0, int) and self.full0 == 0:
            return None
        return "D", self.ev0["D"] + (cg + 1 - G)


def chunk(d, j):
    return j if d == 0 or j == NC_LAT else NC_LAT - 1 - j


class Chain:

    def __init__(self, eng, sem):
        self.eng, self.sem, self.n, self.base, self.per = eng, sem, 0, 0, 0

    def step(self, ins):
        ins.then_inc(self.sem, 1)
        self.n += 1

    def settle(self):
        self.eng.wait_ge(self.sem, self.base + self.n)

    def enter(self, it, per):
        self.start, self.per = self.n, per
        self.base = it * per

    def leave(self, times):
        assert self.n - self.start == self.per, (self.n - self.start, self.per)
        self.n = self.start + times * self.per
        self.base = 0


def flow_step(nc, xs, xp, wblocks, pack, packl, vecs, csil_in, consts, gfin, y_out, yp_out, st_out):
    ctx = ExitStack()
    with ctx:
        def sem(name):
            return ctx.enter_context(nc.semaphore(name))

        def scratch(name, n=KT):
            return nc.dram_tensor(name, [n, P, T], F32, kind="Internal").ap()

        xt_d, xa_d, xb_d, ga_d, gb_d = (scratch(n) for n in ("xt_d", "xa_d", "xb_d", "ga_d", "gb_d"))

        banks = [ctx.enter_context(nc.psum_tensor(f"bank{i}", [P, 512], F32)) for i in range(8)]

        def sb(st, name, shape, dt=F32):
            return st.enter_context(nc.sbuf_tensor(name, shape, dt))

        ring = [sb(ctx, f"ring{s}", [P, KT, P]) for s in range(RING)]
        ident = sb(ctx, "ident", [P, P])
        bones = sb(ctx, "bones", [P, P])
        ones = sb(ctx, "ones", [P, P])
        mods = sb(ctx, "mods", [P, 48, 2])
        csil = sb(ctx, "csil", [P, KT, 2])
        eps_t = sb(ctx, "eps_t", [P, 2])
        vec = sb(ctx, "vec", [P, 48 + 16])
        mul1 = sb(ctx, "mul1", [P, KT, 2])
        mul2 = sb(ctx, "mul2", [P, KT, 2])
        hgt1 = sb(ctx, "hgt1", [P, KT, 2])

        mark_all = ExitStack()
        pair_st = mark_all
        xn = sb(pair_st, "xn", [P, KT, T])
        wl = sb(pair_st, "wl", [P, T])
        al = sb(pair_st, "al", [P, T])
        gl = sb(pair_st, "gl", [P, T])
        offm = sb(pair_st, "offm", [P, LEVELS, P], BF16)
        trim = sb(pair_st, "trim", [P, LEVELS, P], BF16)
        m1c = sb(pair_st, "m1c", [P, P], BF16)
        gmask = sb(pair_st, "gmask", [P, 2, 2 * P], BF16)

        pro = ExitStack()
        x0 = sb(pro, "x0", [P, NC, D])
        xnrm = sb(pro, "xnrm", [P, NC, D])
        xt_s = sb(pro, "xt_s", [P, 2, T])
        cst = sb(pro, "cst", [P, K_ALL - K_OFF])
        cth = sb(pro, "cth", [P, KT, 2])
        ss1 = sb(pro, "ss1", [P, NC])
        rs1 = sb(pro, "rs1", [P, NC])
        pro.close()

        pw = ExitStack()
        pk = sb(pw, "pk", [P, PK])
        pl = sb(pw, "pl", [P, PL])
        half = sb(pw, "half", [P, 6])
        rt, kt, kk, kds, yf = (sb(pw, n, [P, T]) for n in ("rt", "kt", "kk", "kds", "yf"))
        yb = kk
        vp = sb(pw, "vp", [P, NC, 2, P])
        vn = sb(pw, "vn", [P, NC, P])
        ar = [sb(pw, f"ar{d}", [P, NC, 2, C]) for d in range(2)]
        bk = [sb(pw, f"bk{d}", [P, NC, 2, C]) for d in range(2)]
        mid, emid, gstep = ([sb(pw, f"{n}{d}", [P, NC]) for d in range(2)] for n in ("mid", "emid", "gstep"))
        sfin = sb(pw, "sfin", [P, 2, HD])
        cct, cv = (sb(pw, n, [P, T]) for n in ("cct", "cv"))
        urp = [sb(pw, f"urp{d}", [P, 2, P]) for d in range(2)]
        up = urp
        state = [[sb(pw, f"state{d}{q}", [P, P]) for q in range(2)] for d in range(2)]
        bkp = [[sb(pw, f"bkp{d}{h}", [P, 2 * C]) for h in range(2)] for d in range(2)]
        padded = [vp] + urp + [st for x in state for st in x] + [b for x in bkp for b in x]
        tmpst = ExitStack()
        thw = [sb(tmpst, f"thw{d}", [P, T]) for d in range(2)]
        tha = [sb(tmpst, f"tha{d}", [P, T]) for d in range(2)]
        cum, en, tmp, gat = (sb(tmpst, n, [P, T]) for n in ("cum", "en", "tmp", "gat"))
        tmpst.close()
        gmat = [[[sb(pw, f"gmat{q}{d}{h}", [P, 4, P]) for h in range(2)] for d in range(2)] for q in range(2)]
        ltc = [[sb(pw, f"ltc{q}{h}", [P, P]) for h in range(2)] for q in range(2)]
        xt = [[sb(pw, f"xt{q}{h}", [P, P]) for h in range(2)] for q in range(2)]
        tc, xtb, p1 = ([sb(pw, f"{n}{h}", [P, P]) for h in range(2)] for n in ("tc", "xtb", "p1"))
        tt = [[sb(pw, f"tt{q}{d}", [P, 2, P]) for d in range(2)] for q in range(2)]
        tok = [sb(pw, f"tok{q}", [P, 2, 2, P]) for q in range(2)]
        pw.close()
        pair_st.close()

        fin = ExitStack()
        xa = sb(fin, "xa", [P, KT, T])
        xb = sb(fin, "xb", [P, KT, T])
        mix = sb(fin, "mix", [P, KT, T])
        x2 = sb(fin, "x2", [P, KT, T])
        gts = sb(fin, "gts", [P, 2, 2, T])
        xts = sb(fin, "xts", [P, 2, T])
        xn2, hid = xb, mix
        sq2 = gts[:, :, 0, :]
        rs2 = gts[:, 0, 1, :]
        mtmp = sb(fin, "mtmp", [P, GN])
        yo = xa[:, :, :].rearrange("p k t -> p (k t)")
        gf = sb(fin, "gf", [P, D])
        squares = hid[:, :, :].rearrange("p k t -> p (k t)")
        fss = sb(fin, "fss", [P, NC, 2])
        frs = sb(fin, "frs", [P, NC])
        fin.close()

        names = """x_in cst_in mask_in pro_full pro_act pro_dve xt_out0 xt_out1 cst_ok ss_ok rs_a1 xnrm_ok csil_a csil_ok ada1_full
            zero_ok lora_ok pk_in pl_in pj_full half_ok ada_full ada_ok kksq_ok nrms_ok lw_ok exp_ok prod_ok yc_ok vp_ok
            ysq_ok s0_ok gram_full gram_ok tok_full tok_ok pad_ok xt0_ok xtb_ok tr_full tc_ok p1_full p1_ok dt_full xt_ok tri_ok
            ur_full ur_ok u_full u_ok sy_full s_ok y_ok sf_ok xb_out xa_out ga_out sf_out act_chain dve_chain
            pool_chain ab_in gt_in xt_in o_full o_free mix_ok sq_ok sum_full rs_a2 n2_ok h_ok
            fin_full fin_sq fin_sum fin_std fin_free fin_out gf_in""".split()
        S = {n: ctx.enter_context(nc.semaphore(n)) for n in names}
        w_full = [ctx.enter_context(nc.semaphore(f"w_full{s}")) for s in range(RING)]
        ev = {e: ctx.enter_context(nc.semaphore(f"emptied_by_{e}")) for e in "AD"}
        NS = 2 * (NC - 1)
        NL = 2 * LEVELS
        MIX_FILLS, WO_FILLS = 6 * KT, 3 * KT

        def s_n(j, d):
            return 2 * (j if j < NC_LAT else j - 1) + d + 1

        def kinds(cg):
            a, b = cg * GN, (cg + 1) * GN
            return [(a, min(b, LAT), 0)] + ([(LAT, b, 1)] if b > LAT else [])

        def cols(cg):
            return slice(cg * GN, (cg + 1) * GN)

        def diag(x):
            return x.rearrange("p h v -> p (h v)").rearrange("p (x v) -> p x v", v=HD)[:, 0::3, :]

        def heads(x):
            return x.rearrange("p (h v) -> p h v", h=2)

        block = ctx.enter_context(nc.Block())

        @block.sync
        def _(sp):
            def load(b, slot):
                sp.dma_start(ring[slot][:], wblocks[b]).then_inc(w_full[slot], 16)

            for dst, k in ((ident, K_ID), (bones, K_BO), (ones, K_ONE)):
                sp.dma_start(dst[:], consts[:, k:k + P]).then_inc(S["cst_in"], 16)
            sp.dma_start(csil[:], csil_in).then_inc(S["cst_in"], 16)
            sp.dma_start(vec[:], vecs).then_inc(S["cst_in"], 16)
            for i in range(NC_LAT):
                sp.dma_start(x0[:, i, :], xs[i * P:(i + 1) * P, :]).then_inc(S["x_in"], 16)
            sp.dma_start(x0[:, NC_LAT, :], xp).then_inc(S["x_in"], 16)
            for b in range(RING):
                load(b, b)
            sp.dma_start(cst[:], consts[:, K_OFF:]).then_inc(S["mask_in"], 16)
            for b in range(RING, N_PRO + RING):
                if b - RING < N_ADA_FIRST:
                    sp.wait_ge(S["ada1_full"], b - RING + 1)
                else:
                    sp.wait_ge(S["pro_full"], 2 * G * KT + G * (b - RING - N_ADA_FIRST + 1))
                load(b, b % RING)
            def turn(tu, p, behind):
                if behind is not None:
                    sp.wait_ge(S["s0_ok"], 2 * p)
                sp.dma_start(pk[:], pack[p]).then_inc(S["pk_in"], 16)
                if behind is not None:
                    sp.wait_ge(ev["D"], tu.ev0["D"])
                    sp.dma_start(pl[:], packl[behind]).then_inc(S["pl_in"], 16)
                for k in range(RING, PAIR_BLOCKS + RING):
                    name = STREAM[k - RING] if k - RING < len(STREAM) else None
                    if name:
                        sp.wait_ge(S["pj_full"], tu.full(name, G - 1))
                    else:
                        sp.wait_ge(S["ada_full"], 4 * p + (k - RING - len(STREAM) + 1))
                    load(PAIR_BLOCKS * p + (N_PAIR0 + k), (N_PAIR0 + k) % RING)
                    if name in ("za", "zb", "cb"):
                        e, n = tu.emptied(name)
                        dst, src, out = {"za": (ga_d, gat, "ga_out"), "zb": (gb_d, gat, "ga_out"), "cb": (xb_d, cv, "xb_out")}[name]
                        sp.wait_ge(ev[e], n)
                        sp.dma_start(dst[p], src[:]).then_inc(S[out], 16)
                    if name == "v" and behind is not None:
                        spill_states(behind)
                    if name == "zb" and behind is not None:
                        spill_branch(tu, behind)

            def spill_states(p):
                sp.wait_ge(S["sf_ok"], 4 * p + 4)
                for d in range(2):
                    sp.dma_start(st_out[d, p], sfin[:, d, :]).then_inc(S["sf_out"], 16)

            def spill_branch(tu, p):
                sp.wait_ge(ev["D"], tu.emptied("g2")[1])
                sp.dma_start(xa_d[p], yf[:]).then_inc(S["xa_out"], 16)

            turn(Turn(FIRST, False), 0, None)
            with sp.Fori(0, PAIRS - 1) as i:
                turn(Turn(TURN, True, i), i + 1, i)
            last = Turn(LAST, True, PAIRS - 1)
            sp.wait_ge(ev["D"], last.ev0["D"])
            sp.dma_start(pl[:], packl[PAIRS - 1]).then_inc(S["pl_in"], 16)
            spill_states(PAIRS - 1)
            spill_branch(last, PAIRS - 1)
            with sp.Fori(0, (N_BLOCKS - N_MIX0 - RING) // RING) as i:
                for s in range(RING):
                    sp.wait_ge(S["o_full"], G * RING * i + G * (s + 1))
                    load(RING * i + (N_MIX0 + RING + s), (N_MIX0 + s) % RING)

        @block.gpsimd
        def _(pool):
            ch = Chain(pool, S["pool_chain"])
            for c in range(KT):
                pool.wait_ge(S["pro_act"], G * (c + 1))
                pool.dma_start(xt_d[c], xt_s[:, c % 2, :]).then_inc(S[f"xt_out{c % 2}"], 16)
            pool.wait_ge(S["pro_full"], 2 * G * KT)

            def first_inverse(p, j, h):
                q = j % 2
                pool.wait_ge(S["gram_ok"], 4 * NC * p + (4 * j + 2 * h + 2))
                ch.step(nc.gpsimd.tensor_tensor(ltc[q][h][:], gmat[q][0][h][:, 0, :], gmat[q][1][h][:, 0, :], ALU.add))
                ch.settle()
                ch.step(nc.gpsimd.tensor_tensor(xt[q][h][:], ltc[q][h][:], m1c[:], ALU.mult))
                ch.settle()
                nc.gpsimd.tensor_tensor(xt[q][h][:], xt[q][h][:], ident[:], ALU.add).then_inc(S["xt0_ok"], 1)

            def pair_scan(p):
                for h in range(2):
                    first_inverse(p, 0, h)
                for j in range(NC):
                    q = j % 2
                    for lev in range(LEVELS):
                        for h in range(2):
                            n = NL * NC * p + (NL * j + 2 * lev + h)
                            if lev:
                                pool.wait_ge(S["xt_ok"], n - 1)
                            else:
                                pool.wait_ge(S["xt0_ok"], 2 * NC * p + (2 * j + h + 1))
                            nc.gpsimd.tensor_tensor(xtb[h][:], xt[q][h][:], trim[:, lev, :], ALU.mult).then_inc(S["xtb_ok"], 1)
                        if lev == LEVELS - 1 and j + 1 < NC:
                            for h in range(2):
                                first_inverse(p, j + 1, h)
                    for h in range(2):
                        pool.wait_ge(S["xt_ok"], NL * NC * p + (NL * j + NL - 1 + h))
                        for d in range(2):
                            nc.gpsimd.tensor_tensor(tt[q][d][:, h, :], xt[q][h][:], gmask[:, d, P:2 * P], ALU.mult).then_inc(S["tri_ok"], 1)

            with pool.Fori(0, PAIRS - 1) as i:
                ch.enter(i, POOL_PAIR)
                pair_scan(i)
            ch.leave(PAIRS - 1)
            pair_scan(PAIRS - 1)
            for name, n in (("xa_out", PAIRS), ("xb_out", PAIRS), ("ga_out", 2 * PAIRS), ("sf_out", 2 * PAIRS), ("xt_out0", KT // 2), ("xt_out1", KT // 2)):
                pool.wait_ge(S[name], 16 * n)
            for k in range(KT):
                pool.dma_start(xa[:, k, :], xa_d[k]).then_inc(S["ab_in"], 16)
                pool.dma_start(xb[:, k, :], xb_d[k]).then_inc(S["ab_in"], 16)
            pool.dma_start(gf[:], gfin).then_inc(S["gf_in"], 16)
            for m in range(KT):
                if m >= 2:
                    pool.wait_ge(S["mix_ok"], m - 1)
                pool.dma_start(gts[:, m % 2, 0, :], ga_d[m]).then_inc(S["gt_in"], 16)
                pool.dma_start(gts[:, m % 2, 1, :], gb_d[m]).then_inc(S["gt_in"], 16)
                pool.wait_ge(S["gt_in"], 32 * (m + 1))
            for m in range(KT):
                if m >= 2:
                    pool.wait_ge(S["o_free"], WAVE + MIX_FILLS + G * (m - 1))
                pool.dma_start(xts[:, m % 2, :], xt_d[m]).then_inc(S["xt_in"], 16)
                pool.wait_ge(S["xt_in"], 16 * (m + 1))
            for i in range(NC):
                pool.wait_ge(S["fin_free"], 2 * i + 2)
                dst = y_out[i * P:(i + 1) * P, :] if i < NC_LAT else yp_out
                pool.dma_start(dst, yo[:, i * D:(i + 1) * D]).then_inc(S["fin_out"], 16)
            pool.wait_ge(S["fin_out"], 16 * NC)

        @block.tensor
        def _(pe):
            def mm(out, lhsT, rhs, start, stop):
                return nc.tensor.matmul(out, lhsT, rhs, start=start, stop=stop)

            def weights(b, it=0, per=0):
                pe.wait_ge(w_full[b % RING], it * (16 * per // RING) + 16 * (b // RING + 1))
                return ring[b % RING]

            pe.wait_ge(S["cst_in"], 5 * 16)
            pe.wait_ge(S["x_in"], 16 * NC)
            for c in range(KT):
                for cg in range(G):
                    n = G * c + cg
                    if n >= WAVE:
                        pe.wait_ge(S["pro_act"], n - WAVE + 1)
                    for i in range(G):
                        ins = nc.tensor.transpose(banks[n % WAVE][:, i * P:(i + 1) * P], x0[:, cg * G + i, c * P:(c + 1) * P], ident[:])
                    ins.then_inc(S["pro_full"], 1)
            pe.wait_ge(S["csil_ok"], 1)
            for b in range(N_ADA_FIRST):
                w = weights(b)
                for k in range(KT):
                    ins = mm(banks[6][:, 2 * b:2 * b + 2], w[:, k, :], csil[:, k, :], k == 0, k == KT - 1)
                ins.then_inc(S["ada1_full"], 1)
            pe.wait_ge(S["xnrm_ok"], 1)
            for c in range(KT):
                for cg in range(G):
                    n = G * (KT + c) + cg
                    if n - WAVE < G * KT:
                        pe.wait_ge(S["pro_act"], n - WAVE + 1)
                    else:
                        pe.wait_ge(S["pro_dve"], n - WAVE - G * KT + 1)
                    for i in range(G):
                        ins = nc.tensor.transpose(banks[n % WAVE][:, i * P:(i + 1) * P], xnrm[:, cg * G + i, c * P:(c + 1) * P], ident[:])
                    ins.then_inc(S["pro_full"], 1)
            pe.wait_ge(S["pro_dve"], G * KT)
            for b in range(3):
                w = weights(N_ADA_FIRST + b)
                for cg in range(G):
                    n = G * (2 * KT + b) + cg
                    if n - WAVE >= 2 * G * KT:
                        pe.wait_ge(S["pro_act"], n - WAVE - G * KT + 1)
                    for k in range(KT):
                        ins = mm(banks[n % WAVE][:, :GN], w[:, k, :], xn[:, k, cols(cg)], k == 0, k == KT - 1)
                    ins.then_inc(S["pro_full"], 1)
            pe.wait_ge(S["pro_act"], G * (KT + 3))
            pe.wait_ge(S["lora_ok"], 1)


            def fills(tu, name, nb, it):
                w = None
                for cg in range(G):
                    n = 0
                    for i in range(G if name == "v" else 1):
                        for k in range(KT):
                            if n == 0:
                                if cg == 0:
                                    w = weights(N_PAIR0 + nb, it, PAIR_BLOCKS)
                                free = tu.freed(name, cg)
                                if free:
                                    pe.wait_ge(ev[free[0]], free[1])
                            n += 1
                            if name == "v":
                                t = cg * G + i
                                ins = mm(banks[cg][:, i * P:(i + 1) * P], xn[:, k, t * P:(t + 1) * P], w[:, k, :], k == 0, k == KT - 1)
                            else:
                                ins = mm(banks[cg][:, :GN], w[:, k, :], xn[:, k, cols(cg)], k == 0, k == KT - 1)
                            if k == KT - 1 and i == (G if name == "v" else 1) - 1:
                                ins.then_inc(S["pj_full"], 1)
                            yield

            def project(tu, name, it):
                for _ in fills(tu, name, STREAM.index(name), it):
                    pass

            def single(tu, name, lhsT, rhs):
                for cg in range(G):
                    e, n = tu.freed(name, cg)
                    pe.wait_ge(ev[e], n)
                    mm(banks[cg][:, :GN], lhsT, rhs[:, cols(cg)], True, True).then_inc(S["pj_full"], 1)

            def prepare(tu, it, behind):
                if it is not None:
                    pe.wait_ge(S["pk_in"], 16 * it + 16)
                    for d in range(2):
                        single(tu, f"w{d}", pk[:, PK_W2 + d * P:PK_W2 + (d + 1) * P], wl)
                        single(tu, f"a{d}", pk[:, PK_A2 + d * P:PK_A2 + (d + 1) * P], al)
                    pe.wait_ge(S["kksq_ok"], it + 1)
                    single(tu, "ks", bones[:], tmp)
                if behind is not None:
                    pe.wait_ge(S["prod_ok"], behind + 1)
                    single(tu, "bon", bones[:], kds)
                    for cg in range(G):
                        e, n = tu.freed("vt", cg)
                        pe.wait_ge(ev[e], n)
                        for i in range(G):
                            for h in range(2):
                                ins = mm(banks[cg][:, i * P:(i + 1) * P], vp[:, cg * G + i, h, :], ident[:], h == 0, h == 1)
                        ins.then_inc(S["pj_full"], 1)
                if it is not None:
                    project(tu, "za", it)
                if behind is not None:
                    pe.wait_ge(S["yc_ok"], behind + 1)
                    single(tu, "mu", bones[:], yf)
                if it is not None:
                    project(tu, "zb", it)
                if behind is not None:
                    pe.wait_ge(S["ysq_ok"], behind + 1)
                    single(tu, "var", bones[:], cct)
                    pe.wait_ge(S["pl_in"], 16 * behind + 16)
                    single(tu, "g2", pl[:, PL_G2:PL_G2 + P], gl)
                if it is not None:
                    for name in ("cc", "ch", "cb"):
                        project(tu, name, it)
                    for b in range(4):
                        w = weights(N_PAIR0 + 8 + b, it, PAIR_BLOCKS)
                        for k in range(KT):
                            ins = mm(banks[7][:, 2 * b:2 * b + 2], w[:, k, :], csil[:, k, :], k == 0, k == KT - 1)
                        ins.then_inc(S["ada_full"], 1)

            def scan(p, filler):
                def fill(n):
                    for _ in range(n):
                        if next(filler, "end") == "end":
                            return

                def serial_ur(j, d):
                    q, c = j % 2, chunk(d, j)
                    o = banks[6 + d][:, 0:P]
                    if 0 < j < NC_LAT:
                        pe.wait_ge(S["s_ok"], NS * p + s_n(j - 1, d))
                    if j:
                        pe.wait_ge(S["y_ok"], 2 * NC * p + (2 * (j - 1) + d + 1))
                    if j < NC_LAT:
                        mm(o, ar[d][:, c, 0, :], state[d][q][:], True, False)
                    mm(o, gmat[q][d][0][:, 2, :], vp[:, c, 0, :], j == NC_LAT, False)
                    mm(o, gmat[q][d][1][:, 2, :], vp[:, c, 1, :], False, True).then_inc(S["ur_full"], 1)

                def serial_u(j, d):
                    q = j % 2
                    pe.wait_ge(S["tri_ok"], 4 * NC * p + (4 * j + 4))
                    pe.wait_ge(S["ur_ok"], 2 * NC * p + (2 * j + d + 1))
                    o = banks[6 + d][:, P:2 * P]
                    mm(o, tt[q][d][:, 0, :], urp[d][:, 0, :], True, False)
                    mm(o, tt[q][d][:, 1, :], urp[d][:, 1, :], False, True).then_inc(S["u_full"], 1)

                def serial_sy(j, d):
                    q, c = j % 2, chunk(d, j)
                    pe.wait_ge(S["u_ok"], 2 * NC * p + (2 * j + d + 1))
                    if j != NC_LAT - 1:
                        o = heads(banks[6 + d][:, 2 * P:3 * P])
                        mm(o, tok[q][:, d, 0, :], diag(up[d][:]), True, False)
                        mm(o, tok[q][:, d, 1, :], diag(vp[:, c]), False, True)
                    o = banks[6 + d][:, 3 * P:4 * P]
                    if j < NC_LAT:
                        mm(o, state[d][q][:], ar[d][:, c, 1, :], True, False)
                    for h in range(2):
                        mm(o, up[d][:, h, :], gmat[q][d][h][:, 1, :], j == NC_LAT and h == 0, False)
                    for h in range(2):
                        ins = mm(o, vp[:, c, h, :], gmat[q][d][h][:, 3, :], False, h == 1)
                    ins.then_inc(S["sy_full"], 1)

                def gram(j, h, d):
                    c = chunk(d, j)
                    n = 4 * NC * p + (4 * j + 2 * h + d)
                    if h or d:
                        pe.wait_ge(S["gram_ok"], n)
                    elif j:
                        pe.wait_ge(S["tok_ok"], NC * p + j)
                    pe.wait_ge(S["pad_ok"], n + 1)
                    rhs = ar[d][:, c, :, :].rearrange("p a t -> p (a t)")
                    mm(banks[3][:, 0:2 * P], bkp[d][h][:, 0:C], rhs, True, True)
                    mm(banks[3][:, 2 * P:4 * P], bkp[d][h][:, C:2 * C], rhs, True, True).then_inc(S["gram_full"], 1)

                def token_major(j):
                    pe.wait_ge(S["gram_ok"], 4 * NC * p + (4 * j + 4))
                    for d in range(2):
                        for x in range(2):
                            ins = nc.tensor.transpose(banks[3][:, (2 * d + x) * P:(2 * d + x + 1) * P], bk[d][:, chunk(d, j), x, :], ident[:])
                    ins.then_inc(S["tok_full"], 1)

                def invert(j, lev, h, part):
                    q, o = j % 2, banks[4 + h][:, 0:P]
                    n = NL * NC * p + (NL * j + 2 * lev + h + 1)
                    if part == "turn":
                        if lev == 0:
                            pe.wait_ge(S["xt0_ok"], 2 * NC * p + (2 * j + h + 1))
                        if lev or j:
                            pe.wait_ge(S["xt_ok"], n - 2)
                        nc.tensor.transpose(o, xt[q][h][:], ident[:]).then_inc(S["tr_full"], 1)
                    elif part == "left":
                        pe.wait_ge(S["tc_ok"], n)
                        mm(o, ltc[q][h][:], tc[h][:], True, True).then_inc(S["p1_full"], 1)
                    else:
                        pe.wait_ge(S["p1_ok"], n)
                        pe.wait_ge(S["xtb_ok"], n)
                        mm(o, p1[h][:], xtb[h][:], True, True).then_inc(S["dt_full"], 1)

                for h in range(2):
                    for d in range(2):
                        gram(0, h, d)
                token_major(0)
                for j in range(NC):
                    for lev in range(LEVELS):
                        for h in range(2):
                            invert(j, lev, h, "turn")
                        fill(3 if lev == LEVELS - 1 else 2)
                        if lev == 3 and j + 1 < NC:
                            gram(j + 1, 0, 0)
                        if lev == 4 and j + 1 < NC:
                            gram(j + 1, 1, 0)
                        for h in range(2):
                            invert(j, lev, h, "left")
                        if j and lev < 3:
                            for d in range(2):
                                (serial_ur, serial_u, serial_sy)[lev](j - 1, d)
                        if lev == 3 and j + 1 < NC:
                            gram(j + 1, 0, 1)
                        if lev == 4 and j + 1 < NC:
                            gram(j + 1, 1, 1)
                        if lev == 5 and j + 1 < NC:
                            token_major(j + 1)
                        for h in range(2):
                            invert(j, lev, h, "right")
                for stage in (serial_ur, serial_u, serial_sy):
                    for d in range(2):
                        if stage is serial_ur:
                            pe.wait_ge(S["tok_ok"], NC * p + NC)
                        stage(NC - 1, d)
                fill(PAIRS * 100)

            def none():
                return iter(())

            def first_projections(tu, it):
                for name in ("r", "k", "v"):
                    yield from fills(tu, name, STREAM.index(name), it)

            def begin(p):
                pe.wait_ge(S["s0_ok"], 2 * p + 2)
                pe.wait_ge(S["vp_ok"], p + 1)

            first = Turn(FIRST, False)
            for _ in first_projections(first, 0):
                pass
            prepare(first, 0, None)
            with pe.Fori(0, PAIRS - 1) as i:
                tu = Turn(TURN, True, i)
                begin(i)
                scan(i, first_projections(tu, i + 1))
                prepare(tu, i + 1, i)
            last = Turn(LAST, True, PAIRS - 1)
            begin(PAIRS - 1)
            scan(PAIRS - 1, none())
            prepare(last, None, PAIRS - 1)

            pe.wait_ge(S["ab_in"], 16 * 2 * KT)

            def wave(n0, it, per_it, b, per_b, src):
                w = weights(b, it, per_b)
                for cg in range(G):
                    n = n0 + cg
                    pe.wait_ge(S["o_free"], it * per_it + n + 1)
                    for k in range(KT):
                        ins = mm(banks[n % WAVE][:, :GN], w[:, k, :], src[:, k, cols(cg)], k == 0, k == KT - 1)
                    ins.then_inc(S["o_full"], 1)

            with pe.Fori(0, KT // 2) as i:
                for s in range(2):
                    wave(6 * s, i, 12, N_MIX0 + 2 * s, 4, xa)
                    wave(6 * s + 3, i, 12, N_MIX0 + 2 * s + 1, 4, xb)
            pe.wait_ge(S["mix_ok"], KT)
            with pe.Fori(0, KT // 4) as i:
                for s in range(4):
                    wave(MIX_FILLS + 3 * s, i, 12, N_WO0 + s, 4, mix)
            n_ff = MIX_FILLS + WO_FILLS
            pe.wait_ge(S["o_free"], WAVE + n_ff)
            for m in range(KT):
                pe.wait_ge(S["sq_ok"], m + 1)
                for cg in range(G):
                    ins = mm(banks[cg][:, :GN], ones[:], sq2[:, m % 2, cols(cg)], m == 0, m == KT - 1)
                ins.then_inc(S["sum_full"], 1)
            pe.wait_ge(S["n2_ok"], KT)
            with pe.Fori(0, FFQ) as i:
                for s in range(KT):
                    wave(n_ff + 3 * s, i, 6 * KT, N_FF0 + s, 2 * KT, xn2)
                pe.wait_ge(S["h_ok"], G * KT * i + G * KT)
                for s in range(KT):
                    wave(n_ff + 3 * (KT + s), i, 6 * KT, N_FF0 + KT + s, 2 * KT, hid)
            pe.wait_ge(S["o_free"], WAVE + n_ff + FFQ * 6 * KT)
            for t in range(NC):
                if t >= 3:
                    pe.wait_ge(S["fin_free"], 2 * (t - 3) + 2)
                for c in range(KT):
                    ins = nc.tensor.transpose(banks[2 * (t % 3) + c // 4][:, (c % 4) * P:(c % 4 + 1) * P], x2[:, c, t * P:(t + 1) * P], ident[:])
                ins.then_inc(S["fin_full"], 1)

        @block.scalar
        def _(act):
            A = nc.scalar.activation
            ch = Chain(act, S["act_chain"])
            act.wait_ge(S["cst_in"], 5 * 16)
            A(cth[:], csil[:], ACT.Tanh, scale=0.5).then_inc(S["csil_a"], 1)
            act.wait_ge(S["x_in"], 16 * NC)
            for i in range(NC):
                A(xnrm[:, i, :], x0[:, i, :], ACT.Square, accum_out=ss1[:, i:i + 1]).then_inc(S["ss_ok"], 1)
            act.wait_ge(S["ss_ok"], NC)
            act.wait_ge(S["cst_ok"], 1)
            A(rs1[:], ss1[:], ACT.Sqrt, scale=1.0 / D, bias=eps_t[:, 0:1]).then_inc(S["rs_a1"], 1)
            for c in range(KT):
                if c >= 2:
                    act.wait_ge(S[f"xt_out{c % 2}"], 16 * (c // 2))
                for cg in range(G):
                    n = G * c + cg
                    act.wait_ge(S["pro_full"], n + 1)
                    A(xt_s[:, c % 2, cols(cg)], banks[n % WAVE][:, :GN], ACT.Copy).then_inc(S["pro_act"], 1)
            for b, (dst, f, sc) in enumerate(((wl, ACT.Tanh, 1.0), (al, ACT.Copy, 1.0), (gl, ACT.Tanh, 0.5))):
                for cg in range(G):
                    n = G * (2 * KT + b) + cg
                    act.wait_ge(S["pro_full"], n + 1)
                    A(dst[:, cols(cg)], banks[n % WAVE][:, :GN], f, scale=sc).then_inc(S["pro_act"], 1)


            def empty(tu, name, out, func, **kw):
                for cg in range(G):
                    act.wait_ge(S["pj_full"], tu.full(name, cg))
                    A(out(cg), banks[cg][:, :GN], func, **kw).then_inc(ev["A"], 1)

            def prepare(tu, it, behind):
                if it is not None:
                    act.wait_ge(S["half_ok"], it + 1)
                    for d in range(2):
                        empty(tu, f"w{d}", lambda cg: thw[d][:, cols(cg)], ACT.Tanh, scale=0.5, bias=half[:, d:d + 1])
                        empty(tu, f"a{d}", lambda cg: tha[d][:, cols(cg)], ACT.Tanh, scale=0.5, bias=half[:, 2 + d:3 + d])
                    act.wait_ge(ev["D"], tu.emptied("ks")[1])
                    A(en[:], en[:], ACT.Sqrt).then_inc(S["nrms_ok"], 1)
                if behind is not None:
                    empty(tu, "bon", lambda cg: cct[:, cols(cg)], ACT.Copy)
                if it is not None:
                    decays(it, 0)
                    if behind is not None:
                        act.wait_ge(S["pj_full"], tu.full("vt", G - 1))
                    for h in range(2):
                        hs = slice(h * HD, (h + 1) * HD)
                        ins = A(vp[:, :, h, hs], vn[:, :, hs], ACT.Copy)
                    ins.then_inc(S["vp_ok"], 1)
                    empty(tu, "za", lambda cg: gat[:, cols(cg)], ACT.Tanh, scale=0.5)
                    act.wait_ge(S["ga_out"], 32 * it + 16)
                    decays(it, 1)
                    empty(tu, "zb", lambda cg: gat[:, cols(cg)], ACT.Tanh, scale=0.5)
                if behind is not None:
                    empty(tu, "var", lambda cg: cct[:, cols(cg)], ACT.Sqrt, scale=1.0 / HD, bias=eps_t[:, 1:2])
                if it is not None:
                    if behind is not None:
                        act.wait_ge(ev["D"], tu.emptied("g2")[1])
                    empty(tu, "cc", lambda cg: cct[:, cols(cg)], ACT.Copy)
                if behind is not None:
                    act.wait_ge(S["xa_out"], 16 * behind + 16)

            def decays(it, d):
                act.wait_ge(S["lw_ok"], 2 * it + d + 1)
                A(en[:], cum[:], ACT.Exp, scale=-1.0).then_inc(S["exp_ok"], 1)
                act.wait_ge(S["exp_ok"], 8 * it + (4 * d + 1))
                A(cum[:], cum[:], ACT.Exp).then_inc(S["exp_ok"], 1)
                A(thw[d][:], thw[d][:], ACT.Exp).then_inc(S["exp_ok"], 1)
                A(emid[d][:], mid[d][:], ACT.Exp).then_inc(S["exp_ok"], 1)

            def scan(p, tu):
                def at(j, d):
                    return 2 * NC * p + (2 * j + d + 1)

                def pads(j):
                    for h in range(2):
                        hs = slice(h * HD, (h + 1) * HD)
                        for d in range(2):
                            if j:
                                act.wait_ge(S["gram_full"], 4 * NC * p + (4 * (j - 1) + 2 * h + d + 1))
                            A(bkp[d][h][hs, :], bk[d][hs, chunk(d, j), :, :].rearrange("p x t -> p (x t)"), ACT.Copy).then_inc(S["pad_ok"], 1)

                def to_diag(dst, j, d, full, col, ok):
                    act.wait_ge(S[full], at(j, d))
                    A(diag(dst[d][:]), heads(banks[6 + d][:, col:col + P]), ACT.Copy).then_inc(S[ok], 1)

                def outputs(j, d):
                    act.wait_ge(S["sy_full"], at(j, d))
                    if j != NC_LAT - 1:
                        act.wait_ge(S["s_ok"], NS * p + s_n(j, d))
                    c = chunk(d, j)
                    A((yf, yb)[d][:, c * C:(c + 1) * C], banks[6 + d][:, 3 * P:4 * P], ACT.Copy).then_inc(S["y_ok"], 1)

                def serial(j, stage):
                    for d in range(2):
                        if stage == 0:
                            to_diag(urp, j, d, "ur_full", 0, "ur_ok")
                        elif stage == 1:
                            to_diag(up, j, d, "u_full", P, "u_ok")
                        else:
                            outputs(j, d)

                def tokens(j):
                    act.wait_ge(S["tok_full"], NC * p + j + 1)
                    A(tok[j % 2][:].rearrange("p d x c -> p (d x c)"), banks[3][:, :], ACT.Copy).then_inc(S["tok_ok"], 1)

                def projected(j):
                    if tu is None:
                        return
                    name, cg = "rkv"[j // G], j % G
                    dst = vn[:, cg * G:(cg + 1) * G, :].rearrange("p t v -> p (t v)") if name == "v" else (rt if name == "r" else kt)[:, cols(cg)]
                    act.wait_ge(S["pj_full"], tu.full(name, cg))
                    A(dst, banks[cg][:, :GN], ACT.Copy).then_inc(ev["A"], 1)

                pads(0)
                tokens(0)
                for j in range(NC):
                    if j + 1 < NC:
                        pads(j + 1)
                    for lev in range(3):
                        if j:
                            serial(j - 1, lev)
                    if j + 1 < NC:
                        projected(j)
                        tokens(j + 1)
                for lev in range(3):
                    serial(NC - 1, lev)
                projected(NC - 1)

            first = Turn(FIRST, False)
            empty(first, "r", lambda cg: rt[:, cols(cg)], ACT.Copy)
            empty(first, "k", lambda cg: kt[:, cols(cg)], ACT.Copy)
            act.wait_ge(S["zero_ok"], 1)
            empty(first, "v", lambda cg: vn[:, cg * G:(cg + 1) * G, :].rearrange("p t v -> p (t v)"), ACT.Copy)
            prepare(first, 0, None)
            with act.Fori(0, PAIRS - 1) as i:
                tu = Turn(TURN, True, i)
                act.wait_ge(S["s0_ok"], 2 * i + 2)
                scan(i, tu)
                prepare(tu, i + 1, i)
            act.wait_ge(S["s0_ok"], 2 * PAIRS)
            scan(PAIRS - 1, None)
            prepare(Turn(LAST, True, PAIRS - 1), None, PAIRS - 1)

            n_sq = WAVE + MIX_FILLS
            for m in range(KT):
                act.wait_ge(S["o_free"], n_sq + G * (m + 1))
                if m >= 2:
                    act.wait_ge(S["sum_full"], m - 1)
                A(sq2[:, m % 2, :], x2[:, m, :], ACT.Square).then_inc(S["sq_ok"], 1)
            act.wait_ge(S["sum_full"], KT)
            for cg in range(G):
                A(rs2[:, cols(cg)], banks[cg][:, :GN], ACT.Sqrt, scale=1.0 / D, bias=eps_t[:, 0:1]).then_inc(S["rs_a2"], 1)
            with act.Fori(0, FFQ) as i:
                for s in range(KT):
                    for cg in range(G):
                        act.wait_ge(S["o_free"], 6 * KT * i + (n_sq + WO_FILLS + G * s + cg + 1))
                        A(hid[:, s, cols(cg)], hid[:, s, cols(cg)], ACT.Square).then_inc(S["h_ok"], 1)
            for t in range(NC):
                act.wait_ge(S["fin_full"], t + 1)
                for i in range(2):
                    A(squares[:, (2 * t + i) * 512:(2 * t + i + 1) * 512], banks[2 * (t % 3) + i][:, :], ACT.Square, accum_out=fss[:, t, i:i + 1]).then_inc(S["fin_sq"], 1)
                act.wait_ge(S["fin_sum"], t + 1)
                A(frs[:, t:t + 1], fss[:, t, 0:1], ACT.Sqrt, scale=1.0 / D, bias=eps_t[:, 0:1]).then_inc(S["fin_std"], 1)

        @block.vector
        def _(dve):
            V = nc.vector
            ch = Chain(dve, S["dve_chain"])
            mul, add, sub = ALU.mult, ALU.add, ALU.subtract
            stt = V.scalar_tensor_tensor

            def bc(x, n):
                return x.to_broadcast([P, x.shape[1], n]) if len(x.shape) == 3 else x.unsqueeze(2).to_broadcast([P, x.shape[1], n])

            ch.step(V.memset(eps_t[:, 0:1], EPS))
            V.memset(eps_t[:, 1:2], LNX_EPS).then_inc(S["cst_ok"], 1)
            dve.wait_ge(S["csil_a"], 1)
            ch.step(V.tensor_scalar(cth[:], cth[:], 0.5, 0.5, mul, add))
            ch.settle()
            V.tensor_tensor(csil[:], csil[:], cth[:], mul).then_inc(S["csil_ok"], 1)
            dve.wait_ge(S["rs_a1"], 1)
            ch.step(V.reciprocal(rs1[:], rs1[:]))
            ch.settle()
            for i in range(NC):
                ins = V.tensor_scalar(xnrm[:, i, :], x0[:, i, :], rs1[:, i:i + 1], None, mul)
            ins.then_inc(S["xnrm_ok"], 1)
            dve.wait_ge(S["mask_in"], 16)
            for dst, k, n in ((offm[:].rearrange("p a b -> p (a b)"), K_OFF, 6 * P), (trim[:].rearrange("p a b -> p (a b)"), K_TRI, 6 * P), (m1c[:], K_M1, P),
                              (gmask[:].rearrange("p a b -> p (a b)"), K_GM, 4 * P)):
                ch.step(V.tensor_copy(dst, cst[:, k - K_OFF:k - K_OFF + n]))
            dve.wait_ge(S["ada1_full"], N_ADA_FIRST)
            ch.step(V.tensor_tensor(mods[:, 0:16, :], banks[6][:, 0:32].rearrange("p (b c) -> p b c", c=2), bc(vec[:, 0:16], 2), add))
            ch.settle()
            ch.step(V.tensor_scalar(mul1[:], mods[:, 8:16, :], 1.0, None, add))
            ch.settle()
            ch.step(V.tensor_tensor(mul1[:], mul1[:], bc(vec[:, 48:56], 2), mul))
            ch.settle()
            for c in range(KT):
                for cg in range(G):
                    n = G * (KT + c) + cg
                    dve.wait_ge(S["pro_full"], n + 1)
                    for a, b, kind in kinds(cg):
                        ins = V.tensor_scalar(xn[:, c, a:b], banks[n % WAVE][:, a - cg * GN:b - cg * GN],
                                              mul1[:, c, kind:kind + 1], mods[:, c, kind:kind + 1], mul, add)
                    ins.then_inc(S["pro_dve"], 1)
            dve.wait_ge(S["xt_out0"], 8 * KT)
            dve.wait_ge(S["xt_out1"], 8 * KT)
            for x in padded[1:]:
                ch.step(V.memset(x[:], 0.0))
            V.memset(vp[:], 0.0).then_inc(S["zero_ok"], 1)
            dve.wait_ge(S["pro_act"], G * (KT + 3))
            V.tensor_scalar(gl[:], gl[:], 0.5, 0.5, mul, add).then_inc(S["lora_ok"], 1)
            dve.wait_ge(S["zero_ok"], 1)
            ch.settle()


            def par(i):
                return pk[:, PK_VEC + i:PK_VEC + i + 1]

            def full(tu, name, cg):
                dve.wait_ge(S["pj_full"], tu.full(name, cg))

            def filled(tu, name):
                e, n = tu.emptied(name)
                dve.wait_ge(ev[e], n)

            def a3(x):
                return x.rearrange("p (c t) -> p c t", t=C)

            def direction(tu, it, d):
                filled(tu, f"a{d}")
                ch.step(V.tensor_scalar(thw[d][:], thw[d][:], -0.5 * DECAY, -0.5 * DECAY, mul, add))
                ch.settle()
                for c in range(NC):
                    o, x = (cum[:, c * C:(c + 1) * C], thw[d][:, c * C:(c + 1) * C])
                    if d == 1:
                        o, x = o[:, ::-1], x[:, ::-1]
                    ch.step(V.tensor_tensor_scan(o, ones[:], x, 0.0, mul, add))
                ch.settle()
                end = C - 1 if d == 0 else 0
                ch.step(V.tensor_scalar(mid[d][:], a3(cum[:])[:, :, end:end + 1].rearrange("p c t -> p (c t)"), 0.5, None, mul))
                ch.settle()
                ch.step(V.tensor_tensor(a3(cum[:]), a3(cum[:]), bc(mid[d][:], C), sub))
                ch.settle()
                V.tensor_tensor(thw[d][:], cum[:], thw[d][:], sub).then_inc(S["lw_ok"], 1)
                kd = kds if d == 0 else tmp
                ch.step(V.tensor_scalar(tmp[:], tha[d][:], half[:, 4:5], half[:, 5:6], mul, add))
                ch.step(V.tensor_scalar(tha[d][:], tha[d][:], -0.5, -0.5, mul, add))
                ch.settle()
                ch.step(V.tensor_tensor(kd[:], tmp[:], kt[:], mul))
                ch.step(V.tensor_tensor(tha[d][:], tha[d][:], kk[:], mul))
                ch.settle()
                dve.wait_ge(S["exp_ok"], 8 * it + (4 * d + 1))
                ch.step(V.tensor_tensor(bk[d][:, :, 1, :], a3(kd[:]), a3(en[:]), mul))
                ch.step(V.tensor_tensor(bk[d][:, :, 0, :], a3(tha[d][:]), a3(en[:]), mul))
                dve.wait_ge(S["exp_ok"], 8 * it + (4 * d + 2))
                ch.step(V.tensor_tensor(ar[d][:, :, 1, :], a3(rt[:]), a3(cum[:]), mul))
                dve.wait_ge(S["exp_ok"], 8 * it + (4 * d + 3))
                ch.step(V.tensor_tensor(ar[d][:, :, 0, :], a3(kk[:]), a3(thw[d][:]), mul))
                dve.wait_ge(S["exp_ok"], 8 * it + (4 * d + 4))
                g = gstep[d][:, 0:NC_LAT - 1] if d == 0 else gstep[d][:, 1:NC_LAT]
                ch.step(V.tensor_tensor(g, emid[d][:, 0:NC_LAT - 1], emid[d][:, 1:NC_LAT], mul))
                ch.settle()

            def prepare(tu, it, behind):
                if behind is not None:
                    dve.wait_ge(S["y_ok"], 2 * NC * behind + 2 * NC)
                    V.tensor_tensor(yf[:], yf[:], yb[:], add).then_inc(S["yc_ok"], 1)
                if it is not None:
                    dve.wait_ge(S["pk_in"], 16 * it + 16)
                    ch.step(V.tensor_scalar(half[:, 0:4], pk[:, PK_VEC + V_W0:PK_VEC + V_W0 + 4], 0.5, None, mul))
                    ch.step(V.tensor_scalar(half[:, 4:5], par(V_KA), 0.5, None, mul))
                    V.tensor_scalar(half[:, 5:6], par(V_KA), -0.5, 1.0, mul, add).then_inc(S["half_ok"], 1)
                    if behind is not None:
                        dve.wait_ge(S["yc_ok"], behind + 1)
                    filled(tu, "k")
                    ch.step(V.tensor_scalar(kk[:], kt[:], par(V_KK), None, mul))
                    ch.settle()
                    V.tensor_tensor(tmp[:], kk[:], kk[:], mul).then_inc(S["kksq_ok"], 1)
                    for cg in range(G):
                        full(tu, "ks", cg)
                        V.tensor_scalar(en[:, cols(cg)], banks[cg][:, :GN], 1e-12, None, ALU.max).then_inc(ev["D"], 1)
                if behind is not None:
                    filled(tu, "bon")
                    for cg in range(G):
                        full(tu, "vt", cg)
                        V.tensor_tensor(cv[:, cols(cg)], banks[cg][:, :GN], cct[:, cols(cg)], mul).then_inc(ev["D"], 1)
                if it is not None:
                    dve.wait_ge(S["nrms_ok"], it + 1)
                    ch.step(V.reciprocal(en[:], en[:]))
                    ch.settle()
                    ch.step(V.tensor_tensor(kk[:], kk[:], en[:], mul))
                    ch.settle()
                    direction(tu, it, 0)
                if behind is not None:
                    for cg in range(G):
                        full(tu, "mu", cg)
                        stt(yf[:, cols(cg)], banks[cg][:, :GN], -1.0 / HD, yf[:, cols(cg)], mul, add).then_inc(ev["D"], 1)
                    dve.wait_ge(ev["D"], tu.emptied("mu")[1])
                    V.tensor_tensor(cct[:], yf[:], yf[:], mul).then_inc(S["ysq_ok"], 1)
                if it is not None:
                    direction(tu, it, 1)
                    ch.step(V.tensor_tensor(kds[:], kds[:], tmp[:], add))
                    ch.settle()
                    stt(kds[:], kds[:], par(V_RK), rt[:], mul, mul).then_inc(S["prod_ok"], 1)
                if behind is not None:
                    filled(tu, "var")
                    ch.step(V.reciprocal(cct[:], cct[:]))
                    ch.settle()
                    ch.step(V.tensor_tensor(yf[:], yf[:], cct[:], mul))
                    ch.settle()
                    dve.wait_ge(S["pl_in"], 16 * behind + 16)
                    ch.step(V.tensor_scalar(yf[:], yf[:], pl[:, PL_W:PL_W + 1], pl[:, PL_B:PL_B + 1], mul, add))
                    ch.settle()
                    ch.step(V.tensor_tensor(yf[:], yf[:], cv[:], add))
                    ch.settle()
                    for cg in range(G):
                        full(tu, "g2", cg)
                        V.tensor_tensor(yf[:, cols(cg)], banks[cg][:, :GN], yf[:, cols(cg)], mul).then_inc(ev["D"], 1)
                if it is not None:
                    filled(tu, "cc")
                    for cg in range(G):
                        full(tu, "ch", cg)
                        V.tensor_tensor(cct[:, cols(cg)], banks[cg][:, :GN], cct[:, cols(cg)], mul).then_inc(ev["D"], 1)
                    dve.wait_ge(ev["D"], tu.emptied("ch")[1])
                    ch.step(V.tensor_scalar(cv[:], cct[:], par(V_CONV + 1), None, mul))
                    ch.settle()
                    for a, b, w in ((0, LAT, ROW), (LAT, T, CTX)):
                        u, o = (x[:, a:b].rearrange("p (r w) -> p r w", w=w) for x in (cct, cv))
                        ch.step(stt(o[:, :, 1:w], u[:, :, 0:w - 1], par(V_CONV), o[:, :, 1:w], mul, add))
                        ch.settle()
                        ch.step(stt(o[:, :, 0:w - 1], u[:, :, 1:w], par(V_CONV + 2), o[:, :, 0:w - 1], mul, add))
                        ch.settle()
                    dve.wait_ge(S["ga_out"], 32 * it + 32)
                    for d in range(2):
                        c = chunk(d, 0)
                        for h in range(2):
                            hs = slice(h * HD, (h + 1) * HD)
                            ins = V.tensor_scalar(state[d][0][hs, hs], pk[hs, PK_ST + d * HD:PK_ST + (d + 1) * HD], emid[d][hs, c:c + 1], None, mul)
                        ins.then_inc(S["s0_ok"], 1)
                    for cg in range(G):
                        full(tu, "cb", cg)
                        V.tensor_tensor(cv[:, cols(cg)], banks[cg][:, :GN], cv[:, cols(cg)], mul).then_inc(ev["D"], 1)
                    dve.wait_ge(S["ada_full"], 4 * it + 4)
                    V.tensor_tensor(mods[:, bass.ds(4 * it + 16, 4), :], banks[7][:, 0:8].rearrange("p (b c) -> p b c", c=2),
                                    bc(vec[:, bass.ds(4 * it + 16, 4)], 2), add).then_inc(S["ada_ok"], 1)
                    dve.wait_ge(S["xb_out"], 16 * it + 16)
                if behind is not None:
                    dve.wait_ge(S["sf_out"], 32 * behind + 32)

            def scan(p):
                def states(j, d):
                    q, c = j % 2, chunk(d, j)
                    if j == NC_LAT - 1:
                        return
                    dve.wait_ge(S["sy_full"], 2 * NC * p + (2 * j + d + 1))
                    o = banks[6 + d]
                    if j < NC_LAT:
                        new = state[d][1 - q]
                        ch.step(V.tensor_tensor(new[:], o[:, 2 * P:3 * P], state[d][q][:], add))
                        ch.settle()
                        stt(new[:], new[:], gstep[d][:, c:c + 1], bones[:], mul, mul).then_inc(S["s_ok"], 1)
                    else:
                        for h in range(2):
                            hs = slice(h * HD, (h + 1) * HD)
                            V.tensor_scalar(sfin[hs, d, :], o[hs, 2 * P + h * HD:2 * P + (h + 1) * HD],
                                            emid[d][hs, c:c + 1], None, mul).then_inc(S["sf_ok"], 1)
                        dve.wait_ge(S["sf_ok"], 4 * p + (2 * d + 2))
                        V.tensor_copy(mid[d][:, 0:1], emid[d][:, 0:1]).then_inc(S["s_ok"], 1)

                def gram(j, h, d):
                    dve.wait_ge(S["gram_full"], 4 * NC * p + (4 * j + 2 * h + d + 1))
                    V.tensor_tensor(gmat[j % 2][d][h][:].rearrange("p (x a) t -> p x (a t)", x=2),
                                    banks[3][:, :].rearrange("p (x a) -> p x a", x=2),
                                    gmask[:, d:d + 1, :].to_broadcast([P, 2, 2 * P]), mul).then_inc(S["gram_ok"], 1)

                for h in range(2):
                    for d in range(2):
                        gram(0, h, d)
                for j in range(NC):
                    q = j % 2
                    for lev in range(LEVELS):
                        at = NL * NC * p + (NL * j + 2 * lev + 1)
                        for h in range(2):
                            dve.wait_ge(S["tr_full"], at + h)
                            V.tensor_tensor(tc[h][:], banks[4 + h][:, 0:P], trim[:, lev, :], mul).then_inc(S["tc_ok"], 1)
                        if lev in (3, 4) and j + 1 < NC:
                            gram(j + 1, lev - 3, 0)
                        for h in range(2):
                            dve.wait_ge(S["p1_full"], at + h)
                            V.tensor_tensor(p1[h][:], banks[4 + h][:, 0:P], offm[:, lev, :], mul).then_inc(S["p1_ok"], 1)
                        if j and lev == 2:
                            for d in range(2):
                                states(j - 1, d)
                        if lev in (3, 4) and j + 1 < NC:
                            gram(j + 1, lev - 3, 1)
                        for h in range(2):
                            dve.wait_ge(S["dt_full"], at + h)
                            V.tensor_tensor(xt[q][h][:], banks[4 + h][:, 0:P], xt[q][h][:], add).then_inc(S["xt_ok"], 1)
                for d in range(2):
                    states(NC - 1, d)

            prepare(Turn(FIRST, False), 0, None)
            with dve.Fori(0, PAIRS - 1) as i:
                ch.enter(i, CH_PAIR)
                scan(i)
                prepare(Turn(TURN, True, i), i + 1, i)
            ch.leave(PAIRS - 1)
            scan(PAIRS - 1)
            prepare(Turn(LAST, True, PAIRS - 1), None, PAIRS - 1)

            ch.step(V.tensor_scalar(mul2[:], mods[:, 32:40, :], 1.0, None, add))
            ch.settle()
            ch.step(V.tensor_tensor(mul2[:], mul2[:], bc(vec[:, 56:64], 2), mul))
            V.tensor_scalar(hgt1[:], mods[:, 16:24, :], 0.5, None, mul).then_inc(S["o_free"], WAVE)
            dve.wait_ge(S["o_free"], WAVE)
            ch.settle()
            with dve.Fori(0, KT // 2) as i:
                ch.enter(i, 4)
                for s in range(2):
                    m = 2 * i + s
                    dve.wait_ge(S["gt_in"], 64 * i + 32 * s + 32)
                    for x in range(2):
                        for cg in range(G):
                            n = 6 * s + 3 * x + cg
                            dve.wait_ge(S["o_full"], 12 * i + n + 1)
                            if x == 0:
                                stt(mix[:, m, cols(cg)], gts[:, s, 0, cols(cg)], 1.0, banks[n % WAVE][:, :GN], add, mul).then_inc(S["o_free"], 1)
                            else:
                                stt(mtmp[:], gts[:, s, 1, cols(cg)], 1.0, banks[n % WAVE][:, :GN], add, mul).then_inc(S["o_free"], 1)
                                dve.wait_ge(S["o_free"], 12 * i + (WAVE + n + 1))
                                ins = V.tensor_tensor(mix[:, m, cols(cg)], mix[:, m, cols(cg)], mtmp[:], add)
                                if cg < 2:
                                    ch.step(ins)
                                    ch.settle()
                                else:
                                    ins.then_inc(S["mix_ok"], 1)
                                    dve.wait_ge(S["mix_ok"], 2 * i + s + 1)
            ch.leave(KT // 2)
            with dve.Fori(0, KT // 4) as i:
                for s in range(4):
                    m = 4 * i + s
                    dve.wait_ge(S["xt_in"], 64 * i + 16 * s + 16)
                    for cg in range(G):
                        n = MIX_FILLS + 3 * s + cg
                        dve.wait_ge(S["o_full"], 12 * i + (n + 1))
                        for a, b, kind in kinds(cg):
                            ins = stt(x2[:, m, a:b], banks[n % WAVE][:, a - cg * GN:b - cg * GN], hgt1[:, m, kind:kind + 1], xts[:, s % 2, a:b], mul, add)
                        ins.then_inc(S["o_free"], 1)
            dve.wait_ge(S["rs_a2"], G)
            ch.step(V.reciprocal(rs2, rs2))
            ch.settle()
            for m in range(KT):
                for a, b, kind in ((0, LAT, 0), (LAT, T, 1)):
                    ch.step(stt(xn2[:, m, a:b], x2[:, m, a:b], mul2[:, m, kind:kind + 1], rs2[:, a:b], mul, mul))
                ch.settle()
                for a, b, kind in ((0, LAT, 0), (LAT, T, 1)):
                    ins = V.tensor_scalar(xn2[:, m, a:b], xn2[:, m, a:b], mods[:, 24 + m, kind:kind + 1], None, add)
                ins.then_inc(S["n2_ok"], 1)
            dve.wait_ge(S["n2_ok"], KT)
            n_ff = MIX_FILLS + WO_FILLS
            with dve.Fori(0, FFQ) as i:
                for s in range(KT):
                    for cg in range(G):
                        n = n_ff + 3 * s + cg
                        dve.wait_ge(S["o_full"], 6 * KT * i + (n + 1))
                        V.tensor_scalar(hid[:, s, cols(cg)], banks[n % WAVE][:, :GN], 0.0, None, ALU.max).then_inc(S["o_free"], 1)
                for s in range(KT):
                    for cg in range(G):
                        n = n_ff + 3 * (KT + s) + cg
                        dve.wait_ge(S["o_full"], 6 * KT * i + (n + 1))
                        for a, b, kind in kinds(cg):
                            ins = stt(x2[:, s, a:b], banks[n % WAVE][:, a - cg * GN:b - cg * GN], mods[:, 40 + s, kind:kind + 1], x2[:, s, a:b], mul, add)
                        ins.then_inc(S["o_free"], 1)
            dve.wait_ge(S["gf_in"], 16)
            for t in range(NC):
                dve.wait_ge(S["fin_sq"], 2 * t + 2)
                V.tensor_tensor(fss[:, t, 0:1], fss[:, t, 0:1], fss[:, t, 1:2], add).then_inc(S["fin_sum"], 1)
                dve.wait_ge(S["fin_std"], t + 1)
                ch.step(V.reciprocal(frs[:, t:t + 1], frs[:, t:t + 1]))
                ch.settle()
                for i in range(2):
                    stt(yo[:, t * D + i * 512:t * D + (i + 1) * 512], banks[2 * (t % 3) + i][:, :], frs[:, t:t + 1],
                        gf[:, i * 512:(i + 1) * 512], mul, mul).then_inc(S["fin_free"], 1)


def constants():
    import numpy as np
    k = np.zeros((P, K_ALL), np.float32)
    i = np.arange(P)
    k[:, K_ID:K_ID + P] = np.eye(P)
    k[:, K_BO:K_BO + P] = (i[:, None] // HD) == (i[None, :] // HD)
    k[:, K_ONE:K_ONE + P] = 1.0
    tri = [i[:, None] >= i[None, :], i[:, None] <= i[None, :]]
    for lev in range(LEVELS):
        n = 2 << lev
        blk, blk2 = i // n, i // (2 * n)
        same, same2 = blk[:, None] == blk[None, :], blk2[:, None] == blk2[None, :]
        k[:, K_OFF + lev * P:K_OFF + (lev + 1) * P] = same2 & ~same
        k[:, K_TRI + lev * P:K_TRI + (lev + 1) * P] = same & np.where(blk[:, None] % 2 == 0, tri[0], tri[1])
    k[:, K_M1:K_M1 + P] = (i[:, None] // 2 == i[None, :] // 2) & (i[:, None] != i[None, :])
    for d in range(2):
        s, t = i[:, None], i[None, :]
        c0 = K_GM + d * 2 * P
        k[:, c0:c0 + P] = (s < t) if d == 0 else (s > t)
        k[:, c0 + P:c0 + 2 * P] = (s <= t) if d == 0 else (s >= t)
    return k


def kernel(x_prompt, x_sample, state_rwkv_fwd, state_rwkv_bwd, c, c_ctx, norm1_g, norm2_g, w_ada, b_ada, w_in,
           w0, w2, a0, a2, g2, k_k, k_a, r_k, lnx_w, lnx_b, conv_w, w_pa, w_pb, w_o, w_ff1, w_ff2, final_norm_g):
    import numpy as np
    import concourse.bacc as bacc
    from concourse.bass_utils import run_bass_kernel_spmd

    def col(w, n):
        return w[:, n * P:(n + 1) * P].reshape(KT, P, P).transpose(1, 0, 2).reshape(P, KT * P)

    wi, wada = np.asarray(w_in)[0], np.asarray(w_ada)[0]
    r1, r2, ro = np.asarray(w_pa)[0], np.asarray(w_pb)[0], np.asarray(w_o)[0]
    f1, f2 = np.asarray(w_ff1)[0], np.asarray(w_ff2)[0]
    blocks = [col(wada, n) for n in range(N_ADA_FIRST)] + [col(wi, 24 + n) for n in range(3)]
    for p in range(PAIRS):
        blocks += [col(wi, n + p) for n in (0, 8, 16, 51, 59, 35, 43, 27)]
        blocks += [col(wada, N_ADA_FIRST + 4 * p + n) for n in range(4)]
    for m in range(KT):
        blocks += [col(r1, m), col(r2, m)]
    blocks += [col(ro, m) for m in range(KT)]
    for q in range(FFQ):
        blocks += [col(f1, q * KT + m) for m in range(KT)]
        blocks += [col(f2[q * D:(q + 1) * D], m) for m in range(KT)]
    wblocks = np.stack(blocks).reshape(N_BLOCKS, P, KT, P)

    w2_, a2_, g2_ = np.asarray(w2)[0], np.asarray(a2)[0], np.asarray(g2)[0]
    pack, packl = np.zeros((PAIRS, P, PK), np.float32), np.zeros((PAIRS, P, PL), np.float32)
    rows = [np.asarray(w0)[0, 0], np.asarray(w0)[0, 1], np.asarray(a0)[0, 0], np.asarray(a0)[0, 1], np.asarray(k_k)[0],
            np.asarray(k_a)[0], np.asarray(r_k)[0].reshape(D),
            np.asarray(conv_w)[0, 0], np.asarray(conv_w)[0, 1], np.asarray(conv_w)[0, 2]]
    for p in range(PAIRS):
        cs = slice(p * P, (p + 1) * P)
        for d, st in enumerate((state_rwkv_fwd, state_rwkv_bwd)):
            pack[p, d * HD:(d + 1) * HD, PK_W2 + d * P:PK_W2 + (d + 1) * P] = w2_[d][:, cs]
            pack[p, d * HD:(d + 1) * HD, PK_A2 + d * P:PK_A2 + (d + 1) * P] = a2_[d][:, cs]
            heads_ = np.asarray(st)[0, 0, 2 * p:2 * p + 2].transpose(0, 2, 1).reshape(P, HD)
            pack[p, :, PK_ST + d * HD:PK_ST + (d + 1) * HD] = heads_
        packl[p, :, PL_G2:PL_G2 + P] = g2_[:, cs]
        packl[p, :, PL_W], packl[p, :, PL_B] = np.asarray(lnx_w)[0, cs], np.asarray(lnx_b)[0, cs]
        for i, r in enumerate(rows):
            pack[p, :, PK_VEC + i] = r[cs]
    vecs = np.concatenate([np.asarray(b_ada)[0].reshape(48, P).T, np.asarray(norm1_g)[0].reshape(KT, P).T,
                           np.asarray(norm2_g)[0].reshape(KT, P).T], axis=1)
    cin = np.stack([np.asarray(c)[0].reshape(KT, P).T, np.asarray(c_ctx).reshape(KT, P).T], axis=2)
    gfin = np.broadcast_to(np.asarray(final_norm_g)[None, :], (P, D))

    nc = bacc.Bacc("TRN2", target_bir_lowering=False, num_devices=1)
    arrays = {"xs": np.asarray(x_sample)[0], "xp": np.asarray(x_prompt)[0], "wblocks": wblocks, "pack": pack, "packl": packl,
              "vecs": vecs, "cin": cin, "consts": constants(), "gfin": gfin}
    arrays = {f"in_{n}": np.ascontiguousarray(a) for n, a in arrays.items()}
    ins = [nc.dram_tensor(n, a.shape, mybir.dt.from_np(a.dtype), kind="ExternalInput").ap() for n, a in arrays.items()]
    outs = [nc.dram_tensor(n, s, F32, kind="ExternalOutput").ap()
            for n, s in (("y_out", (LAT, D)), ("yp_out", (CTX, D)), ("st_out", (2, PAIRS, P, HD)))]
    flow_step(nc, *ins, *outs)
    res = run_bass_kernel_spmd(nc, [arrays], core_ids=[0]).results[0]
    st = res["st_out"].reshape(2, 1, 1, 2 * PAIRS, HD, HD).transpose(0, 1, 2, 3, 5, 4)
    return (res["yp_out"].reshape(1, CTX, D), res["y_out"].reshape(1, LAT, D), np.ascontiguousarray(st[0]), np.ascontiguousarray(st[1]))
```

```python
from contextlib import ExitStack

import concourse.bass as bass
from concourse import mybir

F32 = mybir.dt.float32
BF16 = mybir.dt.bfloat16
F32R = mybir.dt.float32r
ALU = mybir.AluOpType
ACT = mybir.ActivationFunctionType

P = 128
D = 1024
KT = D // P
LAT, CTX = 1024, 128
T = LAT + CTX
G = 3
GN = T // G
C = 128
NC_LAT = LAT // C
NC = T // C
PAIRS = 8
HD = 64
ROW = 64
FFE = 8
HB = 4
WAVE = 6
CH_PAIR = 61
POOL_PAIR = 38
RING = 4
LEVELS = 6
EPS = 1e-6
LNX_EPS = 64e-5
DECAY = 0.6065306597126334

MG = 512
N_ADA_FIRST = 16
N_HELD = 8
N_ADA_RING = N_ADA_FIRST - N_HELD
N_PRO = N_ADA_RING + 3
PAIR_BLOCKS = 12
N_PAIR0 = N_PRO
N_MIX0 = N_PAIR0 + PAIRS * PAIR_BLOCKS
N_WO0 = N_MIX0 + 2 * KT
N_FF0 = N_WO0 + KT
N_BLOCKS = N_FF0 + FFE * 2 * HB
N_SPLIT = N_BLOCKS - N_WO0

PK_W2, PK_A2, PK_ST, PK_VEC = 0, 256, 512, 640
V_W0, V_A0, V_KK, V_KA, V_RK, V_CONV, N_VEC = 0, 2, 4, 5, 6, 7, 10
PK = PK_VEC + N_VEC
PL_G2, PL_W, PL_B, PL = 0, 128, 129, 130

K_ID, K_BO, K_ONE, K_OFF, K_TRI, K_M1, K_GM, K_ALL = [P * n for n in (0, 1, 2, 3, 9, 15, 16, 20)]

FILL = [("r", "A"), ("k", "A"), ("v", "A"), ("cc", "A"), ("ch", "D"), ("cb", "D")]
TURN = FILL + [("ks", "A"), ("bon", "A"), ("w0", "A"), ("a0", "A"), ("za", "A"), ("w1", "A"), ("a1", "A"), ("vt", "D"),
               ("mu", "D"), ("var", "A"), ("zb", "A")]
BEHIND = ("bon", "vt", "mu", "var")
FIRST = [g for g in TURN if g[0] not in BEHIND]
LAST = [g for g in TURN if g[0] in BEHIND]
STREAM = ["r", "k", "v", "cc", "ch", "cb", "za", 0, 1, "zb", 2, 3]
PIECE = 8


class Turn:

    def __init__(self, groups, turns, i=0):
        self.groups = [n for n, _ in groups]
        self.eng = dict(groups)
        per = {e: G * sum(1 for _, x in TURN if x == e) for e in "AD"}
        first = {e: G * sum(1 for _, x in FIRST if x == e) for e in "AD"}
        self.full0 = (G * len(FIRST) if turns else 0) + G * len(TURN) * i
        self.ev0 = {e: (first[e] if turns else 0) + per[e] * i for e in "AD"}

    def full(self, name, cg):
        return self.full0 + (G * self.groups.index(name) + cg + 1)

    def emptied(self, name, cg=G - 1):
        e = self.eng[name]
        before = self.groups[:self.groups.index(name)]
        return e, self.ev0[e] + (G * sum(1 for n in before if self.eng[n] == e) + cg + 1)

    def freed(self, name, cg):
        i = self.groups.index(name)
        if i:
            return [self.emptied(self.groups[i - 1], cg)]
        if isinstance(self.full0, int) and self.full0 == 0:
            return []
        return [(e, self.ev0[e] + (cg + 1 - G)) for e in "AD"]


def chunk(d, j):
    return j if d == 0 or j == NC_LAT else NC_LAT - 1 - j


class Chain:

    def __init__(self, eng, sem):
        self.eng, self.sem, self.n, self.base, self.per = eng, sem, 0, 0, 0

    def step(self, ins):
        ins.then_inc(self.sem, 1)
        self.n += 1

    def settle(self):
        self.eng.wait_ge(self.sem, self.base + self.n)

    def enter(self, it, per):
        self.start, self.per = self.n, per
        self.base = it * per

    def leave(self, times):
        assert self.n - self.start == self.per, (self.n - self.start, self.per)
        self.n = self.start + times * self.per
        self.base = 0


def flow_step(nc, xs, xp, wblocks, pack, packl, vecs, csil_in, consts, gfin, y_out, yp_out, st_out):
    ctx = ExitStack()
    with ctx:
        def sem(name):
            return ctx.enter_context(nc.semaphore(name))

        def scratch(name, n=KT):
            return nc.dram_tensor(name, [n, P, T], F32, kind="Internal").ap()

        xt_d, xa_d, xb_d, ga_d, gb_d = (scratch(n) for n in ("xt_d", "xa_d", "xb_d", "ga_d", "gb_d"))

        banks = [ctx.enter_context(nc.psum_tensor(f"bank{i}", [P, 512], F32)) for i in range(8)]

        def sb(st, name, shape, dt=F32):
            return st.enter_context(nc.sbuf_tensor(name, shape, dt))

        ring = [sb(ctx, f"ring{s}", [P, KT, P]) for s in range(RING)]
        ident = sb(ctx, "ident", [P, P])
        bones = sb(ctx, "bones", [P, P])
        ones = sb(ctx, "ones", [P, P])
        mods = sb(ctx, "mods", [P, 48, 2])
        csil = sb(ctx, "csil", [P, KT, 2])
        eps_t = sb(ctx, "eps_t", [P, 2])
        vec = sb(ctx, "vec", [P, 48 + 16])
        mul1 = sb(ctx, "mul1", [P, KT, 2])
        mul2 = sb(ctx, "mul2", [P, KT, 2])
        hgt1 = sb(ctx, "hgt1", [P, KT, 2])

        mark_all = ExitStack()
        pair_st = mark_all
        xn = sb(pair_st, "xn", [P, KT, T])
        wl = sb(pair_st, "wl", [P, T])
        al = sb(pair_st, "al", [P, T])
        gl = sb(pair_st, "gl", [P, T])
        offm = sb(pair_st, "offm", [P, LEVELS, P], BF16)
        trim = sb(pair_st, "trim", [P, LEVELS, P], BF16)
        m1c = sb(pair_st, "m1c", [P, P], BF16)
        gmask = sb(pair_st, "gmask", [P, 2, 2 * P], BF16)

        pro = ExitStack()
        x0 = sb(pro, "x0", [P, NC, D])
        xnrm = sb(pro, "xnrm", [P, NC, D])
        xt_s = sb(pro, "xt_s", [P, 2, T])
        cst = sb(pro, "cst", [P, K_ALL - K_OFF])
        held = sb(pro, "held", [P, N_HELD, KT * P])
        cth = sb(pro, "cth", [P, KT, 2])
        mrow1 = sb(pro, "mrow1", [P, 4, MG])
        ss1 = sb(pro, "ss1", [P, NC])
        rs1 = sb(pro, "rs1", [P, NC])
        pro.close()

        pw = ExitStack()
        pk = sb(pw, "pk", [P, PK])
        pl = sb(pw, "pl", [P, PL])
        half = sb(pw, "half", [P, 6])
        rt, kt, kk, kds, yf = (sb(pw, n, [P, T]) for n in ("rt", "kt", "kk", "kds", "yf"))
        yb = kk
        vp = sb(pw, "vp", [P, NC, 2, P])
        vn = sb(pw, "vn", [P, NC, P])
        ar = [sb(pw, f"ar{d}", [P, NC, 2, C]) for d in range(2)]
        bk = [sb(pw, f"bk{d}", [P, NC, 2, C]) for d in range(2)]
        mid, emid, gstep = ([sb(pw, f"{n}{d}", [P, NC]) for d in range(2)] for n in ("mid", "emid", "gstep"))
        sfin = sb(pw, "sfin", [P, 2, HD])
        cct, cv = (sb(pw, n, [P, T]) for n in ("cct", "cv"))
        urp = [sb(pw, f"urp{d}", [P, 2, P]) for d in range(2)]
        up = urp
        state = [[sb(pw, f"state{d}{q}", [P, P]) for q in range(2)] for d in range(2)]
        bkp = [[sb(pw, f"bkp{d}{h}", [P, 2 * C]) for h in range(2)] for d in range(2)]
        mrow = cv[0:2, 0:MG]
        padded = [vp] + urp + [st for x in state for st in x] + [b for x in bkp for b in x]
        tmpst = ExitStack()
        thw = [sb(tmpst, f"thw{d}", [P, T]) for d in range(2)]
        tha = [sb(tmpst, f"tha{d}", [P, T]) for d in range(2)]
        cum, en, tmp, gat = (sb(tmpst, n, [P, T]) for n in ("cum", "en", "tmp", "gat"))
        tmpst.close()
        gmat = [[[sb(pw, f"gmat{q}{d}{h}", [P, 4, P]) for h in range(2)] for d in range(2)] for q in range(2)]
        ltc = [[sb(pw, f"ltc{q}{h}", [P, P]) for h in range(2)] for q in range(2)]
        xt = [[sb(pw, f"xt{q}{h}", [P, P]) for h in range(2)] for q in range(2)]
        tc, xtb, p1 = ([sb(pw, f"{n}{h}", [P, P]) for h in range(2)] for n in ("tc", "xtb", "p1"))
        tt = [[sb(pw, f"tt{q}{d}", [P, 2, P]) for d in range(2)] for q in range(2)]
        tok = [sb(pw, f"tok{q}", [P, 2, 2, P]) for q in range(2)]
        pw.close()
        pair_st.close()

        later = ExitStack()
        x2 = sb(later, "x2", [P, KT, T])
        xn2_hi = sb(later, "xn2_hi", [P, KT, T], F32R)
        xn2_raw = sb(later, "xn2_raw", [P, KT, T])
        mix_raw = sb(later, "mix_raw", [P, KT, T])
        later.close()
        fin = ExitStack()
        xa = sb(fin, "xa", [P, KT, T])
        xb = sb(fin, "xb", [P, KT, T])
        mix_hi = sb(fin, "mix_hi", [P, KT, T], F32R)
        mix_lo = sb(fin, "mix_lo", [P, KT, T], F32R)
        wsp = [[sb(fin, f"wsp{x}{q}", [P, KT, P], F32R) for x in range(2)] for q in range(2)]
        gts = sb(fin, "gts", [P, 2, 2, T])
        xts = sb(fin, "xts", [P, 2, T])
        mtmp = sb(fin, "mtmp", [P, GN])
        xn2_lo = mix_hi
        hid_hi, hid_lo = mix_lo[:, 0:HB, :], mix_lo[:, HB:, :]
        sq2 = gts[:, :, 0, :]
        rs2 = gts[:, 0, 1, :]
        hsq = gts[:, 0, 0, 0:2 * GN].rearrange("p (q t) -> p q t", q=2)
        acc = gts[:, 1, 1, :]
        gf = gts[:, 1, 1, 0:D]
        yo = xb[:, :, :].rearrange("p k t -> p (k t)")
        squares = mix_raw[:, :, :].rearrange("p k t -> p (k t)")
        fss = sb(fin, "fss", [P, NC, 2])
        frs = sb(fin, "frs", [P, NC])
        fin.close()

        names = """mul1_ok x_in held_in cst_in mask_in pro_full pro_act pro_dve xt_out0 xt_out1 cst_ok ss_ok rs_a1 xnrm_ok csil_a csil_ok ada1_full
            zero_ok lora_ok pk_in pl_in pj_full half_ok ada_full mrow1_ok mt1_full mrow_ok mt_full ada_ok kksq_ok logw_ok kf_ok kd_ok lw_ok exp_ok prod_ok gate_full gate_ok yc_ok vp_ok
            ysq_ok s0_ok gram_full gram_ok tok_full tok_ok pad_ok xt0_ok xtb_ok tr_full tc_ok p1_full p1_ok dt_full xt_ok tri_ok
            ur_full ur_ok u_full u_ok sy_full s_ok y_ok sf_ok xb_out xa_out ga_out sf_out act_chain dve_chain
            pool_chain a_in b_in gt_in xt_in0 xt_in1 wh_ok wl_ok o_full o_free raw_ok hi_ok mix_ok sq_ok acc_ok sum_full rs_a2 xs_ok raw2_ok n2hi_ok n2_ok hsq_ok hhi_ok h_ok
            fin_full fin_sq fin_sum fin_std fin_free fin_out gf_in""".split()
        S = {n: ctx.enter_context(nc.semaphore(n)) for n in names}
        w_full = [ctx.enter_context(nc.semaphore(f"w_full{s}")) for s in range(RING)]
        ev = {e: ctx.enter_context(nc.semaphore(f"emptied_by_{e}")) for e in "AD"}
        NS = 2 * (NC - 1)
        NL = 2 * LEVELS
        PRO_COPIES = G * (KT + KT // 2)
        MIX_FILLS, WO_FILLS, FF_FILLS = 6 * KT, 3 * KT, 3 * (HB + KT)

        def s_n(j, d):
            return 2 * (j if j < NC_LAT else j - 1) + d + 1

        def kinds(cg):
            a, b = cg * GN, (cg + 1) * GN
            return [(a, min(b, LAT), 0)] + ([(LAT, b, 1)] if b > LAT else [])

        def cols(cg):
            return slice(cg * GN, (cg + 1) * GN)

        def diag(x):
            return x.rearrange("p h v -> p (h v)").rearrange("p (x v) -> p x v", v=HD)[:, 0::3, :]

        def heads(x):
            return x.rearrange("p (h v) -> p h v", h=2)

        block = ctx.enter_context(nc.Block())

        @block.sync
        def _(sp):
            def load(b, slot):
                sp.dma_start(ring[slot][:], wblocks[N_HELD + b]).then_inc(w_full[slot], 16)

            for dst, k in ((ident, K_ID), (bones, K_BO), (ones, K_ONE)):
                sp.dma_start(dst[:], consts[:, k:k + P]).then_inc(S["cst_in"], 16)
            sp.dma_start(csil[:], csil_in).then_inc(S["cst_in"], 16)
            sp.dma_start(vec[:], vecs).then_inc(S["cst_in"], 16)
            for b in range(RING):
                load(b, b)
            for i in range(0, NC_LAT, 2):
                sp.dma_start(x0[:, i, :], xs[i * P:(i + 1) * P, :]).then_inc(S["x_in"], 16)
            sp.dma_start(cst[:], consts[:, K_OFF:]).then_inc(S["mask_in"], 16)
            for b in range(RING, N_PRO + RING):
                if b - RING < N_ADA_RING:
                    sp.wait_ge(S["ada1_full"], b - RING + 1)
                else:
                    sp.wait_ge(S["pro_full"], 2 * G * KT + G * (b - RING - N_ADA_RING + 1))
                load(b, b % RING)
            def turn(tu, p, behind):
                if behind is not None:
                    sp.wait_ge(S["s0_ok"], 2 * p)
                sp.dma_start(pk[:], pack[p]).then_inc(S["pk_in"], 16)
                for k, name in enumerate(STREAM):
                    if isinstance(name, str):
                        sp.wait_ge(S["pj_full"], tu.full(name, G - 1))
                    else:
                        sp.wait_ge(S["ada_full"], 4 * p + name + 1)
                    load(PAIR_BLOCKS * p + (N_PAIR0 + RING + k), (N_PAIR0 + k) % RING)
                    if name in ("za", "zb", "cb"):
                        e, n = tu.emptied(name)
                        dst, src, out = {"za": (ga_d, gat, "ga_out"), "zb": (gb_d, gat, "ga_out"), "cb": (xb_d, cv, "xb_out")}[name]
                        sp.wait_ge(ev[e], n)
                        sp.dma_start(dst[p], src[:]).then_inc(S[out], 16)
                    if name == "cb" and behind is not None:
                        spill_states(behind)
                if behind is not None:
                    spill_branch(behind)
                    sp.dma_start(pl[:], packl[behind + 1]).then_inc(S["pl_in"], 16)

            def spill_states(p):
                sp.wait_ge(S["sf_ok"], 4 * p + 4)
                for d in range(2):
                    sp.dma_start(st_out[d, p], sfin[:, d, :]).then_inc(S["sf_out"], 16)

            def spill_branch(p):
                sp.wait_ge(S["gate_ok"], G * p + G)
                sp.dma_start(xa_d[p], yf[:]).then_inc(S["xa_out"], 16)

            turn(Turn(FIRST, False), 0, None)
            sp.dma_start(pl[:], packl[0]).then_inc(S["pl_in"], 16)
            with sp.Fori(0, PAIRS - 1) as i:
                turn(Turn(TURN, True, i), i + 1, i)
            spill_states(PAIRS - 1)
            with sp.Fori(0, 2 * KT // RING) as i:
                for s in range(RING):
                    sp.wait_ge(S["o_full"], G * RING * i + G * (s + 1))
                    load(RING * i + (N_MIX0 + RING + s), (N_MIX0 + s) % RING)
            with sp.Fori(0, (N_SPLIT - RING) // RING) as i:
                for s in range(RING):
                    sp.wait_ge(S["wl_ok"], RING * i + s + 1)
                    load(RING * i + (N_WO0 + RING + s), (N_WO0 + s) % RING)

        @block.gpsimd
        def _(pool):
            ch = Chain(pool, S["pool_chain"])
            for c in range(KT):
                pool.wait_ge(S["pro_act"], G * (c + 1))
                pool.dma_start(xt_d[c], xt_s[:, c % 2, :]).then_inc(S[f"xt_out{c % 2}"], 16)
            pool.wait_ge(S["pro_full"], 2 * G * KT)

            def first_inverse(p, j, h):
                q = j % 2
                pool.wait_ge(S["gram_ok"], 4 * NC * p + (4 * j + 2 * h + 2))
                ch.step(nc.gpsimd.tensor_tensor(ltc[q][h][:], gmat[q][0][h][:, 0, :], gmat[q][1][h][:, 0, :], ALU.add))
                ch.settle()
                ch.step(nc.gpsimd.tensor_tensor(xt[q][h][:], ltc[q][h][:], m1c[:], ALU.mult))
                ch.settle()
                nc.gpsimd.tensor_tensor(xt[q][h][:], xt[q][h][:], ident[:], ALU.add).then_inc(S["xt0_ok"], 1)

            def pair_scan(p):
                for h in range(2):
                    first_inverse(p, 0, h)
                for j in range(NC):
                    q = j % 2
                    for lev in range(LEVELS):
                        for h in range(2):
                            n = NL * NC * p + (NL * j + 2 * lev + h)
                            if lev:
                                pool.wait_ge(S["xt_ok"], n - 1)
                            else:
                                pool.wait_ge(S["xt0_ok"], 2 * NC * p + (2 * j + h + 1))
                            nc.gpsimd.tensor_tensor(xtb[h][:], xt[q][h][:], trim[:, lev, :], ALU.mult).then_inc(S["xtb_ok"], 1)
                        if lev == LEVELS - 1 and j + 1 < NC:
                            for h in range(2):
                                first_inverse(p, j + 1, h)
                    for h in range(2):
                        pool.wait_ge(S["xt_ok"], NL * NC * p + (NL * j + NL - 1 + h))
                        for d in range(2):
                            nc.gpsimd.tensor_tensor(tt[q][d][:, h, :], xt[q][h][:], gmask[:, d, P:2 * P], ALU.mult).then_inc(S["tri_ok"], 1)

            def keys(it):
                pool.wait_ge(S["kd_ok"], 2 * it + 2)
                ch.step(nc.gpsimd.tensor_tensor(kds[:], kds[:], tmp[:], ALU.add))
                ch.settle()
                ch.step(nc.gpsimd.tensor_tensor(kds[:], kds[:], rt[:], ALU.mult))
                ch.settle()
                nc.gpsimd.tensor_tensor(kds[:], kds[:], pk[:, PK_VEC + V_RK:PK_VEC + V_RK + 1].to_broadcast([P, T]), ALU.mult).then_inc(S["prod_ok"], 1)

            def both_ways(p):
                pool.wait_ge(S["y_ok"], 2 * NC * p + 2 * NC)
                nc.gpsimd.tensor_tensor(yf[:], yf[:], yb[:], ALU.add).then_inc(S["yc_ok"], 1)

            keys(0)
            with pool.Fori(0, PAIRS - 1) as i:
                ch.enter(i, POOL_PAIR)
                pair_scan(i)
                both_ways(i)
                keys(i + 1)
            ch.leave(PAIRS - 1)
            pool.wait_ge(S["pj_full"], Turn(LAST, True, PAIRS - 1).full0)
            pool.wait_ge(S["xa_out"], 16 * (PAIRS - 1))
            for k in range(KT - 1):
                pool.dma_start(xa[:, k, :], xa_d[k]).then_inc(S["a_in"], 16)
            pair_scan(PAIRS - 1)
            both_ways(PAIRS - 1)
            pool.wait_ge(S["gate_ok"], G * PAIRS)
            for name, n in (("xa_out", PAIRS - 1), ("xb_out", PAIRS), ("ga_out", 2 * PAIRS), ("sf_out", 2 * PAIRS), ("xt_out0", KT // 2), ("xt_out1", KT // 2)):
                pool.wait_ge(S[name], 16 * n)
            for m in range(KT):
                if m >= 2:
                    pool.wait_ge(S["raw_ok"], G * (m - 1))
                pool.dma_start(gts[:, m % 2, 0, :], ga_d[m]).then_inc(S["gt_in"], 16)
                pool.dma_start(gts[:, m % 2, 1, :], gb_d[m]).then_inc(S["gt_in"], 16)
                if m == 1:
                    for k in range(KT):
                        pool.dma_start(xb[:, k, :], xb_d[k]).then_inc(S["b_in"], 16)
                    for x in range(2):
                        pool.dma_start(xts[:, x, :], xt_d[x]).then_inc(S[f"xt_in{x}"], 16)
                pool.wait_ge(S["gt_in"], 32 * (m + 1))

            def low(b, it=0, per=0):
                pool.wait_ge(S["wh_ok"], per * it + (b + 1))
                nc.gpsimd.tensor_tensor(wsp[b % 2][1][:], ring[(N_WO0 + b) % RING][:], wsp[b % 2][0][:].bitcast(F32), ALU.subtract).then_inc(S["wl_ok"], 1)

            low(0)
            for m in range(KT):
                if 2 <= m + 1 < KT:
                    pool.wait_ge(S["o_free"], WAVE + MIX_FILLS + G * m)
                    pool.dma_start(xts[:, (m + 1) % 2, :], xt_d[m + 1]).then_inc(S[f"xt_in{(m + 1) % 2}"], 16)
                low(m + 1)
            pool.wait_ge(S["sum_full"], G)
            pool.dma_start(gf[:], gfin).then_inc(S["gf_in"], 16)
            with pool.Fori(0, FFE - 1) as i:
                for b in range(2 * HB):
                    low(KT + 1 + b, i, 2 * HB)
            for b in range(2 * HB - 1):
                low(N_SPLIT - 2 * HB + 1 + b)
            for i in range(NC):
                pool.wait_ge(S["fin_free"], 2 * i + 2)
                dst = y_out[i * P:(i + 1) * P, :] if i < NC_LAT else yp_out
                pool.dma_start(dst, yo[:, i * D:(i + 1) * D]).then_inc(S["fin_out"], 16)
            pool.wait_ge(S["fin_out"], 16 * NC)

        @block.tensor
        def _(pe):
            def mm(out, lhsT, rhs, start, stop):
                return nc.tensor.matmul(out, lhsT, rhs, start=start, stop=stop)

            def weights(b, it=0, per=0):
                pe.wait_ge(w_full[b % RING], it * (16 * per // RING) + 16 * (b // RING + 1))
                return ring[b % RING]

            pe.wait_ge(S["cst_in"], 5 * 16)
            pe.wait_ge(S["csil_ok"], 1)

            def first_modulation(g):
                if g >= 2:
                    pe.wait_ge(S["mrow1_ok"], g - 1)
                for x in range(4):
                    b = 4 * g + x
                    w = weights(b)[:, :, :].rearrange("p k o -> p (k o)") if b < N_ADA_RING else held[:, b - N_ADA_RING, :]
                    for k in range(2):
                        ins = mm(banks[6 + g % 2][0:2, :], csil[:, 2 * x + k, :], w[:, k * MG:(k + 1) * MG], x == 0 and k == 0, x == 3 and k == 1)
                    ins.then_inc(S["ada1_full"], 1)

            first_modulation(0)
            first_modulation(1)
            pe.wait_ge(S["x_in"], 16 * NC)
            for c in range(KT):
                for cg in range(G):
                    n = G * c + cg
                    if n >= WAVE:
                        pe.wait_ge(S["pro_act"], n - WAVE + 1)
                    for i in range(G):
                        ins = nc.tensor.transpose(banks[n % WAVE][:, i * P:(i + 1) * P], x0[:, cg * G + i, c * P:(c + 1) * P], ident[:])
                    ins.then_inc(S["pro_full"], 1)
            pe.wait_ge(S["held_in"], 16)
            first_modulation(2)
            first_modulation(3)
            pe.wait_ge(S["mrow1_ok"], 4)
            for b in range(N_ADA_FIRST):
                ins = mm(banks[6][:, 2 * b:2 * b + 2], mrow1[0:2, b // 4, (b % 4) * P:(b % 4 + 1) * P], ident[0:2, 0:2], True, True)
            ins.then_inc(S["mt1_full"], 1)
            pe.wait_ge(S["xnrm_ok"], 1)
            for c in range(KT):
                for cg in range(G):
                    n = G * (KT + c) + cg
                    if c < 2:
                        pe.wait_ge(S["pro_act"], n - WAVE + 1)
                    elif c % 2:
                        pe.wait_ge(S["pro_act"], G * KT + G * (c // 2 - 1) + cg + 1)
                    else:
                        pe.wait_ge(S["pro_dve"], G * (c // 2 - 1) + cg + 1)
                    for i in range(G):
                        ins = nc.tensor.transpose(banks[n % WAVE][:, i * P:(i + 1) * P], xnrm[:, cg * G + i, c * P:(c + 1) * P], ident[:])
                    ins.then_inc(S["pro_full"], 1)
            pe.wait_ge(S["pro_dve"], G * KT // 2)
            pe.wait_ge(S["pro_act"], PRO_COPIES)
            for b in range(3):
                w = weights(N_ADA_RING + b)
                for cg in range(G):
                    n = G * (2 * KT + b) + cg
                    if n - WAVE >= 2 * G * KT:
                        pe.wait_ge(S["pro_act"], PRO_COPIES + n - WAVE - 2 * G * KT + 1)
                    for k in range(KT):
                        ins = mm(banks[n % WAVE][:, :GN], w[:, k, :], xn[:, k, cols(cg)], k == 0, k == KT - 1)
                    ins.then_inc(S["pro_full"], 1)
            pe.wait_ge(S["pro_act"], PRO_COPIES + G * 3)
            pe.wait_ge(S["lora_ok"], 1)


            def fills(tu, name, it):
                w = None
                for cg in range(G):
                    for n in range(PIECE):
                        if n == 0:
                            if cg == 0:
                                w = weights(N_PAIR0 + STREAM.index(name), it, PAIR_BLOCKS)
                            for e, count in tu.freed(name, cg):
                                pe.wait_ge(ev[e], count)
                        if name == "v":
                            for x in range(G * n, G * n + G):
                                i, k = x // KT, x % KT
                                t = cg * G + i
                                ins = mm(banks[cg][:, i * P:(i + 1) * P], xn[:, k, t * P:(t + 1) * P], w[:, k, :], k == 0, k == KT - 1)
                        else:
                            ins = mm(banks[cg][:, :GN], w[:, n, :], xn[:, n, cols(cg)], n == 0, n == KT - 1)
                        if n == PIECE - 1:
                            ins.then_inc(S["pj_full"], 1)
                        yield

            def project(tu, name, it):
                for _ in fills(tu, name, it):
                    pass

            def modulation(it, x):
                w = weights(N_PAIR0 + STREAM.index(x), it, PAIR_BLOCKS)[:, :, :].rearrange("p k o -> p (k o)")
                for k in range(2):
                    ins = mm(banks[7][0:2, :], csil[:, 2 * x + k, :], w[:, k * MG:(k + 1) * MG], x == 0 and k == 0, x == 3 and k == 1)
                ins.then_inc(S["ada_full"], 1)

            def single(tu, name, lhsT, rhs):
                for cg in range(G):
                    for e, n in tu.freed(name, cg):
                        pe.wait_ge(ev[e], n)
                    mm(banks[cg][:, :GN], lhsT, rhs[:, cols(cg)], True, True).then_inc(S["pj_full"], 1)

            def prepare(tu, it, behind):
                if it is not None:
                    pe.wait_ge(S["kksq_ok"], it + 1)
                    single(tu, "ks", bones[:], tmp)
                if behind is not None:
                    pe.wait_ge(S["prod_ok"], behind + 1)
                    single(tu, "bon", bones[:], kds)
                def low_rank(d):
                    single(tu, f"w{d}", pk[:, PK_W2 + d * P:PK_W2 + (d + 1) * P], wl)
                    single(tu, f"a{d}", pk[:, PK_A2 + d * P:PK_A2 + (d + 1) * P], al)

                if it is not None:
                    pe.wait_ge(S["pk_in"], 16 * it + 16)
                    low_rank(0)
                    project(tu, "za", it)
                    low_rank(1)
                if behind is not None:
                    for cg in range(G):
                        for e, n in tu.freed("vt", cg):
                            pe.wait_ge(ev[e], n)
                        for i in range(G):
                            for h in range(2):
                                ins = mm(banks[cg][:, i * P:(i + 1) * P], vp[:, cg * G + i, h, :], ident[:], h == 0, h == 1)
                        ins.then_inc(S["pj_full"], 1)
                    pe.wait_ge(S["yc_ok"], behind + 1)
                    single(tu, "mu", bones[:], yf)
                if it is not None:
                    modulation(it, 0)
                    modulation(it, 1)
                if behind is not None:
                    pe.wait_ge(S["ysq_ok"], behind + 1)
                    single(tu, "var", bones[:], cct)
                    pe.wait_ge(S["pl_in"], 16 * behind + 16)
                    for cg in range(G):
                        mm(banks[3 + cg][:, :GN], pl[:, PL_G2:PL_G2 + P], gl[:, cols(cg)], True, True).then_inc(S["gate_full"], 1)
                if it is not None:
                    project(tu, "zb", it)
                    modulation(it, 2)
                    modulation(it, 3)

            def scan(p, filler):
                def fill(n):
                    for _ in range(n):
                        if next(filler, "end") == "end":
                            return

                def serial_ur(j, d):
                    q, c = j % 2, chunk(d, j)
                    o = banks[6 + d][:, 0:P]
                    if 0 < j < NC_LAT:
                        pe.wait_ge(S["s_ok"], NS * p + s_n(j - 1, d))
                    if j:
                        pe.wait_ge(S["y_ok"], 2 * NC * p + (2 * (j - 1) + d + 1))
                    if j < NC_LAT:
                        mm(o, ar[d][:, c, 0, :], state[d][q][:], True, False)
                    mm(o, gmat[q][d][0][:, 2, :], vp[:, c, 0, :], j == NC_LAT, False)
                    mm(o, gmat[q][d][1][:, 2, :], vp[:, c, 1, :], False, True).then_inc(S["ur_full"], 1)

                def serial_u(j, d):
                    q = j % 2
                    pe.wait_ge(S["tri_ok"], 4 * NC * p + (4 * j + 4))
                    pe.wait_ge(S["ur_ok"], 2 * NC * p + (2 * j + d + 1))
                    o = banks[6 + d][:, P:2 * P]
                    mm(o, tt[q][d][:, 0, :], urp[d][:, 0, :], True, False)
                    mm(o, tt[q][d][:, 1, :], urp[d][:, 1, :], False, True).then_inc(S["u_full"], 1)

                def serial_sy(j, d):
                    q, c = j % 2, chunk(d, j)
                    pe.wait_ge(S["u_ok"], 2 * NC * p + (2 * j + d + 1))
                    if j != NC_LAT - 1:
                        o = heads(banks[6 + d][:, 2 * P:3 * P])
                        mm(o, tok[q][:, d, 0, :], diag(up[d][:]), True, False)
                        mm(o, tok[q][:, d, 1, :], diag(vp[:, c]), False, True)
                    o = banks[6 + d][:, 3 * P:4 * P]
                    if j < NC_LAT:
                        mm(o, state[d][q][:], ar[d][:, c, 1, :], True, False)
                    for x, (src, part) in enumerate(((up[d], 1), (vp[:, c], 3))):
                        for h in range(2):
                            hs = slice(h * HD, (h + 1) * HD)
                            ins = mm(o[hs, :], src[:, h, hs], gmat[q][d][h][:, part, :], j == NC_LAT and x == 0, x == 1)
                    ins.then_inc(S["sy_full"], 1)

                def gram(j, h, d):
                    c = chunk(d, j)
                    n = 4 * NC * p + (4 * j + 2 * h + d)
                    if h or d:
                        pe.wait_ge(S["gram_ok"], n)
                    elif j:
                        pe.wait_ge(S["tok_ok"], NC * p + j)
                    pe.wait_ge(S["pad_ok"], n + 1)
                    rhs = ar[d][:, c, :, :].rearrange("p a t -> p (a t)")
                    mm(banks[3][:, 0:2 * P], bkp[d][h][:, 0:C], rhs, True, True)
                    mm(banks[3][:, 2 * P:4 * P], bkp[d][h][:, C:2 * C], rhs, True, True).then_inc(S["gram_full"], 1)

                def token_major(j):
                    pe.wait_ge(S["gram_ok"], 4 * NC * p + (4 * j + 4))
                    for d in range(2):
                        for x in range(2):
                            ins = nc.tensor.transpose(banks[3][:, (2 * d + x) * P:(2 * d + x + 1) * P], bk[d][:, chunk(d, j), x, :], ident[:])
                    ins.then_inc(S["tok_full"], 1)

                def invert(j, lev, h, part):
                    q, o = j % 2, banks[4 + h][:, 0:P]
                    n = NL * NC * p + (NL * j + 2 * lev + h + 1)
                    if part == "turn":
                        if lev == 0:
                            pe.wait_ge(S["xt0_ok"], 2 * NC * p + (2 * j + h + 1))
                        if lev or j:
                            pe.wait_ge(S["xt_ok"], n - 2)
                        nc.tensor.transpose(o, xt[q][h][:], ident[:]).then_inc(S["tr_full"], 1)
                    elif part == "left":
                        pe.wait_ge(S["tc_ok"], n)
                        mm(o, ltc[q][h][:], tc[h][:], True, True).then_inc(S["p1_full"], 1)
                    else:
                        pe.wait_ge(S["p1_ok"], n)
                        pe.wait_ge(S["xtb_ok"], n)
                        mm(o, p1[h][:], xtb[h][:], True, True).then_inc(S["dt_full"], 1)

                fill(4)
                pe.wait_ge(S["s0_ok"], 2 * p + 2)
                for h in range(2):
                    for d in range(2):
                        gram(0, h, d)
                        fill(1)
                token_major(0)
                pe.wait_ge(S["mrow_ok"], p + 1)
                for b in range(4):
                    ins = mm(banks[7][:, 2 * b:2 * b + 2], mrow[:, b * P:(b + 1) * P], ident[0:2, 0:2], True, True)
                ins.then_inc(S["mt_full"], 1)
                for j in range(NC):
                    for lev in range(LEVELS):
                        for h in range(2):
                            invert(j, lev, h, "turn")
                        fill(1)
                        if lev == 3 and j + 1 < NC:
                            gram(j + 1, 0, 0)
                        if lev == 4 and j + 1 < NC:
                            gram(j + 1, 1, 0)
                        for h in range(2):
                            invert(j, lev, h, "left")
                        if j == 1 and lev == 0:
                            pe.wait_ge(S["vp_ok"], p + 1)
                            pe.wait_ge(S["ada_ok"], p + 1)
                        if j and lev < 3:
                            for d in range(2):
                                (serial_ur, serial_u, serial_sy)[lev](j - 1, d)
                        if j == 0:
                            fill(2 if lev < 2 else 1)
                        elif j + 1 < NC and lev in (3, 4):
                            fill(1)
                        if j + 1 < NC:
                            if lev == 3:
                                gram(j + 1, 0, 1)
                            if lev == 4:
                                gram(j + 1, 1, 1)
                            if lev == 5:
                                token_major(j + 1)
                        for h in range(2):
                            invert(j, lev, h, "right")
                        fill(1)
                for stage in (serial_ur, serial_u, serial_sy):
                    for d in range(2):
                        if stage is serial_ur:
                            pe.wait_ge(S["tok_ok"], NC * p + NC)
                        stage(NC - 1, d)
                    fill(2)
                for _ in filler:
                    pass

            def none():
                return iter(())

            def first_projections(tu, it):
                for name, _ in FILL:
                    yield from fills(tu, name, it)

            first = Turn(FIRST, False)
            for _ in first_projections(first, 0):
                pass
            prepare(first, 0, None)
            with pe.Fori(0, PAIRS - 1) as i:
                tu = Turn(TURN, True, i)
                scan(i, first_projections(tu, i + 1))
                prepare(tu, i + 1, i)
            last = Turn(LAST, True, PAIRS - 1)
            scan(PAIRS - 1, none())
            prepare(last, None, PAIRS - 1)

            pe.wait_ge(S["a_in"], 16 * (KT - 1))
            pe.wait_ge(S["gate_ok"], G * PAIRS)

            def wave(n0, it, per_it, b, per_b, src):
                w = weights(b, it, per_b)
                for cg in range(G):
                    n = n0 + cg
                    pe.wait_ge(S["o_free"], it * per_it + n + 1)
                    for k in range(KT):
                        ins = mm(banks[n % WAVE][:, :GN], w[:, k, :], src[:, k, cols(cg)], k == 0, k == KT - 1)
                    ins.then_inc(S["o_full"], 1)

            def mix_pair(it):
                for s in range(2):
                    wave(3 * s, it, 12, N_MIX0 + s, 4, xa)
                pe.wait_ge(S["b_in"], 16 * KT)
                for s in range(2):
                    wave(6 + 3 * s, it, 12, N_MIX0 + 2 + s, 4, xb)

            with pe.Fori(0, KT // 2) as i:
                mix_pair(i)
            pe.wait_ge(S["mix_ok"], G * KT)
            def wave3(n0, it, per_it, b, per_b, ks, x, tail=0, ready=None):
                if tail == 0:
                    pe.wait_ge(S["wl_ok"], it * per_b + (b + 1))
                hi, lo = wsp[b % 2]
                for cg in range(G):
                    n = n0 + cg
                    pe.wait_ge(S["o_free"], it * per_it + n + 1)
                    if ready:
                        pe.wait_ge(S[ready[0]], it * ready[1] + (ready[2] + cg + 1))
                    for k, kw in enumerate(ks):
                        o = banks[n % WAVE][:, :GN]
                        mm(o, hi[:, kw, :], x[0][:, k, cols(cg)], k == 0, False)
                        mm(o, hi[:, kw, :], x[1][:, k, cols(cg)], False, False)
                        ins = mm(o, lo[:, kw, :], x[0][:, k, cols(cg)], False, k == len(ks) - 1)
                    ins.then_inc(S["o_full"], 1)

            with pe.Fori(0, KT // 4) as i:
                for s in range(4):
                    wave3(MIX_FILLS + 3 * s, i, 12, s, 4, range(KT), (mix_hi, mix_lo))
            n_ff = MIX_FILLS + WO_FILLS
            pe.wait_ge(S["o_free"], WAVE + n_ff)
            pe.wait_ge(S["acc_ok"], KT + 1)
            for cg in range(G):
                mm(banks[cg][:, :GN], ones[:], acc[:, cols(cg)], True, True).then_inc(S["sum_full"], 1)
            def first_hidden():
                pe.wait_ge(S["wl_ok"], KT + 1)
                hi, lo = wsp[KT % 2]
                for k in range(KT):
                    pe.wait_ge(S["n2_ok"], k + 1)
                    for cg in range(G):
                        o = banks[(n_ff + cg) % WAVE][:, :GN]
                        mm(o, hi[:, k, :], xn2_hi[:, k, cols(cg)], k == 0, False)
                        mm(o, hi[:, k, :], xn2_lo[:, k, cols(cg)], False, False)
                        ins = mm(o, lo[:, k, :], xn2_hi[:, k, cols(cg)], False, k == KT - 1)
                        if k == KT - 1:
                            ins.then_inc(S["o_full"], 1)

            def feed_forward(i, first):
                if first:
                    first_hidden()
                for s in range(1 if first else 0, HB):
                    wave3(n_ff + 3 * s, i, FF_FILLS, KT + s, 2 * HB, range(KT), (xn2_hi, xn2_lo))
                for s in range(KT):
                    wave3(n_ff + 3 * (HB + s), i, FF_FILLS, KT + HB + s // 2, 2 * HB, range(HB * (s % 2), HB * (s % 2) + HB), (hid_hi, hid_lo),
                          s % 2, ("h_ok", G * HB, G * (HB - 1)) if s == 0 else None)

            feed_forward(0, True)
            with pe.Fori(0, FFE - 1) as i:
                feed_forward(i + 1, False)
            pe.wait_ge(S["o_free"], WAVE + n_ff + FFE * FF_FILLS)
            for t in range(NC):
                if t >= 3:
                    pe.wait_ge(S["fin_free"], 2 * (t - 3) + 2)
                for c in range(KT):
                    ins = nc.tensor.transpose(banks[2 * (t % 3) + c // 4][:, (c % 4) * P:(c % 4 + 1) * P], x2[:, c, t * P:(t + 1) * P], ident[:])
                ins.then_inc(S["fin_full"], 1)

        @block.scalar
        def _(act):
            A = nc.scalar.activation
            for i in range(1, NC_LAT, 2):
                act.dma_start(x0[:, i, :], xs[i * P:(i + 1) * P, :]).then_inc(S["x_in"], 16)
            act.dma_start(x0[:, NC_LAT, :], xp).then_inc(S["x_in"], 16)
            act.dma_start(held[:], wblocks[0:N_HELD].rearrange("b p k o -> p b (k o)")).then_inc(S["held_in"], 16)
            act.wait_ge(S["cst_in"], 5 * 16)
            A(cth[:], csil[:], ACT.Tanh, scale=0.5).then_inc(S["csil_a"], 1)
            act.wait_ge(S["x_in"], 16 * NC)
            for i in range(NC):
                A(xnrm[:, i, :], x0[:, i, :], ACT.Square, accum_out=ss1[:, i:i + 1]).then_inc(S["ss_ok"], 1)
            act.wait_ge(S["ss_ok"], NC)
            act.wait_ge(S["cst_ok"], 1)
            A(rs1[:], ss1[:], ACT.Sqrt, scale=1.0 / D, bias=eps_t[:, 0:1]).then_inc(S["rs_a1"], 1)
            for c in range(KT):
                if c >= 2:
                    act.wait_ge(S[f"xt_out{c % 2}"], 16 * (c // 2))
                for cg in range(G):
                    n = G * c + cg
                    act.wait_ge(S["pro_full"], n + 1)
                    A(xt_s[:, c % 2, cols(cg)], banks[n % WAVE][:, :GN], ACT.Copy).then_inc(S["pro_act"], 1)
            act.wait_ge(S["mul1_ok"], 1)
            for c in range(1, KT, 2):
                for cg in range(G):
                    n = G * (KT + c) + cg
                    act.wait_ge(S["pro_full"], n + 1)
                    for a, b, kind in kinds(cg):
                        ins = A(xn[:, c, a:b], banks[n % WAVE][:, a - cg * GN:b - cg * GN], ACT.Identity,
                                scale=mul1[:, c, kind:kind + 1], bias=mods[:, c, kind:kind + 1])
                    ins.then_inc(S["pro_act"], 1)
            for b, (dst, f, sc) in enumerate(((wl, ACT.Tanh, 1.0), (al, ACT.Copy, 1.0), (gl, ACT.Tanh, 0.5))):
                for cg in range(G):
                    n = G * (2 * KT + b) + cg
                    act.wait_ge(S["pro_full"], n + 1)
                    A(dst[:, cols(cg)], banks[n % WAVE][:, :GN], f, scale=sc).then_inc(S["pro_act"], 1)


            def empty(tu, name, out, func, groups=range(G), **kw):
                for cg in groups:
                    act.wait_ge(S["pj_full"], tu.full(name, cg))
                    A(out(cg), banks[cg][:, :GN], func, **kw).then_inc(ev["A"], 1)

            def prepare(tu, it, behind):
                if it is not None:
                    act.wait_ge(S["half_ok"], it + 1)
                    A(tmp[:], kt[:], ACT.Square, scale=pk[:, PK_VEC + V_KK:PK_VEC + V_KK + 1]).then_inc(S["kksq_ok"], 1)
                    empty(tu, "ks", lambda cg: en[:, cols(cg)], ACT.Sqrt)
                if behind is not None:
                    empty(tu, "bon", lambda cg: cct[:, cols(cg)], ACT.Copy)
                def low_rank(d):
                    empty(tu, f"w{d}", lambda cg: thw[d][:, cols(cg)], ACT.Tanh, scale=0.5, bias=half[:, d:d + 1])
                    act.wait_ge(ev["A"], tu.emptied(f"w{d}")[1])
                    A(thw[d][:], thw[d][:], ACT.Copy, scale=-0.5 * DECAY, bias=-0.5 * DECAY).then_inc(S["logw_ok"], 1)
                    empty(tu, f"a{d}", lambda cg: tha[d][:, cols(cg)], ACT.Tanh, scale=0.5, bias=half[:, 2 + d:3 + d])

                if it is not None:
                    low_rank(0)
                    act.wait_ge(S["pj_full"], tu.full("ks", G - 1))
                    k_factor(tu, 0)
                    if behind is not None:
                        act.wait_ge(S["ga_out"], 32 * it)
                    empty(tu, "za", lambda cg: gat[:, cols(cg)], ACT.Tanh, (0, 1), scale=0.5)
                    decays(it, 0)
                    empty(tu, "za", lambda cg: gat[:, cols(cg)], ACT.Tanh, (2,), scale=0.5)
                    low_rank(1)
                    act.wait_ge(S["kd_ok"], 2 * it + 1)
                    k_factor(tu, 1)
                if behind is not None:
                    act.wait_ge(ev["D"], tu.emptied("mu")[1])
                    A(cct[:], yf[:], ACT.Square).then_inc(S["ysq_ok"], 1)
                    empty(tu, "var", lambda cg: cct[:, cols(cg)], ACT.Sqrt, scale=1.0 / HD, bias=eps_t[:, 1:2])
                if it is not None:
                    decays(it, 1)
                    for h in range(2):
                        hs = slice(h * HD, (h + 1) * HD)
                        ins = A(vp[:, :, h, hs], vn[:, :, hs], ACT.Copy)
                    ins.then_inc(S["vp_ok"], 1)
                    act.wait_ge(S["ga_out"], 32 * it + 16)
                    empty(tu, "zb", lambda cg: gat[:, cols(cg)], ACT.Tanh, scale=0.5)
                if behind is not None and it is not None:
                    act.wait_ge(S["xa_out"], 16 * behind + 16)

            def k_factor(tu, d):
                act.wait_ge(ev["A"], tu.emptied(f"a{d}")[1])
                A(tmp[:], tha[d][:], ACT.Identity, scale=half[:, 4:5], bias=half[:, 5:6]).then_inc(S["kf_ok"], 1)

            def decays(it, d):
                act.wait_ge(S["lw_ok"], 2 * it + d + 1)
                A(en[:], cum[:], ACT.Exp, scale=-1.0).then_inc(S["exp_ok"], 1)
                act.wait_ge(S["exp_ok"], 8 * it + (4 * d + 1))
                A(cum[:], cum[:], ACT.Exp).then_inc(S["exp_ok"], 1)
                A(thw[d][:], thw[d][:], ACT.Exp).then_inc(S["exp_ok"], 1)
                A(emid[d][:], mid[d][:], ACT.Exp).then_inc(S["exp_ok"], 1)

            def scan(p, tu):
                def at(j, d):
                    return 2 * NC * p + (2 * j + d + 1)

                def pads(j):
                    for h in range(2):
                        hs = slice(h * HD, (h + 1) * HD)
                        for d in range(2):
                            if j:
                                act.wait_ge(S["gram_full"], 4 * NC * p + (4 * (j - 1) + 2 * h + d + 1))
                            A(bkp[d][h][hs, :], bk[d][hs, chunk(d, j), :, :].rearrange("p x t -> p (x t)"), ACT.Copy).then_inc(S["pad_ok"], 1)

                def to_diag(dst, j, d, full, col, ok):
                    act.wait_ge(S[full], at(j, d))
                    A(diag(dst[d][:]), heads(banks[6 + d][:, col:col + P]), ACT.Copy).then_inc(S[ok], 1)

                def outputs(j, d):
                    act.wait_ge(S["sy_full"], at(j, d))
                    if j != NC_LAT - 1:
                        act.wait_ge(S["s_ok"], NS * p + s_n(j, d))
                    c = chunk(d, j)
                    A((yf, yb)[d][:, c * C:(c + 1) * C], banks[6 + d][:, 3 * P:4 * P], ACT.Copy).then_inc(S["y_ok"], 1)

                def serial(j, stage):
                    for d in range(2):
                        if stage == 0:
                            to_diag(urp, j, d, "ur_full", 0, "ur_ok")
                        elif stage == 1:
                            to_diag(up, j, d, "u_full", P, "u_ok")
                        else:
                            outputs(j, d)

                def tokens(j):
                    act.wait_ge(S["tok_full"], NC * p + j + 1)
                    A(tok[j % 2][:].rearrange("p d x c -> p (d x c)"), banks[3][:, :], ACT.Copy).then_inc(S["tok_ok"], 1)

                def projected(n):
                    name, cg = FILL[n // G][0], n % G
                    if tu is None or FILL[n // G][1] != "A":
                        return
                    dst = {"r": rt, "k": kt, "cc": cct}[name][:, cols(cg)] if name != "v" else vn[:, cg * G:(cg + 1) * G, :].rearrange("p t v -> p (t v)")
                    act.wait_ge(S["pj_full"], tu.full(name, cg))
                    A(dst, banks[cg][:, :GN], ACT.Copy).then_inc(ev["A"], 1)

                early = {0: (0, 1), 1: (3,), 2: (5,), 3: (7,), 4: (8,), 5: (10,)}
                late = {0: (2,), 1: (4,), 2: (6,), 4: (9,), 5: (11,)}
                pads(0)
                tokens(0)
                for j in range(NC):
                    if j + 1 < NC:
                        pads(j + 1)
                    for lev in range(3):
                        if j:
                            serial(j - 1, lev)
                    if j + 1 < NC:
                        for n in early.get(j, ()):
                            projected(n)
                        tokens(j + 1)
                        for n in late.get(j, ()):
                            projected(n)
                for lev in range(3):
                    serial(NC - 1, lev)

            first = Turn(FIRST, False)
            empty(first, "r", lambda cg: rt[:, cols(cg)], ACT.Copy)
            empty(first, "k", lambda cg: kt[:, cols(cg)], ACT.Copy)
            act.wait_ge(S["zero_ok"], 1)
            empty(first, "v", lambda cg: vn[:, cg * G:(cg + 1) * G, :].rearrange("p t v -> p (t v)"), ACT.Copy)
            empty(first, "cc", lambda cg: cct[:, cols(cg)], ACT.Copy)
            prepare(first, 0, None)
            with act.Fori(0, PAIRS - 1) as i:
                tu = Turn(TURN, True, i)
                act.wait_ge(S["s0_ok"], 2 * i + 2)
                scan(i, tu)
                prepare(tu, i + 1, i)
            act.wait_ge(S["s0_ok"], 2 * PAIRS)
            scan(PAIRS - 1, None)
            prepare(Turn(LAST, True, PAIRS - 1), None, PAIRS - 1)

            def high(b, it=0, per=0, before=0):
                slot = (N_WO0 + b) % RING
                act.wait_ge(w_full[slot], it * (16 * per // RING) + 16 * ((N_WO0 + b) // RING + 1))
                if before is not None:
                    act.wait_ge(S["o_full"], before)
                A(wsp[b % 2][0][:], ring[slot][:], ACT.Copy).then_inc(S["wh_ok"], 1)

            act.wait_ge(S["gate_ok"], G * PAIRS)
            for m in range(KT):
                for cg in range(G):
                    act.wait_ge(S["raw_ok"], G * m + cg + 1)
                    A(mix_hi[:, m, cols(cg)], mix_raw[:, m, cols(cg)], ACT.Copy).then_inc(S["hi_ok"], 1)
                if m == KT - 2:
                    high(0, before=None)
            for m in range(KT):
                high(m + 1, before=MIX_FILLS + G * m if m else None)
                act.wait_ge(S["o_free"], WAVE + MIX_FILLS + G * (m + 1))
                if m >= 2:
                    act.wait_ge(S["acc_ok"], m)
                A(sq2[:, m % 2, :], x2[:, m, :], ACT.Square).then_inc(S["sq_ok"], 1)
            for cg in range(G):
                act.wait_ge(S["sum_full"], cg + 1)
                A(rs2[:, cols(cg)], banks[cg][:, :GN], ACT.Sqrt, scale=1.0 / D, bias=eps_t[:, 0:1]).then_inc(S["rs_a2"], 1)
            for m in range(KT):
                act.wait_ge(S["xs_ok"], m + 1)
                for a, b, kind in ((0, LAT, 0), (LAT, T, 1)):
                    ins = A(xn2_raw[:, m, a:b], xn2_raw[:, m, a:b], ACT.Identity,
                            scale=mul2[:, m, kind:kind + 1], bias=mods[:, 24 + m, kind:kind + 1])
                ins.then_inc(S["raw2_ok"], 1)
                act.wait_ge(S["raw2_ok"], m + 1)
                A(xn2_hi[:, m, :], xn2_raw[:, m, :], ACT.Copy).then_inc(S["n2hi_ok"], 1)

            n_ff = MIX_FILLS + WO_FILLS

            def hidden(it, s):
                for cg in range(G):
                    act.wait_ge(S["hsq_ok"], G * HB * it + (G * s + cg + 1))
                    A(hid_hi[:, s, cols(cg)], hsq[:, (G * s + cg) % 2, :], ACT.Copy).then_inc(S["hhi_ok"], 1)

            def feed_forward(it, last):
                for b in range(2 * HB):
                    used = n_ff + (G * b if b <= HB else G * HB + 2 * G * (b - HB))
                    if not (last and b == 2 * HB - 1):
                        high(KT + b + 1, it, 2 * HB, FF_FILLS * it + used)
                    if b < HB:
                        hidden(it, b)

            with act.Fori(0, FFE - 1) as i:
                feed_forward(i, False)
            feed_forward(FFE - 1, True)
            for t in range(NC):
                act.wait_ge(S["fin_full"], t + 1)
                for i in range(2):
                    A(squares[:, (2 * t + i) * 512:(2 * t + i + 1) * 512], banks[2 * (t % 3) + i][:, :], ACT.Square, accum_out=fss[:, t, i:i + 1]).then_inc(S["fin_sq"], 1)
                act.wait_ge(S["fin_sum"], t + 1)
                A(frs[:, t:t + 1], fss[:, t, 0:1], ACT.Sqrt, scale=1.0 / D, bias=eps_t[:, 0:1]).then_inc(S["fin_std"], 1)

        @block.vector
        def _(dve):
            V = nc.vector
            ch = Chain(dve, S["dve_chain"])
            mul, add, sub = ALU.mult, ALU.add, ALU.subtract
            stt = V.scalar_tensor_tensor

            def bc(x, n):
                return x.to_broadcast([P, x.shape[1], n]) if len(x.shape) == 3 else x.unsqueeze(2).to_broadcast([P, x.shape[1], n])

            ch.step(V.memset(eps_t[:, 0:1], EPS))
            V.memset(eps_t[:, 1:2], LNX_EPS).then_inc(S["cst_ok"], 1)
            dve.wait_ge(S["csil_a"], 1)
            ch.step(V.tensor_scalar(cth[:], cth[:], 0.5, 0.5, mul, add))
            ch.settle()
            V.tensor_tensor(csil[:], csil[:], cth[:], mul).then_inc(S["csil_ok"], 1)

            def first_rows(g):
                dve.wait_ge(S["ada1_full"], 4 * g + 4)
                V.tensor_copy(mrow1[0:2, g, :], banks[6 + g % 2][0:2, :]).then_inc(S["mrow1_ok"], 1)

            for g in range(2):
                first_rows(g)
            dve.wait_ge(S["rs_a1"], 1)
            ch.step(V.reciprocal(rs1[:], rs1[:]))
            ch.settle()
            for i in range(NC):
                ins = V.tensor_scalar(xnrm[:, i, :], x0[:, i, :], rs1[:, i:i + 1], None, mul)
            ins.then_inc(S["xnrm_ok"], 1)
            dve.wait_ge(S["mask_in"], 16)
            for dst, k, n in ((offm[:].rearrange("p a b -> p (a b)"), K_OFF, 6 * P), (trim[:].rearrange("p a b -> p (a b)"), K_TRI, 6 * P), (m1c[:], K_M1, P),
                              (gmask[:].rearrange("p a b -> p (a b)"), K_GM, 4 * P)):
                ch.step(V.tensor_copy(dst, cst[:, k - K_OFF:k - K_OFF + n]))
            for g in range(2, 4):
                first_rows(g)
            dve.wait_ge(S["mt1_full"], 1)
            ch.step(V.tensor_tensor(mods[:, 0:16, :], banks[6][:, 0:32].rearrange("p (b c) -> p b c", c=2), bc(vec[:, 0:16], 2), add))
            ch.settle()
            ch.step(V.tensor_scalar(mul1[:], mods[:, 8:16, :], 1.0, None, add))
            ch.settle()
            V.tensor_tensor(mul1[:], mul1[:], bc(vec[:, 48:56], 2), mul).then_inc(S["mul1_ok"], 1)
            dve.wait_ge(S["mul1_ok"], 1)
            for c in range(0, KT, 2):
                for cg in range(G):
                    n = G * (KT + c) + cg
                    dve.wait_ge(S["pro_full"], n + 1)
                    for a, b, kind in kinds(cg):
                        ins = V.tensor_scalar(xn[:, c, a:b], banks[n % WAVE][:, a - cg * GN:b - cg * GN],
                                              mul1[:, c, kind:kind + 1], mods[:, c, kind:kind + 1], mul, add)
                    ins.then_inc(S["pro_dve"], 1)
            dve.wait_ge(S["xt_out0"], 8 * KT)
            dve.wait_ge(S["xt_out1"], 8 * KT)
            for x in padded[1:]:
                ch.step(V.memset(x[:], 0.0))
            V.memset(vp[:], 0.0).then_inc(S["zero_ok"], 1)
            dve.wait_ge(S["pro_act"], PRO_COPIES + G * 3)
            V.tensor_scalar(gl[:], gl[:], 0.5, 0.5, mul, add).then_inc(S["lora_ok"], 1)
            dve.wait_ge(S["zero_ok"], 1)
            ch.settle()


            def par(i):
                return pk[:, PK_VEC + i:PK_VEC + i + 1]

            def full(tu, name, cg):
                dve.wait_ge(S["pj_full"], tu.full(name, cg))

            def filled(tu, name):
                e, n = tu.emptied(name)
                dve.wait_ge(ev[e], n)

            def a3(x):
                return x.rearrange("p (c t) -> p c t", t=C)

            def direction(tu, it, d):
                dve.wait_ge(S["logw_ok"], 2 * it + d + 1)
                for c in range(NC):
                    o, x = (cum[:, c * C:(c + 1) * C], thw[d][:, c * C:(c + 1) * C])
                    if d == 1:
                        o, x = o[:, ::-1], x[:, ::-1]
                    ch.step(V.tensor_tensor_scan(o, ones[:], x, 0.0, mul, add))
                ch.settle()
                end = C - 1 if d == 0 else 0
                ch.step(V.tensor_scalar(mid[d][:], a3(cum[:])[:, :, end:end + 1].rearrange("p c t -> p (c t)"), 0.5, None, mul))
                ch.settle()
                ch.step(V.tensor_tensor(a3(cum[:]), a3(cum[:]), bc(mid[d][:], C), sub))
                ch.settle()
                V.tensor_tensor(thw[d][:], cum[:], thw[d][:], sub).then_inc(S["lw_ok"], 1)
                kd = kds if d == 0 else tmp
                dve.wait_ge(S["kf_ok"], 2 * it + d + 1)
                V.tensor_tensor(kd[:], tmp[:], kt[:], mul).then_inc(S["kd_ok"], 1)
                filled(tu, f"a{d}")
                ch.step(stt(tha[d][:], tha[d][:], 1.0, kk[:], add, mul))
                ch.settle()

            def operands(it, d):
                kd = kds if d == 0 else tmp
                dve.wait_ge(S["kd_ok"], 2 * it + d + 1)
                dve.wait_ge(S["exp_ok"], 8 * it + (4 * d + 1))
                ch.step(V.tensor_tensor(bk[d][:, :, 1, :], a3(kd[:]), a3(en[:]), mul))
                ch.step(stt(bk[d][:, :, 0, :], a3(tha[d][:]), -0.5, a3(en[:]), mul, mul))
                dve.wait_ge(S["exp_ok"], 8 * it + (4 * d + 2))
                ch.step(V.tensor_tensor(ar[d][:, :, 1, :], a3(rt[:]), a3(cum[:]), mul))
                dve.wait_ge(S["exp_ok"], 8 * it + (4 * d + 3))
                ch.step(V.tensor_tensor(ar[d][:, :, 0, :], a3(kk[:]), a3(thw[d][:]), mul))
                dve.wait_ge(S["exp_ok"], 8 * it + (4 * d + 4))
                g = gstep[d][:, 0:NC_LAT - 1] if d == 0 else gstep[d][:, 1:NC_LAT]
                ch.step(V.tensor_tensor(g, emid[d][:, 0:NC_LAT - 1], emid[d][:, 1:NC_LAT], mul))
                ch.settle()

            def halves(it):
                dve.wait_ge(S["pk_in"], 16 * it + 16)
                ch.step(V.tensor_scalar(half[:, 0:4], pk[:, PK_VEC + V_W0:PK_VEC + V_W0 + 4], 0.5, None, mul))
                ch.step(V.tensor_scalar(half[:, 4:5], par(V_KA), 0.5, None, mul))
                V.tensor_scalar(half[:, 5:6], par(V_KA), -0.5, 1.0, mul, add).then_inc(S["half_ok"], 1)

            def branch_b(tu, it, part):
                grid, line = [[x[:, a:b].rearrange("p (r w) -> p r w", w=w) for x in (cct, cv)] for a, b, w in ((0, LAT, ROW), (LAT, T, CTX))]
                if part < 3:
                    e, n = tu.emptied("cc", part)
                    dve.wait_ge(ev[e], n)
                    full(tu, "ch", part)
                    V.tensor_tensor(cct[:, cols(part)], banks[part][:, :GN], cct[:, cols(part)], mul).then_inc(ev["D"], 1)
                elif part == 3:
                    halves(it)
                    dve.wait_ge(ev["D"], tu.emptied("ch")[1])
                    ch.step(V.tensor_scalar(cv[:], cct[:], par(V_CONV + 1), None, mul))
                elif part == 4:
                    ch.settle()
                    for (u, o), w in ((grid, ROW), (line, CTX)):
                        ch.step(stt(o[:, :, 1:w], u[:, :, 0:w - 1], par(V_CONV), o[:, :, 1:w], mul, add))
                elif part == 5:
                    ch.settle()
                    for (u, o), w in ((grid, ROW), (line, CTX)):
                        ch.step(stt(o[:, :, 0:w - 1], u[:, :, 1:w], par(V_CONV + 2), o[:, :, 0:w - 1], mul, add))
                else:
                    cg = part - 6
                    if cg == 0:
                        ch.settle()
                    full(tu, "cb", cg)
                    V.tensor_tensor(cv[:, cols(cg)], banks[cg][:, :GN], cv[:, cols(cg)], mul).then_inc(ev["D"], 1)

            def prepare(tu, it, behind):
                if it is not None:
                    filled(tu, "ks")
                    ch.step(V.tensor_scalar(en[:], en[:], 1e-6, None, ALU.max))
                    ch.settle()
                    ch.step(V.reciprocal(en[:], en[:]))
                    ch.settle()
                    if behind is not None:
                        dve.wait_ge(S["yc_ok"], behind + 1)
                    ch.step(stt(kk[:], kt[:], par(V_KK), en[:], mul, mul))
                    ch.settle()
                    if behind is not None:
                        full(tu, "bon", G - 1)
                    direction(tu, it, 0)
                    operands(it, 0)
                if behind is not None:
                    filled(tu, "bon")
                    if it is not None:
                        dve.wait_ge(S["xb_out"], 16 * it + 16)
                    for cg in range(G):
                        full(tu, "vt", cg)
                        V.tensor_tensor(cv[:, cols(cg)], banks[cg][:, :GN], cct[:, cols(cg)], mul).then_inc(ev["D"], 1)
                    for cg in range(G):
                        full(tu, "mu", cg)
                        stt(yf[:, cols(cg)], banks[cg][:, :GN], -1.0 / HD, yf[:, cols(cg)], mul, add).then_inc(ev["D"], 1)
                if it is not None:
                    direction(tu, it, 1)
                if behind is not None:
                    filled(tu, "var")
                    ch.step(V.reciprocal(cct[:], cct[:]))
                    ch.settle()
                    ch.step(V.tensor_tensor(yf[:], yf[:], cct[:], mul))
                    ch.settle()
                    dve.wait_ge(S["pl_in"], 16 * behind + 16)
                    ch.step(stt(yf[:], yf[:], pl[:, PL_W:PL_W + 1], cv[:], mul, add))
                    ch.settle()
                if it is not None:
                    operands(it, 1)
                if behind is not None:
                    for cg in range(G):
                        dve.wait_ge(S["gate_full"], G * behind + cg + 1)
                        dst = yf[:, cols(cg)] if it is not None else xa[:, KT - 1, cols(cg)]
                        stt(dst, yf[:, cols(cg)], pl[:, PL_B:PL_B + 1], banks[3 + cg][:, :GN], add, mul).then_inc(S["gate_ok"], 1)
                if it is not None:
                    dve.wait_ge(S["prod_ok"], it + 1)
                    for d in range(2):
                        c = chunk(d, 0)
                        for h in range(2):
                            hs = slice(h * HD, (h + 1) * HD)
                            ins = V.tensor_scalar(state[d][0][hs, hs], pk[hs, PK_ST + d * HD:PK_ST + (d + 1) * HD], emid[d][hs, c:c + 1], None, mul)
                        ins.then_inc(S["s0_ok"], 1)
                if it is not None:
                    dve.wait_ge(S["xb_out"], 16 * it + 16)
                    dve.wait_ge(S["ada_full"], 4 * it + 4)
                    V.tensor_copy(mrow, banks[7][0:2, :]).then_inc(S["mrow_ok"], 1)
                if behind is not None:
                    dve.wait_ge(S["sf_out"], 32 * behind + 32)

            spread = {(6, 5): 0, (7, 1): 1, (7, 5): 2, (8, 0): 3, (8, 1): 4, (8, 2): 5, (8, 4): 6, (8, 5): 7}

            def scan(p, tu, it):
                def states(j, d):
                    q, c = j % 2, chunk(d, j)
                    if j == NC_LAT - 1:
                        return
                    dve.wait_ge(S["sy_full"], 2 * NC * p + (2 * j + d + 1))
                    o = banks[6 + d]
                    if j < NC_LAT:
                        new = state[d][1 - q]
                        ch.step(V.tensor_tensor(new[:], o[:, 2 * P:3 * P], state[d][q][:], add))
                        ch.settle()
                        stt(new[:], new[:], gstep[d][:, c:c + 1], bones[:], mul, mul).then_inc(S["s_ok"], 1)
                    else:
                        for h in range(2):
                            hs = slice(h * HD, (h + 1) * HD)
                            V.tensor_scalar(sfin[hs, d, :], o[hs, 2 * P + h * HD:2 * P + (h + 1) * HD],
                                            emid[d][hs, c:c + 1], None, mul).then_inc(S["sf_ok"], 1)
                        dve.wait_ge(S["sf_ok"], 4 * p + (2 * d + 2))
                        V.tensor_copy(mid[d][:, 0:1], emid[d][:, 0:1]).then_inc(S["s_ok"], 1)

                def gram(j, h, d):
                    dve.wait_ge(S["gram_full"], 4 * NC * p + (4 * j + 2 * h + d + 1))
                    V.tensor_tensor(gmat[j % 2][d][h][:].rearrange("p (x a) t -> p x (a t)", x=2),
                                    banks[3][:, :].rearrange("p (x a) -> p x a", x=2),
                                    gmask[:, d:d + 1, :].to_broadcast([P, 2, 2 * P]), mul).then_inc(S["gram_ok"], 1)

                for h in range(2):
                    for d in range(2):
                        gram(0, h, d)
                for j in range(NC):
                    q = j % 2
                    for lev in range(LEVELS):
                        at = NL * NC * p + (NL * j + 2 * lev + 1)
                        for h in range(2):
                            dve.wait_ge(S["tr_full"], at + h)
                            V.tensor_tensor(tc[h][:], banks[4 + h][:, 0:P], trim[:, lev, :], mul).then_inc(S["tc_ok"], 1)
                        if lev in (3, 4) and j + 1 < NC:
                            gram(j + 1, lev - 3, 0)
                        for h in range(2):
                            dve.wait_ge(S["p1_full"], at + h)
                            V.tensor_tensor(p1[h][:], banks[4 + h][:, 0:P], offm[:, lev, :], mul).then_inc(S["p1_ok"], 1)
                        if j and lev == 2:
                            for d in range(2):
                                states(j - 1, d)
                        if lev in (3, 4) and j + 1 < NC:
                            gram(j + 1, lev - 3, 1)
                        for h in range(2):
                            dve.wait_ge(S["dt_full"], at + h)
                            V.tensor_tensor(xt[q][h][:], banks[4 + h][:, 0:P], xt[q][h][:], add).then_inc(S["xt_ok"], 1)
                        if (j, lev) == (0, 1):
                            dve.wait_ge(S["mt_full"], p + 1)
                            V.tensor_tensor(mods[:, bass.ds(4 * p + 16, 4), :], banks[7][:, 0:8].rearrange("p (b c) -> p b c", c=2),
                                            bc(vec[:, bass.ds(4 * p + 16, 4)], 2), add).then_inc(S["ada_ok"], 1)
                        if tu is not None and (j, lev) in spread:
                            branch_b(tu, it, spread[j, lev])
                for d in range(2):
                    states(NC - 1, d)
                if tu is not None:
                    branch_b(tu, it, 8)

            first = Turn(FIRST, False)
            for part in range(9):
                branch_b(first, 0, part)
            prepare(first, 0, None)
            with dve.Fori(0, PAIRS - 1) as i:
                tu = Turn(TURN, True, i)
                ch.enter(i, CH_PAIR)
                scan(i, tu, i + 1)
                prepare(tu, i + 1, i)
            ch.leave(PAIRS - 1)
            scan(PAIRS - 1, None, None)
            prepare(Turn(LAST, True, PAIRS - 1), None, PAIRS - 1)

            ch.step(V.tensor_scalar(mul2[:], mods[:, 32:40, :], 1.0, None, add))
            ch.settle()
            ch.step(V.tensor_tensor(mul2[:], mul2[:], bc(vec[:, 56:64], 2), mul))
            V.tensor_scalar(hgt1[:], mods[:, 16:24, :], 0.5, None, mul).then_inc(S["o_free"], WAVE)
            dve.wait_ge(S["o_free"], WAVE)
            ch.settle()
            def mix_low(it, s, cg):
                dve.wait_ge(S["hi_ok"], 2 * G * it + (G * s + cg + 1))
                m = 2 * it + s
                V.tensor_tensor(mix_lo[:, m, cols(cg)], mix_raw[:, m, cols(cg)], mix_hi[:, m, cols(cg)].bitcast(F32), sub).then_inc(S["mix_ok"], 1)

            with dve.Fori(0, KT // 2) as i:
                for x in range(2):
                    for s in range(2):
                        m = 2 * i + s
                        if x == 0:
                            dve.wait_ge(S["gt_in"], 64 * i + 32 * s + 32)
                        for cg in range(G):
                            n = 6 * x + 3 * s + cg
                            dve.wait_ge(S["o_full"], 12 * i + n + 1)
                            raw = mix_raw[:, m, cols(cg)]
                            if x == 0:
                                stt(raw, gts[:, s, 0, cols(cg)], 1.0, banks[n % WAVE][:, :GN], add, mul).then_inc(S["o_free"], 1)
                            else:
                                if n > 6:
                                    dve.wait_ge(S["raw_ok"], 2 * G * i + (G * s + cg))
                                stt(mtmp[:], gts[:, s, 1, cols(cg)], 1.0, banks[n % WAVE][:, :GN], add, mul).then_inc(S["o_free"], 1)
                                dve.wait_ge(S["o_free"], 12 * i + (WAVE + n + 1))
                                V.tensor_tensor(raw, raw, mtmp[:], add).then_inc(S["raw_ok"], 1)
                                if cg:
                                    mix_low(i, s, cg - 1)
                        if x == 1:
                            mix_low(i, s, G - 1)
            V.memset(acc, 0.0).then_inc(S["acc_ok"], 1)
            with dve.Fori(0, KT // 4) as i:
                for s in range(4):
                    m = 4 * i + s
                    dve.wait_ge(S[f"xt_in{s % 2}"], 32 * i + 16 * (s // 2) + 16)
                    for cg in range(G):
                        n = MIX_FILLS + 3 * s + cg
                        dve.wait_ge(S["o_full"], 12 * i + (n + 1))
                        for a, b, kind in kinds(cg):
                            ins = stt(x2[:, m, a:b], banks[n % WAVE][:, a - cg * GN:b - cg * GN], hgt1[:, m, kind:kind + 1], xts[:, s % 2, a:b], mul, add)
                        ins.then_inc(S["o_free"], 1)
                    dve.wait_ge(S["sq_ok"], 4 * i + s + 1)
                    dve.wait_ge(S["acc_ok"], 4 * i + s + 1)
                    V.tensor_tensor(acc, acc, sq2[:, s % 2, :], add).then_inc(S["acc_ok"], 1)
            dve.wait_ge(S["rs_a2"], G)
            ch.step(V.reciprocal(rs2, rs2))
            ch.settle()
            def norm_low(m):
                dve.wait_ge(S["n2hi_ok"], m + 1)
                V.tensor_tensor(xn2_lo[:, m, :], xn2_raw[:, m, :], xn2_hi[:, m, :].bitcast(F32), sub).then_inc(S["n2_ok"], 1)

            for m in range(KT):
                V.tensor_tensor(xn2_raw[:, m, :], x2[:, m, :], rs2, mul).then_inc(S["xs_ok"], 1)
                if m >= 2:
                    norm_low(m - 2)
            norm_low(KT - 2)
            norm_low(KT - 1)
            n_ff = MIX_FILLS + WO_FILLS

            def hidden_low(it, n):
                s, cg = n // G, n % G
                dve.wait_ge(S["hhi_ok"], G * HB * it + (n + 1))
                V.tensor_tensor(hid_lo[:, s, cols(cg)], hsq[:, n % 2, :], hid_hi[:, s, cols(cg)].bitcast(F32), sub).then_inc(S["h_ok"], 1)

            with dve.Fori(0, FFE) as i:
                for n in range(G * HB):
                    bank = banks[(n_ff + n) % WAVE][:, :GN]
                    dve.wait_ge(S["o_full"], FF_FILLS * i + (n_ff + n + 1))
                    if n >= 2:
                        dve.wait_ge(S["h_ok"], G * HB * i + (n - 1))
                    V.tensor_scalar(hsq[:, n % 2, :], bank, 0.0, None, ALU.max).then_inc(S["o_free"], 1)
                    dve.wait_ge(S["o_free"], FF_FILLS * i + (WAVE + n_ff + n + 1))
                    V.tensor_tensor(hsq[:, n % 2, :], hsq[:, n % 2, :], hsq[:, n % 2, :], mul).then_inc(S["hsq_ok"], 1)
                    if n:
                        hidden_low(i, n - 1)
                hidden_low(i, G * HB - 1)
                for s in range(KT):
                    for cg in range(G):
                        n = n_ff + G * (HB + s) + cg
                        dve.wait_ge(S["o_full"], FF_FILLS * i + (n + 1))
                        for a, b, kind in kinds(cg):
                            ins = stt(x2[:, s, a:b], banks[n % WAVE][:, a - cg * GN:b - cg * GN], mods[:, 40 + s, kind:kind + 1], x2[:, s, a:b], mul, add)
                        ins.then_inc(S["o_free"], 1)
            dve.wait_ge(S["gf_in"], 16)
            for t in range(NC):
                dve.wait_ge(S["fin_sq"], 2 * t + 2)
                V.tensor_tensor(fss[:, t, 0:1], fss[:, t, 0:1], fss[:, t, 1:2], add).then_inc(S["fin_sum"], 1)
                dve.wait_ge(S["fin_std"], t + 1)
                ch.step(V.reciprocal(frs[:, t:t + 1], frs[:, t:t + 1]))
                ch.settle()
                for i in range(2):
                    stt(yo[:, t * D + i * 512:t * D + (i + 1) * 512], banks[2 * (t % 3) + i][:, :], frs[:, t:t + 1],
                        gf[:, i * 512:(i + 1) * 512], mul, mul).then_inc(S["fin_free"], 1)


def constants():
    import numpy as np
    k = np.zeros((P, K_ALL), np.float32)
    i = np.arange(P)
    k[:, K_ID:K_ID + P] = np.eye(P)
    k[:, K_BO:K_BO + P] = (i[:, None] // HD) == (i[None, :] // HD)
    k[:, K_ONE:K_ONE + P] = 1.0
    tri = [i[:, None] >= i[None, :], i[:, None] <= i[None, :]]
    for lev in range(LEVELS):
        n = 2 << lev
        blk, blk2 = i // n, i // (2 * n)
        same, same2 = blk[:, None] == blk[None, :], blk2[:, None] == blk2[None, :]
        k[:, K_OFF + lev * P:K_OFF + (lev + 1) * P] = same2 & ~same
        k[:, K_TRI + lev * P:K_TRI + (lev + 1) * P] = same & np.where(blk[:, None] % 2 == 0, tri[0], tri[1])
    k[:, K_M1:K_M1 + P] = (i[:, None] // 2 == i[None, :] // 2) & (i[:, None] != i[None, :])
    for d in range(2):
        s, t = i[:, None], i[None, :]
        c0 = K_GM + d * 2 * P
        k[:, c0:c0 + P] = (s < t) if d == 0 else (s > t)
        k[:, c0 + P:c0 + 2 * P] = (s <= t) if d == 0 else (s >= t)
    return k


def kernel(x_prompt, x_sample, state_rwkv_fwd, state_rwkv_bwd, c, c_ctx, norm1_g, norm2_g, w_ada, b_ada, w_in,
           w0, w2, a0, a2, g2, k_k, k_a, r_k, lnx_w, lnx_b, conv_w, w_pa, w_pb, w_o, w_ff1, w_ff2, final_norm_g):
    import numpy as np
    import concourse.bacc as bacc
    from concourse.bass_utils import run_bass_kernel_spmd

    def col(w, n):
        return w[:, n * P:(n + 1) * P].reshape(KT, P, P).transpose(1, 0, 2).reshape(P, KT * P)

    wi, wada = np.asarray(w_in)[0], np.asarray(w_ada)[0]
    r1, r2, ro = np.asarray(w_pa)[0], np.asarray(w_pb)[0], np.asarray(w_o)[0]
    f1, f2 = np.asarray(w_ff1)[0], np.asarray(w_ff2)[0]
    def quarter(b):
        g, x = divmod(b, 4)
        return wada[2 * x * P:(2 * x + 2) * P, g * MG:(g + 1) * MG].reshape(2, P, MG).transpose(1, 0, 2).reshape(P, KT * P)

    blocks = [quarter(b) for b in list(range(N_ADA_RING, N_ADA_FIRST)) + list(range(N_ADA_RING))] + [col(wi, 24 + n) for n in range(3)]
    for p in range(PAIRS):
        first = {"r": 0, "k": 8, "v": 16, "cb": 27, "cc": 35, "ch": 43, "za": 51, "zb": 59}
        blocks += [col(wi, first[n] + p) if isinstance(n, str) else quarter(N_ADA_FIRST + 4 * p + n) for n in STREAM]
    for m in range(0, KT, 2):
        blocks += [col(r1, m), col(r1, m + 1), col(r2, m), col(r2, m + 1)]
    blocks += [col(ro, m) for m in range(KT)]
    for e in range(FFE):
        blocks += [col(f1, e * HB + m) for m in range(HB)]
        for m in range(0, KT, 2):
            both = f2[e * HB * P:(e + 1) * HB * P, m * P:(m + 2) * P].reshape(HB, P, 2, P)
            blocks.append(both.transpose(1, 2, 0, 3).reshape(P, KT * P))
    wblocks = np.stack(blocks).reshape(N_HELD + N_BLOCKS, P, KT, P)

    w2_, a2_, g2_ = np.asarray(w2)[0], np.asarray(a2)[0], np.asarray(g2)[0]
    pack, packl = np.zeros((PAIRS, P, PK), np.float32), np.zeros((PAIRS, P, PL), np.float32)
    rows = [np.asarray(w0)[0, 0], np.asarray(w0)[0, 1], np.asarray(a0)[0, 0], np.asarray(a0)[0, 1], np.asarray(k_k)[0],
            np.asarray(k_a)[0], np.asarray(r_k)[0].reshape(D),
            np.asarray(conv_w)[0, 0], np.asarray(conv_w)[0, 1], np.asarray(conv_w)[0, 2]]
    for p in range(PAIRS):
        cs = slice(p * P, (p + 1) * P)
        for d, st in enumerate((state_rwkv_fwd, state_rwkv_bwd)):
            pack[p, d * HD:(d + 1) * HD, PK_W2 + d * P:PK_W2 + (d + 1) * P] = w2_[d][:, cs]
            pack[p, d * HD:(d + 1) * HD, PK_A2 + d * P:PK_A2 + (d + 1) * P] = a2_[d][:, cs]
            heads_ = np.asarray(st)[0, 0, 2 * p:2 * p + 2].transpose(0, 2, 1).reshape(P, HD)
            pack[p, :, PK_ST + d * HD:PK_ST + (d + 1) * HD] = heads_
        packl[p, :, PL_G2:PL_G2 + P] = g2_[:, cs]
        packl[p, :, PL_W], packl[p, :, PL_B] = np.asarray(lnx_w)[0, cs], np.asarray(lnx_b)[0, cs]
        for i, r in enumerate(rows):
            pack[p, :, PK_VEC + i] = r[cs]
    vecs = np.concatenate([np.asarray(b_ada)[0].reshape(48, P).T, np.asarray(norm1_g)[0].reshape(KT, P).T,
                           np.asarray(norm2_g)[0].reshape(KT, P).T], axis=1)
    cin = np.stack([np.asarray(c)[0].reshape(KT, P).T, np.asarray(c_ctx).reshape(KT, P).T], axis=2)
    gfin = np.broadcast_to(np.asarray(final_norm_g)[None, :], (P, D))

    nc = bacc.Bacc("TRN2", target_bir_lowering=False, num_devices=1)
    arrays = {"xs": np.asarray(x_sample)[0], "xp": np.asarray(x_prompt)[0], "wblocks": wblocks, "pack": pack, "packl": packl,
              "vecs": vecs, "cin": cin, "consts": constants(), "gfin": gfin}
    arrays = {f"in_{n}": np.ascontiguousarray(a) for n, a in arrays.items()}
    ins = [nc.dram_tensor(n, a.shape, mybir.dt.from_np(a.dtype), kind="ExternalInput").ap() for n, a in arrays.items()]
    outs = [nc.dram_tensor(n, s, F32, kind="ExternalOutput").ap()
            for n, s in (("y_out", (LAT, D)), ("yp_out", (CTX, D)), ("st_out", (2, PAIRS, P, HD)))]
    flow_step(nc, *ins, *outs)
    res = run_bass_kernel_spmd(nc, [arrays], core_ids=[0]).results[0]
    st = res["st_out"].reshape(2, 1, 1, 2 * PAIRS, HD, HD).transpose(0, 1, 2, 3, 5, 4)
    return (res["yp_out"].reshape(1, CTX, D), res["y_out"].reshape(1, LAT, D), np.ascontiguousarray(st[0]), np.ascontiguousarray(st[1]))
```
